# Optimizing a Trainium2 kernel written in Bass

```python
import math
import jax
import jax.numpy as jnp
from jax import lax
import numpy as np

D_MODEL = 1024
BATCH = 1
SEQ = 512
DEPTH = 2

GRID_W = 64
CTX_LEN = 256
HEAD_DIM = 64
ROPE_THETA = 10000.0
EPS = 1e-6
Q_BLOCK = 128
FFN_DIM = 2816
N_MOD = 9

A_Q_HEADS = 4
A_KV_HEADS = 2
WINDOW = 128
B_Q_HEADS = 4
B_KV_HEADS = 2
C_HEADS = 4
C_Q_LORA = 256
C_KV_LORA = 128
C_NOPE = 64
C_ROPE = 32
C_V = 64
D_HEADS = 4
D_HEAD_DIM = 64
D_STATE = 128
D_GROUPS = 2
D_CONV = 5
SSD_CHUNK = 128

MIX_A = A_Q_HEADS * HEAD_DIM
MIX_B = B_Q_HEADS * HEAD_DIM
MIX_C = C_HEADS * C_V
MIX_D = D_HEADS * D_HEAD_DIM
MIX_WIDTH = MIX_A + MIX_B + MIX_C + MIX_D
IN_A = (A_Q_HEADS + 2 * A_KV_HEADS) * HEAD_DIM
IN_B = (B_Q_HEADS + 2 * B_KV_HEADS) * HEAD_DIM
IN_C = C_Q_LORA + C_KV_LORA + C_ROPE
D_CONV_CH = MIX_D + 2 * D_GROUPS * D_STATE
IN_D = MIX_D + D_CONV_CH + 2 * D_HEADS
IN_WIDTH = IN_A + IN_B + IN_C + IN_D

kernel_name = "hybrid_prefix_dit_block"

def _rms(x, g):
    xf = x.astype(jnp.float32)
    y = xf * lax.rsqrt(jnp.mean(xf * xf, axis=-1, keepdims=True) + EPS)
    return (y * g.astype(jnp.float32)).astype(x.dtype)

def _modulate(n, shift, scale):
    return n * (1.0 + scale) + shift

def _swiglu(n, wi, wo):
    a, b = jnp.split(n @ wi, 2, axis=-1)
    return (jax.nn.silu(a) * b) @ wo

def _ffn_half(h, mods, norm_g, wi, wo):
    shift, scale, gate = mods
    n = _modulate(_rms(h, norm_g), shift, scale)
    return h + 0.5 * gate * _swiglu(n, wi, wo)

def _axial_angles(seq_len, rot_dim):
    rows = seq_len // GRID_W
    r = jnp.repeat(jnp.arange(rows, dtype=jnp.float32), GRID_W)
    col = jnp.tile(jnp.arange(GRID_W, dtype=jnp.float32), rows)
    axis_dim = rot_dim // 2
    inv = ROPE_THETA ** (-jnp.arange(0, axis_dim, 2, dtype=jnp.float32) / axis_dim)
    return (r[:, None] * inv[None, :], col[:, None] * inv[None, :])

def _rope_axis(x, ang):
    shape = (1, ang.shape[0]) + (1,) * (x.ndim - 3) + (ang.shape[1],)
    cos = jnp.cos(ang).reshape(shape)
    sin = jnp.sin(ang).reshape(shape)
    x1, x2 = jnp.split(x.astype(jnp.float32), 2, axis=-1)
    return jnp.concatenate([x1 * cos - x2 * sin, x2 * cos + x1 * sin], axis=-1).astype(x.dtype)

def _rope_2d(x, angs):
    xr, xc = jnp.split(x, 2, axis=-1)
    return jnp.concatenate([_rope_axis(xr, angs[0]), _rope_axis(xc, angs[1])], axis=-1)

def _attend(q, k, v, scale, sink=None):
    s = jnp.einsum('bqkgd,btkd->bkgqt', q, k).astype(jnp.float32) * scale
    if sink is not None:
        col = jnp.broadcast_to(sink.astype(jnp.float32)[None, :, :, None, None], s.shape[:-1] + (1,))
        p = jax.nn.softmax(jnp.concatenate([s, col], axis=-1), axis=-1)[..., :-1]
    else:
        p = jax.nn.softmax(s, axis=-1)
    return jnp.einsum('bkgqt,btke->bqkge', p.astype(v.dtype), v)

def _attend_blocked(q, k, v, scale):
    bsz, s = q.shape[:2]
    nb = s // Q_BLOCK
    qb = jnp.moveaxis(q.reshape((bsz, nb, Q_BLOCK) + q.shape[2:]), 1, 0)
    out = lax.map(lambda qi: _attend(qi, k, v, scale), qb)
    return jnp.moveaxis(out, 0, 1).reshape((bsz, s) + out.shape[3:])

def _window_attend(q, k, v, kc, vc, sink, scale):
    bsz, s = q.shape[:2]
    nb = s // WINDOW

    def bands(t):
        tp = jnp.pad(t, ((0, 0), (WINDOW, WINDOW), (0, 0), (0, 0)))
        tb = tp.reshape((bsz, nb + 2, WINDOW) + t.shape[2:])
        return jnp.concatenate([tb[:, :-2], tb[:, 1:-1], tb[:, 2:]], axis=2)

    kb, vb = bands(k), bands(v)
    qb = q.reshape((bsz, nb, WINDOW) + q.shape[2:])
    blk = jnp.arange(nb)[:, None] * WINDOW
    qpos = blk + jnp.arange(WINDOW)[None, :]
    kpos = blk - WINDOW + jnp.arange(3 * WINDOW)[None, :]
    valid = ((jnp.abs(qpos[:, :, None] - kpos[:, None, :]) <= WINDOW)
             & (kpos >= 0)[:, None, :] & (kpos < s)[:, None, :])
    s_loc = jnp.einsum('bnqkgd,bnjkd->bnkgqj', qb, kb).astype(jnp.float32) * scale
    s_loc = jnp.where(valid[None, :, None, None], s_loc, -jnp.inf)
    s_ctx = jnp.einsum('bnqkgd,bckd->bnkgqc', qb, kc).astype(jnp.float32) * scale
    s_sink = jnp.broadcast_to(sink.astype(jnp.float32)[None, None, :, :, None, None], s_loc.shape[:-1] + (1,))
    p = jax.nn.softmax(jnp.concatenate([s_loc, s_ctx, s_sink], axis=-1), axis=-1)
    p_loc = p[..., :3 * WINDOW].astype(v.dtype)
    p_ctx = p[..., 3 * WINDOW:3 * WINDOW + kc.shape[1]].astype(v.dtype)
    out = (jnp.einsum('bnkgqj,bnjkd->bnqkgd', p_loc, vb)
           + jnp.einsum('bnkgqc,bckd->bnqkgd', p_ctx, vc))
    return out.reshape((bsz, s) + out.shape[3:])

def _dwconv_centred(u, w, b):
    ch = u.shape[-1]
    y = lax.conv_general_dilated(u, w.reshape(w.shape[0], 1, ch).astype(u.dtype), window_strides=(1,),
                                 padding=[(D_CONV // 2, D_CONV // 2)],
                                 dimension_numbers=('NWC', 'WIO', 'NWC'), feature_group_count=ch)
    return y + b

def _ssd(x, dt, a_neg, bh, ch, h0):
    bsz, n, nh, hp = x.shape
    nc = n // SSD_CHUNK

    def chunk(t):
        return t.astype(jnp.float32).reshape((bsz, nc, SSD_CHUNK) + t.shape[2:])

    a = chunk(dt * a_neg)
    xdt = chunk(x.astype(jnp.float32) * dt[..., None])
    bc, cc = chunk(bh), chunk(ch)
    a_cs = jnp.cumsum(a, axis=2)
    seg = a_cs[:, :, :, None, :] - a_cs[:, :, None, :, :]
    lower = jnp.tril(jnp.ones((SSD_CHUNK, SSD_CHUNK), dtype=bool))
    decay = jnp.exp(jnp.where(lower[None, None, :, :, None], seg, -jnp.inf))
    scores = jnp.einsum('bcihn,bcjhn->bcijh', cc, bc) * decay
    y_diag = jnp.einsum('bcijh,bcjhp->bcihp', scores, xdt)
    decay_to_end = jnp.exp(a_cs[:, :, -1:, :] - a_cs)
    states = jnp.einsum('bcjhn,bcjh,bcjhp->bchpn', bc, decay_to_end, xdt)
    chunk_decay = jnp.exp(a_cs[:, :, -1, :])

    def step(h, inp):
        st, d = inp
        return d[:, :, None, None] * h + st, h

    h_final, h_in = lax.scan(step, h0, (jnp.swapaxes(states, 0, 1), jnp.swapaxes(chunk_decay, 0, 1)))
    h_in = jnp.swapaxes(h_in, 0, 1)
    y_off = jnp.einsum('bcihn,bchpn->bcihp', cc, h_in) * jnp.exp(a_cs)[..., None]
    y = (y_diag + y_off).reshape(bsz, n, nh, hp)
    return y.astype(x.dtype), h_final

def _mixer_a(px, pc, sink, ang, with_ctx):
    scale = HEAD_DIM ** -0.5
    grp = A_Q_HEADS // A_KV_HEADS
    nq, nkv = A_Q_HEADS * HEAD_DIM, A_KV_HEADS * HEAD_DIM

    def heads(p):
        bsz, n = p.shape[:2]
        q = p[..., :nq].reshape(bsz, n, A_KV_HEADS, grp, HEAD_DIM)
        k = p[..., nq:nq + nkv].reshape(bsz, n, A_KV_HEADS, HEAD_DIM)
        v = p[..., nq + nkv:].reshape(bsz, n, A_KV_HEADS, HEAD_DIM)
        return q, k, v

    qx, kx, vx = heads(px)
    qc, kc, vc = heads(pc)
    qx, kx = _rope_2d(qx, ang), _rope_2d(kx, ang)
    sink_kg = sink.reshape(A_KV_HEADS, grp)
    ox = _window_attend(qx, kx, vx, kc, vc, sink_kg, scale).reshape(px.shape[0], px.shape[1], MIX_A)
    oc = _attend(qc, kc, vc, scale, sink_kg).reshape(pc.shape[0], pc.shape[1], MIX_A) if with_ctx else None
    return ox, oc

def _mixer_b(px, pc, q_norm, k_norm, ang, with_ctx):
    scale = HEAD_DIM ** -0.5
    grp = B_Q_HEADS // B_KV_HEADS
    nq, nkv = B_Q_HEADS * HEAD_DIM, B_KV_HEADS * HEAD_DIM

    def heads(p):
        bsz, n = p.shape[:2]
        q = _rms(p[..., :nq].reshape(bsz, n, B_KV_HEADS, grp, HEAD_DIM), q_norm)
        k = _rms(p[..., nq:nq + nkv].reshape(bsz, n, B_KV_HEADS, HEAD_DIM), k_norm)
        v = p[..., nq + nkv:].reshape(bsz, n, B_KV_HEADS, HEAD_DIM)
        return q, k, v

    qx, kx, vx = heads(px)
    qc, kc, vc = heads(pc)
    qx, kx = _rope_2d(qx, ang), _rope_2d(kx, ang)
    k_all = jnp.concatenate([kx, kc], axis=1)
    v_all = jnp.concatenate([vx, vc], axis=1)
    ox = _attend_blocked(qx, k_all, v_all, scale).reshape(px.shape[0], px.shape[1], MIX_B)
    oc = _attend(qc, kc, vc, scale).reshape(pc.shape[0], pc.shape[1], MIX_B) if with_ctx else None
    return ox, oc

def _mixer_c(px, pc, q_norm, w_uq, kv_norm, w_ukv, ang, with_ctx):
    scale = (C_NOPE + C_ROPE) ** -0.5

    def proj(p, rope):
        bsz, n = p.shape[:2]
        cq = p[..., :C_Q_LORA]
        ckv = p[..., C_Q_LORA:C_Q_LORA + C_KV_LORA]
        k_rope = p[..., C_Q_LORA + C_KV_LORA:][:, :, None, :]
        q = (_rms(cq, q_norm) @ w_uq).reshape(bsz, n, C_HEADS, C_NOPE + C_ROPE)
        kv = (_rms(ckv, kv_norm) @ w_ukv).reshape(bsz, n, C_HEADS, C_NOPE + C_V)
        q_nope, q_rope = q[..., :C_NOPE], q[..., C_NOPE:]
        k_nope, v = kv[..., :C_NOPE], kv[..., C_NOPE:]
        if rope:
            q_rope, k_rope = _rope_2d(q_rope, ang), _rope_2d(k_rope, ang)
        q = jnp.concatenate([q_nope, q_rope], axis=-1)[:, :, :, None, :]
        k = jnp.concatenate([k_nope, jnp.broadcast_to(k_rope, k_nope.shape[:-1] + (C_ROPE,))], axis=-1)
        return q, k, v

    qx, kx, vx = proj(px, True)
    qc, kc, vc = proj(pc, False)
    k_all = jnp.concatenate([kx, kc], axis=1)
    v_all = jnp.concatenate([vx, vc], axis=1)
    ox = _attend_blocked(qx, k_all, v_all, scale).reshape(px.shape[0], px.shape[1], MIX_C)
    oc = _attend(qc, kc, vc, scale).reshape(pc.shape[0], pc.shape[1], MIX_C) if with_ctx else None
    return ox, oc

def _mixer_d(px, pc, conv_w, conv_b, a_log, dt_bias, d_skip, out_norm, with_ctx):
    a_neg = -jnp.exp(a_log.astype(jnp.float32))
    rep = D_HEADS // D_GROUPS
    gn = D_GROUPS * D_STATE

    def prep(p):
        bsz, n = p.shape[:2]
        z = p[..., :MIX_D]
        xbc = jax.nn.silu(_dwconv_centred(p[..., MIX_D:MIX_D + D_CONV_CH], conv_w, conv_b))
        xs = xbc[..., :MIX_D].reshape(bsz, n, D_HEADS, D_HEAD_DIM)
        bm = jnp.repeat(xbc[..., MIX_D:MIX_D + gn].reshape(bsz, n, D_GROUPS, D_STATE), rep, axis=2)
        cm = jnp.repeat(xbc[..., MIX_D + gn:].reshape(bsz, n, D_GROUPS, D_STATE), rep, axis=2)
        dt = jax.nn.softplus(p[..., MIX_D + D_CONV_CH:].astype(jnp.float32).reshape(bsz, n, 2, D_HEADS)
                             + dt_bias.astype(jnp.float32))
        return z, xs, bm, cm, dt

    def flip(t):
        return jnp.flip(t, axis=1)

    def scan_pair(xs, bm, cm, dt, h_f, h_b):
        y_f, s_f = _ssd(xs, dt[:, :, 0], a_neg[0], bm, cm, h_f)
        y_b, s_b = _ssd(flip(xs), flip(dt[:, :, 1]), a_neg[1], flip(bm), flip(cm), h_b)
        return y_f + flip(y_b), s_f, s_b

    def finish(y, xs, z):
        bsz, n = z.shape[:2]
        y = (y + d_skip[:, None] * xs).reshape(bsz, n, MIX_D)
        return _rms(y * jax.nn.silu(z), out_norm)

    zc, xc, bc, cc, dtc = prep(pc)
    h0 = jnp.zeros((pc.shape[0], D_HEADS, D_HEAD_DIM, D_STATE), jnp.float32)
    yc, sc_f, sc_b = scan_pair(xc, bc, cc, dtc, h0, h0)
    zx, xx, bx, cx, dtx = prep(px)
    yx, _, _ = scan_pair(xx, bx, cx, dtx, sc_f, sc_b)
    ox = finish(yx, xx, zx)
    oc = finish(yc, xc, zc) if with_ctx else None
    return ox, oc

def setup_inputs(seed: int = 0) -> dict:
    key = jax.random.key(seed)
    ks = list(jax.random.split(key, 32))

    def nrm(shape, scale):
        return jax.random.normal(ks.pop(), shape, jnp.float32) * scale

    def gain(shape):
        return 1.0 + nrm(shape, 0.05)

    L, D = DEPTH, D_MODEL
    x = nrm((BATCH, SEQ, D), 1.0)
    c = nrm((BATCH, D), 1.0)
    ctx = nrm((BATCH, CTX_LEN, D), 1.0)
    c_ctx = nrm((D,), 1.0)
    ada_w = nrm((L, D, N_MOD * D), 0.5 * D ** -0.5)
    ada_b = nrm((L, N_MOD * D), 0.02)
    ffn1_norm = gain((L, D))
    ffn1_wi = nrm((L, D, 2 * FFN_DIM), D ** -0.5)
    ffn1_wo = nrm((L, FFN_DIM, D), FFN_DIM ** -0.5)
    mix_norm = gain((L, D))
    w_in = nrm((L, D, IN_WIDTH), D ** -0.5)
    w_out = nrm((L, MIX_WIDTH, D), MIX_WIDTH ** -0.5)
    a_sink = nrm((L, A_Q_HEADS), 0.5)
    b_q_norm = gain((L, HEAD_DIM))
    b_k_norm = gain((L, HEAD_DIM))
    c_q_norm = gain((L, C_Q_LORA))
    c_w_uq = nrm((L, C_Q_LORA, C_HEADS * (C_NOPE + C_ROPE)), C_Q_LORA ** -0.5)
    c_kv_norm = gain((L, C_KV_LORA))
    c_w_ukv = nrm((L, C_KV_LORA, C_HEADS * (C_NOPE + C_V)), C_KV_LORA ** -0.5)
    d_conv_w = nrm((L, D_CONV, D_CONV_CH), D_CONV ** -0.5)
    d_conv_b = nrm((L, D_CONV_CH), 0.02)
    dt0 = jnp.exp(jax.random.uniform(ks.pop(), (L, 2, D_HEADS), jnp.float32,
                                     minval=math.log(1e-3), maxval=math.log(1e-1)))
    d_dt_bias = dt0 + jnp.log(-jnp.expm1(-dt0))
    d_a_log = jnp.log(jax.random.uniform(ks.pop(), (L, 2, D_HEADS), jnp.float32, minval=1.0, maxval=16.0))
    d_skip = gain((L, D_HEADS))
    d_out_norm = gain((L, MIX_D))
    ffn2_norm = gain((L, D))
    ffn2_wi = nrm((L, D, 2 * FFN_DIM), D ** -0.5)
    ffn2_wo = nrm((L, FFN_DIM, D), FFN_DIM ** -0.5)
    final_norm = gain((D,))
    return {"x": x, "c": c, "ctx": ctx, "c_ctx": c_ctx, "ada_w": ada_w, "ada_b": ada_b,
            "ffn1_norm": ffn1_norm, "ffn1_wi": ffn1_wi, "ffn1_wo": ffn1_wo,
            "mix_norm": mix_norm, "w_in": w_in, "w_out": w_out, "a_sink": a_sink,
            "b_q_norm": b_q_norm, "b_k_norm": b_k_norm, "c_q_norm": c_q_norm, "c_w_uq": c_w_uq,
            "c_kv_norm": c_kv_norm, "c_w_ukv": c_w_ukv, "d_conv_w": d_conv_w, "d_conv_b": d_conv_b,
            "d_a_log": d_a_log, "d_dt_bias": d_dt_bias, "d_skip": d_skip, "d_out_norm": d_out_norm,
            "ffn2_norm": ffn2_norm, "ffn2_wi": ffn2_wi, "ffn2_wo": ffn2_wo, "final_norm": final_norm}

def reference(x, c, ctx, c_ctx, ada_w, ada_b, ffn1_norm, ffn1_wi, ffn1_wo, mix_norm, w_in, w_out,
              a_sink, b_q_norm, b_k_norm, c_q_norm, c_w_uq, c_kv_norm, c_w_ukv, d_conv_w, d_conv_b,
              d_a_log, d_dt_bias, d_skip, d_out_norm, ffn2_norm, ffn2_wi, ffn2_wo, final_norm):
    hx, hc = x, ctx
    seq_len = x.shape[1]
    ang_head = _axial_angles(seq_len, HEAD_DIM)
    ang_mla = _axial_angles(seq_len, C_ROPE)
    cuts = [IN_A, IN_A + IN_B, IN_A + IN_B + IN_C]
    for l in range(DEPTH):
        with_ctx = l < DEPTH - 1
        mx = jnp.split((jax.nn.silu(c) @ ada_w[l] + ada_b[l])[:, None, :], N_MOD, axis=-1)
        mc = jnp.split((jax.nn.silu(c_ctx) @ ada_w[l] + ada_b[l])[None, None, :], N_MOD, axis=-1)
        hx = _ffn_half(hx, mx[0:3], ffn1_norm[l], ffn1_wi[l], ffn1_wo[l])
        hc = _ffn_half(hc, mc[0:3], ffn1_norm[l], ffn1_wi[l], ffn1_wo[l])
        px = _modulate(_rms(hx, mix_norm[l]), mx[3], mx[4]) @ w_in[l]
        pc = _modulate(_rms(hc, mix_norm[l]), mc[3], mc[4]) @ w_in[l]
        pxa, pxb, pxc, pxd = jnp.split(px, cuts, axis=-1)
        pca, pcb, pcc, pcd = jnp.split(pc, cuts, axis=-1)
        oxa, oca = _mixer_a(pxa, pca, a_sink[l], ang_head, with_ctx)
        oxb, ocb = _mixer_b(pxb, pcb, b_q_norm[l], b_k_norm[l], ang_head, with_ctx)
        oxc, occ = _mixer_c(pxc, pcc, c_q_norm[l], c_w_uq[l], c_kv_norm[l], c_w_ukv[l], ang_mla, with_ctx)
        oxd, ocd = _mixer_d(pxd, pcd, d_conv_w[l], d_conv_b[l], d_a_log[l], d_dt_bias[l], d_skip[l],
                            d_out_norm[l], with_ctx)
        hx = hx + mx[5] * (jnp.concatenate([oxa, oxb, oxc, oxd], axis=-1) @ w_out[l])
        hx = _ffn_half(hx, mx[6:9], ffn2_norm[l], ffn2_wi[l], ffn2_wo[l])
        if with_ctx:
            hc = hc + mc[5] * (jnp.concatenate([oca, ocb, occ, ocd], axis=-1) @ w_out[l])
            hc = _ffn_half(hc, mc[6:9], ffn2_norm[l], ffn2_wi[l], ffn2_wo[l])
    return _rms(hx, final_norm)


_drawn_inputs = setup_inputs


def setup_inputs(seed=0):
    import zlib

    import numpy as np

    out = dict(_drawn_inputs(seed))
    spreads = {}
    factors = {'ctx': 3.285,
     'ffn1_norm': 5.338,
     'mix_norm': 4.087,
     'a_sink': 8.0,
     'b_q_norm': 8.0,
     'b_k_norm': 8.0,
     'c_q_norm': 8.0,
     'c_w_uq': 3.099,
     'c_kv_norm': 8.0,
     'd_conv_b': 8.0,
     'd_skip': 8.0,
     'd_out_norm': 6.018,
     'ffn2_norm': 5.604}
    for name, (base, spread) in spreads.items():
        noise = np.random.default_rng([zlib.crc32(name.encode()), seed]).standard_normal(out[name].shape)
        drawn = base * np.exp(spread * noise) if base else spread * noise
        out[name] = jnp.asarray(drawn.astype(out[name].dtype))
    for name, factor in factors.items():
        out[name] = (out[name] * factor).astype(out[name].dtype)
    return out
```

```python
from contextlib import ExitStack

import concourse.bass as bass
from concourse import mybir

ALU = mybir.AluOpType
ACT = mybir.ActivationFunctionType
F32 = mybir.dt.float32
F32R = mybir.dt.float32r
AX_X = mybir.AxisListType.X

P = 128
DEPTH = 2
DM = 1024
KD = DM // P
SEQ, CTX = 512, 256
TOK = SEQ + CTX
NX, NT = SEQ // P, TOK // P
FFN = 2816
FT = FFN // P
FG = FT // 2
NMOD = 9
EPS = 1e-6
GRID_W = 64
THETA = 10000.0
HD = 64
C_ROPE = 32
SEGS = [(0, SEQ), (SEQ, CTX)]

A0, B0, C0, Z0 = 0, 512, 1024, 1440
DT0 = Z0 + 256
TOKW = DT0 + 8
XBC_COL = 1696
DT_COL = 2464
XW = TOK + 6
NEG = -float(2 ** 100)

UNITS = [("conv", [(XBC_COL, 256, 0)]), ("conv", [(XBC_COL + 256, 256, 2)]), ("conv", [(XBC_COL + 512, 256, 4)]),
         ("tok", [(1280, 160, 1280), (DT_COL, 8, DT0)]), ("tok", [(1440, 256, Z0)]), ("tok", [(1024, 256, C0)]),
         ("tok", [(0, 256, A0)]), ("tok", [(256, 256, 256)]), ("tok", [(512, 256, B0)]), ("tok", [(768, 256, 768)])]
NU = len(UNITS)
OUTU = 4

CST = {}
_n = 0
for _name, _w in (("ident", P), ("ones", P), ("le", P), ("gt", P), ("ge", P), ("lt", P), ("prev", P), ("next", P),
                  ("cosh", NX * 32), ("sinh", NX * 32), ("cosc", NX * 16), ("sinc", NX * 16)):
    CST[_name] = (_n, _w)
    _n += _w
CSTW = _n

ROWS = {}
_n = 0
for _name, _w in (("b_q_norm", 64), ("b_k_norm", 64), ("c_q_norm", 256), ("c_kv_norm", 128), ("a_sink", 4),
                  ("d_dt_bias", 8), ("d_a_log", 8), ("d_skip", 4), ("d_out_norm", 256)):
    ROWS[_name] = (_n, _w)
    _n += _w
ROWW = _n

V_ADAB, V_FFN1, V_MIX, V_FFN2, V_FIN, V_C, V_CC = 0, 144, 160, 176, 192, 200, 208
V_CONVW, V_CONVB = 216, 276
VECW = 288

ADAW = 256
BATCH = 3 * ADAW
ADA_AT = [(0, 4), (4, 10), (14, 10)]
NBATCH = DEPTH * NMOD * DM // BATCH

STOP_AFTER = None
DEBUG = None


def conv_col(t):
    return t * P if t < NX else SEQ + 2 + (t - NX) * P


def hybrid_block(nc, I, out, mod_dram, stop_after=None):
    stages = [("ffn", 0, 0), ("mix", 0, 0), ("ffn", 0, 1), ("ffn", 1, 0), ("mix", 1, 0), ("ffn", 1, 1)]
    if stop_after is not None:
        stages = stages[:int(stop_after)]

    with ExitStack() as ctx:
        at = [16512]

        def place(name, shape, dt=F32, offset=None):
            size = 4
            for s in shape[1:]:
                size *= s
            size = (size + 31) // 32 * 32
            if offset is None:
                offset = at[0]
                at[0] += size
            assert offset + size <= nc.sbuf_usable_end, (name, offset + size)
            return nc.alloc_sbuf_tensor_at(name, shape, dt, offset=offset)

        def sem(name):
            return ctx.enter_context(nc.semaphore(name))

        h = place("h", [P, KD, TOK])
        mods = place("mods", [P, DEPTH * NMOD * KD, 2])
        vec = place("vec", [P, VECW])
        gain = place("gain", [P, DEPTH, 3, KD, 2])
        half_gate = place("half_gate", [P, DEPTH, 2, KD, 2])
        cst = place("cst", [P, CSTW])
        rows = place("rows", [P, DEPTH, ROWW])
        silu_c = place("silu_c", [P, KD, 2])
        silu_r = place("silu_r", [P, KD, 4], F32R)
        eps = place("eps", [P, 1])
        sq_at = at[0]
        sq = place("sq", [P, 2, TOK])
        sumsq_at = at[0]
        sumsq = place("sumsq", [P, TOK])
        rstd_at = at[0]
        rstd = place("rstd", [P, TOK])
        wi_raw, wi_lo, wi_hi = [], [], []
        for s in range(2):
            a = at[0]
            wi_raw.append(place(f"wi_raw{s}", [P, KD, 256]))
            wi_lo.append(place(f"wi_lo{s}", [P, KD, 256], F32R, offset=a))
            wi_hi.append(place(f"wi_hi{s}", [P, KD, 256], F32R))
        wo_at = at[0]
        wo_raw = place("wo_raw", [P, 2, DM])
        wo_lo = place("wo_lo", [P, 2, DM], F32R, offset=wo_at)
        wo_hi = place("wo_hi", [P, 2, DM], F32R)
        n_at = at[0]
        n_hi = place("n_hi", [P, KD, TOK], F32R)
        n_lo = place("n_lo", [P, KD, TOK], F32R)
        m_at = at[0]
        n_tmp = sq

        g_hi = place("g_hi", [P, 2, TOK], F32R)
        g_lo = place("g_lo", [P, 2, TOK], F32R)
        silu_a = place("silu_a", [P, 2, TOK], offset=sq_at)
        prod = silu_a
        ada_raw, ada_lo, ada_hi = [], [], []
        for s in range(3):
            a = at[0]
            ada_raw.append(place(f"ada_raw{s}", [P, KD, ADAW]))
            ada_lo.append(place(f"ada_lo{s}", [P, KD, ADAW], F32R, offset=a))
            ada_hi.append(place(f"ada_hi{s}", [P, KD, ADAW], F32R))
        ada_rows = place("ada_rows", [4, 3 * ADAW], offset=rstd_at)
        mod_rows = place("mod_rows", [P, 4, P], offset=m_at + 4 * 2 * TOK * 4)

        at[0] = m_at
        tok = place("tok", [P, NT, TOKW])
        xbc = place("xbc", [P, 6, XW])
        small = place("small", [P, 384], offset=sumsq_at)
        free_at = wo_at
        at[0] = n_at
        xsb = place("xsb", [P, NT, 512])
        xdt = place("xdt", [P, 2, NT, 256])
        xdec_at = at[0]
        xdec = place("xdec", [P, 2, NT, 256])
        cb = place("cb", [P, NT, 2, 2, P], offset=xdec_at)
        h_in = place("h_in", [P, 2, NT, 256])
        assert at[0] <= m_at
        at[0] = free_at
        seg_rhs = place("seg_rhs", [P, 2, 512])
        decay = place("decay", [P, 2, 512])
        y_tmp = place("y_tmp", [P, 512])
        conv_acc = place("conv_acc", [P, 2, XW - 4], offset=free_at)
        at[0] = n_at
        qkT = place("qkT", [96, 8, TOK])
        probs = place("probs", [P, 2, TOK])
        probsT = place("probsT", [P, 2, TOK])
        vc = place("vc", [P, NT, 256])
        assert at[0] <= m_at
        xbc_at = n_at + 2 * KD * TOK * 4 + NT * TOKW * 4
        qc = place("qc", [P, NT, 4, 96], offset=xbc_at)
        kc = place("kc", [P, NT, 4, 96], offset=xbc_at + NT * 384 * 4)
        cT = place("cT", [P, 3, TOK], offset=n_at + 8 * TOK * 4)
        w_uq = place("w_uq", [P, 2, 384], offset=free_at + 2048 * 5)
        w_ukv = place("w_ukv", [P, 512], offset=free_at + 2048 * 5 + 3072)
        m_tmp = place("m_tmp", [P, NX, 192], offset=sq_at)
        m_sq = place("m_sq", [P, NT, 384], offset=free_at)
        stat = place("stat", [P, 4, 160], offset=rstd_at)
        ps = ctx.enter_context(nc.psum_tensor("ps", [P, 8, 512], F32))

        def C(name):
            a, w = CST[name]
            return cst[:, a:a + w]

        def R(l, name):
            a, w = ROWS[name]
            return rows[:, l, a:a + w]

        ident, ones = C("ident"), C("ones")

        in_loaded, cst_loaded = sem("in_loaded"), sem("cst_loaded")
        vec_done, vec_copied = sem("vec_done"), sem("vec_copied")
        h0_done, h0_x, h0_c = sem("h0_done"), sem("h0_x"), sem("h0_c")
        silu_c_ready = sem("silu_c_ready")
        ada_loaded = [sem(f"ada_loaded{s}") for s in range(3)]
        ada_hi_ready = [sem(f"ada_hi_ready{s}") for s in range(3)]
        ada_lo_ready = [sem(f"ada_lo_ready{s}") for s in range(3)]
        ada_used = [sem(f"ada_used{s}") for s in range(3)]
        silu_hi_ready, silu_lo_ready = sem("silu_hi_ready"), sem("silu_lo_ready")
        rows_copied, rows_stored, mod_rows_loaded = sem("rows_copied"), sem("rows_stored"), sem("mod_rows_loaded")
        mod_turned, mods_ready = sem("mod_turned"), sem("mods_ready")
        wi_loaded = [sem(f"wi_loaded{s}") for s in range(2)]
        wi_hi_ready = [sem(f"wi_hi_ready{s}") for s in range(2)]
        wi_lo_ready = [sem(f"wi_lo_ready{s}") for s in range(2)]
        up_done = [sem(f"up_done{s}") for s in range(2)]
        wo_loaded, wo_hi_ready, wo_lo_ready, down_end = sem("wo_loaded"), sem("wo_hi_ready"), sem("wo_lo_ready"), sem("down_end")
        silu_ready = [sem(f"silu_ready{s}") for s in range(2)]
        prod_ready = [sem(f"prod_ready{s}") for s in range(2)]
        g_hi_ready = [sem(f"g_hi_ready{s}") for s in range(2)]
        g_lo_ready = [sem(f"g_lo_ready{s}") for s in range(2)]
        down_done, h_added = sem("down_done"), sem("h_added")
        sq_ready, sq_summed, ssum_done, rstd_ready = sem("sq_ready"), sem("sq_summed"), sem("ssum_done"), sem("rstd_ready")
        n_tmp_ready, n_hi_ready, n_lo_ready = sem("n_tmp_ready"), sem("n_hi_ready"), sem("n_lo_ready")
        proj_done, proj_copied = sem("proj_done"), sem("proj_copied")
        conv_ready, xbc_ready = sem("conv_ready"), sem("xbc_ready")
        fence = {e: sem(f"fence_{e}") for e in ("pe", "act", "dve", "pool")}
        prep_done = sem("prep_done")
        prep_copied = [sem("prep_copied_dve"), sem("prep_copied_act")]
        s_done, bias_ready, exp_done = sem("s_done"), sem("bias_ready"), sem("exp_done")
        t_done, t_copied_x, t_copied_c = sem("t_done"), sem("t_copied_x"), sem("t_copied_c")
        pv_done, o_ready = sem("pv_done"), sem("o_ready")
        oT_done, oT_hi, oT_lo = sem("oT_done"), sem("oT_hi"), sem("oT_lo")
        out_done, out_added = sem("out_done"), sem("out_added")
        dt_sums, dt_exps = sem("dt_sums"), sem("dt_exps")
        a_ready = sem("a_ready")
        st_done, h_in_ready = sem("st_done"), sem("h_in_ready")
        cb_done, cb_ready = sem("cb_done"), sem("cb_ready")
        seg_in, seg_done, seg_exp, m_ready = sem("seg_in"), sem("seg_done"), sem("seg_exp"), sem("m_ready")
        y_done, y_ready = sem("y_done"), sem("y_ready")
        xdt_ready = sem("xdt_ready")
        wc_loaded = sem("wc_loaded")
        act_dve, dve_act = sem("act_dve"), sem("dve_act")
        fin_done, fin_copied, stored = sem("fin_done"), sem("fin_copied"), [sem("stored0"), sem("stored1")]
        dve_chain, act_chain, pool_chain = sem("dve_chain"), sem("act_chain"), sem("pool_chain")

        info = []
        ffns = mixes = 0
        slot_units, jobs, oj, pj, sj, norms, projs = 0, 1, 0, 0, 0, 0, 0
        NPROJ = sum(NT if k == "tok" else 4 for k, _ in UNITS)
        for kind, l, which in stages:
            last = l == DEPTH - 1
            d = dict(kind=kind, l=l, which=which, units=slot_units, norm=norms)
            norms += 1
            if kind == "ffn":
                nseg = 1 if (last and which == 1) else 2
                d.update(ada=ADA_AT[1 + which] if l == 0 else None)
                d.update(k=ffns, segs=SEGS[:nseg], g0=ffns * FG, jobs=jobs, nj=KD * nseg)
                ffns += 1
                jobs += FG * KD * nseg
                slot_units += FG
            else:
                nseg = 1 if last else 2
                d.update(k=mixes, segs=SEGS, osegs=SEGS[:nseg], nq=NX if last else NT, out=oj, proj=projs,
                         ffn_units=ffns * FG)
                mixes += 1
                oj += KD * nseg
                projs += NPROJ
                slot_units += (NU + OUTU) // 2
            info.append(d)
        final_norm = dict(norm=norms, segs=SEGS[:1], kind="final")
        norm_adds = KD - 1

        def fence_all(eng, me, n):
            eng.drain().then_inc(fence[me], 1)
            for e, s in fence.items():
                if e != me:
                    eng.wait_ge(s, n)

        def wait_slot_used(eng, i, u):
            st = info[i]
            s = u % 2
            if st["kind"] == "mix" and u >= 2:
                if u - 2 < NU:
                    eng.wait_ge(proj_done, st["proj"] + sum(NT if k == "tok" else 4 for k, _ in UNITS[:u - 1]))
                else:
                    eng.wait_ge(out_done, st["out"] + len(st["osegs"]) * 2 * (u - 1 - NU))
            elif i > 0:
                pr = info[i - 1]
                if pr["kind"] == "ffn":
                    eng.wait_ge(up_done[s], pr["g0"] + FG)
                else:
                    eng.wait_ge(out_done, pr["out"] + len(pr["osegs"]) * KD)

        def act_split(act, s, n, w=256):
            act.wait_ge(wi_loaded[s], 32 * n)
            nc.scalar.copy(wi_hi[s][:, :, 0:w], wi_raw[s][:, :, 0:w]).then_inc(wi_hi_ready[s], 1)

        def dve_split(dve, s, n, w=256):
            dve.wait_ge(wi_hi_ready[s], n)
            nc.vector.tensor_tensor(wi_lo[s][:, :, 0:w], wi_raw[s][:, :, 0:w], wi_hi[s][:, :, 0:w].bitcast(F32),
                                    ALU.subtract).then_inc(wi_lo_ready[s], 1)

        def unit_w(u):
            return sum(w for _, w, _ in UNITS[u][1]) if u < NU else 256

        def wait_h(eng, i, d):
            if i == 0:
                eng.wait_ge(h0_x, d + 1)
                eng.wait_ge(h0_c, d + 1)
                return
            pr = info[i - 1]
            if pr["kind"] == "ffn":
                eng.wait_ge(h_added, pr["jobs"] + (FG - 1) * pr["nj"] + (d + 1) * len(pr["segs"]))
            else:
                eng.wait_ge(out_added, pr["out"] + (d + 1) * len(pr["osegs"]))

        def ncols(segs):
            return segs[-1][0] + segs[-1][1]

        def norm_act_sums(act, i, st):
            w = ncols(st["segs"])
            b = st["norm"] * norm_adds
            for d in range(KD):
                wait_h(act, i, d)
                if d >= 2:
                    act.wait_ge(sq_summed, b + max(1, d - 2))
                elif i > 0:
                    act.wait_ge(n_lo_ready, st["norm"] and n_count(i - 1))
                nc.scalar.activation(sq[:, d % 2, 0:w], h[:, d, 0:w], ACT.Square).then_inc(sq_ready, 1)

        def n_count(i):
            return sum(KD * len(x["segs"]) for x in info[:i + 1])

        def norm_dve_sums(dve, i, st):
            w = ncols(st["segs"])
            for d in range(1, KD):
                dve.wait_ge(sq_ready, st["norm"] * KD + d + 1)
                if d == 1 and st["norm"] > 0:
                    dve.wait_ge(ssum_done, st["norm"])
                if d > 1:
                    dve.wait_ge(sq_summed, st["norm"] * norm_adds + d - 1)
                nc.vector.tensor_tensor(sumsq[:, 0:w], sq[:, 0, 0:w] if d == 1 else sumsq[:, 0:w], sq[:, d % 2, 0:w],
                                        ALU.add).then_inc(sq_summed, 1)

        def norm_pe(pe, i, st):
            pe.wait_ge(sq_summed, (st["norm"] + 1) * norm_adds)
            if i > 0:
                wait_h(pe, i, KD - 1)
            for j, (a, w) in enumerate(st["segs"]):
                last = nc.tensor.matmul(ps[:, 6 + j, 0:w], ones, sumsq[:, a:a + w], start=True, stop=True)
            last.then_inc(ssum_done, 1)

        def norm_act_rstd(act, st):
            act.wait_ge(ssum_done, st["norm"] + 1)
            act.wait_ge(rows_stored, 16 * sum(nb for _, nb in ADA_AT[:1 + min(2, (st["norm"] + 1) // 2)]))
            if st["norm"] > 0:
                act.wait_ge(n_tmp_ready, n_count(st["norm"] - 1))
            for j, (a, w) in enumerate(st["segs"]):
                act_link(nc.scalar.activation(rstd[:, a:a + w], ps[:, 6 + j, 0:w], ACT.Ln, bias=eps[:, 0:1], scale=1.0 / DM))
            w = ncols(st["segs"])
            nc.scalar.activation(rstd[:, 0:w], rstd[:, 0:w], ACT.Exp, scale=-0.5).then_inc(rstd_ready, 1)

        def shift_of(st, d, j):
            m = {"ffn": 6 * st["which"], "mix": 3}[st["kind"]]
            c = (st["l"] * NMOD + m) * KD + d
            return mods[:, c, j:j + 1]

        def gain_of(st, d, j):
            m = {"ffn": 2 * st["which"], "mix": 1}[st["kind"]]
            return gain[:, st["l"], m, d, j:j + 1]

        def norm_act_mod(act, i, st):
            b = n_count(i - 1) if i else 0
            ns = len(st["segs"])
            for d in range(KD):
                for j, (a, w) in enumerate(st["segs"]):
                    act.wait_ge(n_tmp_ready, b + d * ns + j + 1)
                    nc.scalar.activation(n_hi[:, d, a:a + w], n_tmp[:, d % 2, a:a + w], ACT.Identity,
                                         bias=shift_of(st, d, j)).then_inc(n_hi_ready, 1)

        def norm_dve_mod(dve, i, st):
            b = n_count(i - 1) if i else 0
            ns = len(st["segs"])
            dve.wait_ge(rstd_ready, st["norm"] + 1)
            for d in range(KD + 1):
                if d < KD:
                    for j, (a, w) in enumerate(st["segs"]):
                        if d >= 2:
                            dve.wait_ge(n_lo_ready, b + (d - 2) * ns + j + 1)
                        nc.vector.scalar_tensor_tensor(out=n_tmp[:, d % 2, a:a + w], in0=h[:, d, a:a + w],
                                                       scalar=gain_of(st, d, j), in1=rstd[:, a:a + w],
                                                       op0=ALU.mult, op1=ALU.mult).then_inc(n_tmp_ready, 1)
                if d >= 1:
                    for j, (a, w) in enumerate(st["segs"]):
                        dve.wait_ge(n_hi_ready, b + (d - 1) * ns + j + 1)
                        nc.vector.scalar_tensor_tensor(out=n_lo[:, d - 1, a:a + w], in0=n_tmp[:, (d - 1) % 2, a:a + w],
                                                       scalar=shift_of(st, d - 1, j),
                                                       in1=n_hi[:, d - 1, a:a + w].bitcast(F32),
                                                       op0=ALU.add, op1=ALU.subtract).then_inc(n_lo_ready, 1)

        def ada_load(pool, b, layer, wait=True):
            src = I["ada_w"][layer].rearrange("(k p) n -> p k n", p=P)
            for s in range(3):
                if wait:
                    pool.wait_ge(ada_used[s], b)
                pool.dma_start(ada_raw[s][:, :, :], src[:, :, bass.ds(b * BATCH + (s * ADAW - layer * NMOD * DM), ADAW)]).then_inc(ada_loaded[s], 16)

        def ada_store(pool, b):
            pool.wait_ge(rows_copied, b + 1)
            pool.dma_start(mod_dram[:, bass.ds(b * BATCH, BATCH)], ada_rows[:, :]).then_inc(rows_stored, 16)

        def ada_pool(pool, b0, nb):
            half = NBATCH // DEPTH
            ada_load(pool, b0, b0 // half, wait=b0 > 0)
            cuts = sorted({b0, min(max(half - 1, b0), b0 + nb - 1), b0 + nb - 1})
            for x, y in zip(cuts, cuts[1:]):
                with pool.Fori(x, y) as b:
                    ada_load(pool, b + 1, (x + 1) // half)
                    ada_store(pool, b)
            ada_store(pool, b0 + nb - 1)
            pool.wait_ge(rows_stored, 16 * (b0 + nb))
            n = nb * BATCH // P
            pool.dma_start(mod_rows[0:n, :, :], mod_dram[:, b0 * BATCH:(b0 + nb) * BATCH].rearrange("j (c p) -> c j p", p=P)).then_inc(mod_rows_loaded, 16)

        def ada_act(act, b):
            for s in range(3):
                act.wait_ge(ada_loaded[s], (b + 1) * 16)
                nc.scalar.copy(ada_hi[s][:, :, :], ada_raw[s][:, :, :]).then_inc(ada_hi_ready[s], 1)

        def ada_dve(dve, b):
            for s in range(3):
                dve.wait_ge(ada_hi_ready[s], b + 1)
                nc.vector.tensor_tensor(ada_lo[s][:, :, :], ada_raw[s][:, :, :], ada_hi[s][:, :, :].bitcast(F32),
                                        ALU.subtract).then_inc(ada_lo_ready[s], 1)

        def ada_pe(pe, b):
            for s in range(3):
                pe.wait_ge(ada_lo_ready[s], b + 1)
                for k in range(KD):
                    for w in (ada_hi, ada_lo):
                        last = nc.tensor.matmul(ps[0:4, 6 + s // 2, (s % 2) * ADAW:(s % 2 + 1) * ADAW], silu_r[:, k, :], w[s][:, k, :],
                                                start=(k == 0 and w is ada_hi), stop=(k == KD - 1 and w is ada_lo))
                last.then_inc(ada_used[s], 1)

        def ada_rows_act(act, b, first=False):
            for s in range(3):
                act.wait_ge(ada_used[s], b + 1)
            if not first:
                act.wait_ge(rows_stored, b * 16)
            nc.scalar.copy(ada_rows[:, :], ps[0:4, 6:8, :].rearrange("p a b -> p (a b)")[:, 0:BATCH]).then_inc(rows_copied, 1)

        def mods_pe(pe, b0):
            grp = [x for x, _ in ADA_AT].index(b0)
            n = ADA_AT[grp][1] * BATCH // P
            pe.wait_ge(mod_rows_loaded, 16 * (grp + 1))
            for j in range(2):
                for r in (j, j + 2):
                    last = nc.tensor.matmul(ps[:, 0, j * P:j * P + n], mod_rows[0:n, r, :], ident[0:n, 0:n], start=(r < 2), stop=(r >= 2))
            last.then_inc(mod_turned, 1)

        def mods_dve(dve, b0):
            grp = [x for x, _ in ADA_AT].index(b0)
            c0, n = b0 * BATCH // P, ADA_AT[grp][1] * BATCH // P
            dve.wait_ge(mod_turned, grp + 1)
            dve_link(nc.vector.tensor_tensor(mods[:, c0:c0 + n, :], ps[:, 0, 0:2 * P].rearrange("p (j c) -> p c j", c=P)[:, 0:n, :],
                                             bc(vec[:, c0:c0 + n].unsqueeze(2), [P, n, 2]), ALU.add))
            for l in range(DEPTH):
                for m, c in ((0, V_FFN1), (1, V_MIX), (2, V_FFN2)):
                    sc = (l * NMOD + 3 * m + 1) * KD
                    if c0 < sc + KD <= c0 + n:
                        dve_link(nc.vector.scalar_tensor_tensor(out=gain[:, l, m], in0=mods[:, sc:sc + KD, :], scalar=1.0,
                                                                in1=bc(vec[:, c + l * KD:c + (l + 1) * KD].unsqueeze(2), [P, KD, 2]),
                                                                op0=ALU.add, op1=ALU.mult))
                for m in range(2):
                    gc = (l * NMOD + 6 * m + 2) * KD
                    if c0 < gc + KD <= c0 + n:
                        dve_link(nc.vector.tensor_scalar(half_gate[:, l, m], mods[:, gc:gc + KD, :], 0.5, None, ALU.mult))

        def wi_src(st, s, g, part):
            w = I["ffn1_wi" if st["which"] == 0 else "ffn2_wi"][st["l"]].rearrange("(k p) n -> p k n", p=P)
            return w[:, :, bass.ds(g * 256 + (s * P + part * FFN), P)]

        def wo_src(st, g):
            w = I["ffn1_wo" if st["which"] == 0 else "ffn2_wo"][st["l"]].rearrange("(k p) n -> p k n", p=P)
            return w[:, bass.ds(g * 2, 2), :]

        def ffn_load_wi(sp, st, s, g):
            for part in range(2):
                sp.dma_start(wi_raw[s][:, :, part * P:(part + 1) * P], wi_src(st, s, g, part)).then_inc(wi_loaded[s], 16)

        def ffn_sync(sp, i, st):
            g0 = st["g0"]
            for s in range(2):
                wait_slot_used(sp, i, s)
                ffn_load_wi(sp, st, s, 0)
            if i > 0 and info[i - 1]["kind"] == "mix":
                for e in ("pe", "act", "dve"):
                    sp.wait_ge(fence[e], 6 * (info[i - 1]["k"] + 1))
            elif g0:
                sp.wait_ge(down_end, g0)
            sp.dma_start(wo_raw[:, :, :], wo_src(st, 0)).then_inc(wo_loaded, 16)
            sp.wait_ge(up_done[0], g0 + 1)
            ffn_load_wi(sp, st, 0, 1)

            def body(g, more):
                sp.wait_ge(up_done[1], g0 + g)
                ffn_load_wi(sp, st, 1, g)
                if more:
                    sp.wait_ge(up_done[0], g0 + g + 1)
                    ffn_load_wi(sp, st, 0, g + 1)
                sp.wait_ge(down_end, g0 + g)
                sp.dma_start(wo_raw[:, :, :], wo_src(st, g)).then_inc(wo_loaded, 16)

            with sp.Fori(1, FG - 1) as g:
                body(g, True)
            body(FG - 1, False)

        def ffn_pe(pe, i, st):
            g0, segs, ns = st["g0"], st["segs"], len(st["segs"])
            if st["kind"] == "ffn" and i > 0 and info[i - 1]["kind"] == "mix":
                wait_h(pe, i, KD - 1)

            def up(s, g, first):
                pe.wait_ge(wi_lo_ready[s], st["units"] + g + 1)
                if first:
                    if g0:
                        pe.wait_ge(prod_ready[s], g0)
                else:
                    pe.wait_ge(prod_ready[s], g0 + g)
                for part in range(2):
                    for k in range(KD):
                        if first and s == 0 and part == 0:
                            pe.wait_ge(n_lo_ready, n_count(i) - (KD - 1 - k) * ns)
                        cols = slice(part * P, (part + 1) * P)
                        for w, n in ((wi_hi, n_hi), (wi_hi, n_lo), (wi_lo, n_hi)):
                            for j, (a, width) in enumerate(segs):
                                o = ps[:, 3 * s + part, 0:width] if j == 0 else ps[:, 3 * s + 2, part * CTX:(part + 1) * CTX]
                                last = nc.tensor.matmul(o, w[s][:, k, cols], n[:, k, a:a + width],
                                                        start=(k == 0 and n is n_hi and w is wi_hi),
                                                        stop=(k == KD - 1 and w is wi_lo))
                last.then_inc(up_done[s], 1)

            def down(g):
                if st["ada"]:
                    pe.wait_ge(rows_copied, g + st["ada"][0])
                pe.wait_ge(wo_lo_ready, g0 + g + 1)
                pe.wait_ge(g_lo_ready[1], g0 + g + 1)
                for d in range(KD):
                    for j, (a, width) in enumerate(segs):
                        n = d * ns + j
                        pe.wait_ge(h_added, g * st["nj"] + (st["jobs"] + max(0, n - 1)))
                        for f in range(2):
                            for w, x in ((wo_hi, g_hi), (wo_hi, g_lo), (wo_lo, g_hi)):
                                last = nc.tensor.matmul(ps[:, 6 + n % 2, 0:width], w[:, f, d * P:(d + 1) * P],
                                                        x[:, f, a:a + width], start=(f == 0 and w is wo_hi and x is g_hi),
                                                        stop=(f == 1 and w is wo_lo))
                        last.then_inc(down_end if n == st["nj"] - 1 else down_done, 1)

            up(0, 0, True)
            up(1, 0, True)
            with pe.Fori(1, FG) as g:
                up(0, g, False)
                down(g - 1)
                up(1, g, False)
                if st["ada"]:
                    pe.wait_ge(h_added, g * st["nj"] + st["jobs"])
                    ada_pe(pe, g + (st["ada"][0] - 1))
            down(FG - 1)
            if st["ada"]:
                mods_pe(pe, st["ada"][0])

        def ffn_act(act, i, st):
            g0, w = st["g0"], ncols(st["segs"])

            def split_wo(g):
                act.wait_ge(wo_loaded, (g + (g0 + 1)) * 16)
                nc.scalar.copy(wo_hi[:, :, :], wo_raw[:, :, :]).then_inc(wo_hi_ready, 1)

            def split_wi(s, g):
                act_split(act, s, g + (st["units"] + 1))

            def gate(s, g, used=False, first=False):
                act.wait_ge(up_done[s], g + (g0 + 1))
                if g0 or not first:
                    act.wait_ge(g_lo_ready[s], g + g0)
                for j, (a, width) in enumerate(st["segs"]):
                    src = ps[:, 3 * s, 0:width] if j == 0 else ps[:, 3 * s + 2, 0:CTX]
                    last = nc.scalar.activation(silu_a[:, s, a:a + width], src, ACT.Silu)
                last.then_inc(silu_ready[s], 1)
                act.wait_ge(prod_ready[s], g + (g0 + 1))
                if used:
                    act.wait_ge(down_end, g + g0)
                nc.scalar.copy(g_hi[:, s, 0:w], prod[:, s, 0:w]).then_inc(g_hi_ready[s], 1)

            def body(g, rows):
                split_wo(g - 1)
                split_wi(0, g)
                gate(1, g - 1, first=isinstance(g, int) and g == 1)
                if rows:
                    ada_rows_act(act, g + (st["ada"][0] - 2))
                split_wi(1, g)
                gate(0, g, used=True)
                if st["ada"]:
                    ada_act(act, g + (st["ada"][0] - 1))

            gate(0, 0, first=True)
            if st["ada"]:
                body(1, False)
            with act.Fori(2 if st["ada"] else 1, FG) as g:
                body(g, st["ada"])
            split_wo(FG - 1)
            gate(1, FG - 1)
            if st["ada"]:
                ada_rows_act(act, st["ada"][0] + FG - 2)

        def ffn_dve(dve, i, st):
            g0, w, ns = st["g0"], ncols(st["segs"]), len(st["segs"])

            def split_wo(g):
                dve.wait_ge(wo_hi_ready, g + (g0 + 1))
                nc.vector.tensor_tensor(wo_lo[:, :, :], wo_raw[:, :, :], wo_hi[:, :, :].bitcast(F32),
                                        ALU.subtract).then_inc(wo_lo_ready, 1)

            def split_wi(s, g):
                dve_split(dve, s, g + (st["units"] + 1))

            def gate(s, g):
                dve.wait_ge(silu_ready[s], g + (g0 + 1))
                for j, (a, width) in enumerate(st["segs"]):
                    src = ps[:, 3 * s + 1, 0:width] if j == 0 else ps[:, 3 * s + 2, CTX:2 * CTX]
                    last = nc.vector.tensor_tensor(prod[:, s, a:a + width], silu_a[:, s, a:a + width], src, ALU.mult)
                last.then_inc(prod_ready[s], 1)
                dve.wait_ge(g_hi_ready[s], g + (g0 + 1))
                nc.vector.tensor_tensor(g_lo[:, s, 0:w], prod[:, s, 0:w], g_hi[:, s, 0:w].bitcast(F32),
                                        ALU.subtract).then_inc(g_lo_ready[s], 1)

            def add(g):
                for d in range(KD):
                    for j, (a, width) in enumerate(st["segs"]):
                        n = d * ns + j
                        if n == st["nj"] - 1:
                            dve.wait_ge(down_end, g + (g0 + 1))
                        else:
                            dve.wait_ge(down_done, g * (st["nj"] - 1) + (st["jobs"] - 1 - g0 + n + 1))
                        nc.vector.scalar_tensor_tensor(out=h[:, d, a:a + width], in0=ps[:, 6 + n % 2, 0:width],
                                                       scalar=half_gate[:, st["l"], st["which"], d, j:j + 1],
                                                       in1=h[:, d, a:a + width], op0=ALU.mult,
                                                       op1=ALU.add).then_inc(h_added, 1)

            gate(0, 0)
            with dve.Fori(1, FG) as g:
                split_wo(g - 1)
                split_wi(0, g)
                gate(1, g - 1)
                split_wi(1, g)
                add(g - 1)
                gate(0, g)
                if st["ada"]:
                    ada_dve(dve, g + (st["ada"][0] - 1))
            split_wo(FG - 1)
            gate(1, FG - 1)
            add(FG - 1)
            if st["ada"]:
                mods_dve(dve, st["ada"][0])

        def mix_load(sp, i, st, u):
            l, s = st["l"], u % 2
            wait_slot_used(sp, i, u)
            if u < NU:
                w = I["w_in"][l].rearrange("(k p) n -> p k n", p=P)
                pieces = UNITS[u][1]
                if len(pieces) == 1:
                    c, n, _ = pieces[0]
                    pieces = [(c, n // 2, 0), (c + n // 2, n // 2, 0)]
            else:
                w = I["w_out"][l].rearrange("(k p) n -> p k n", p=P)
                pieces = [((u - NU) * 256, P, 0), ((u - NU) * 256 + P, P, 0)]
            o = 0
            for c, n, _ in pieces:
                sp.dma_start(wi_raw[s][:, :, o:o + n], w[:, :, c:c + n]).then_inc(wi_loaded[s], 16)
                o += n

        def mix_sync(sp, i, st):
            l = st["l"]
            for u in range(NU + 2):
                mix_load(sp, i, st, u)
            sp.wait_ge(fence["pe"], st["k"] * 6 + 1)
            sp.wait_ge(fence["act"], st["k"] * 6 + 1)
            sp.wait_ge(fence["dve"], st["k"] * 6 + 1)
            sp.dma_start(w_uq[:, :, :], I["c_w_uq"][l].rearrange("(k p) n -> p k n", p=P)).then_inc(wc_loaded, 16)
            sp.dma_start(w_ukv[:, :], I["c_w_ukv"][l]).then_inc(wc_loaded, 16)
            if DEBUG:
                for e in ("pe", "act", "dve"):
                    sp.wait_ge(fence[e], st["k"] * 6 + 5)
                sp.dma_start(DEBUG["tok"][st["k"]], tok[:, :, :]).then_inc(wc_loaded, 16)
            for u in range(NU + 2, NU + OUTU):
                mix_load(sp, i, st, u)

        def proj_jobs():
            for u, (kind, _) in enumerate(UNITS):
                for t in range(NT if kind == "tok" else 4):
                    yield u, t, kind

        def mix_proj_pe(pe, i, st):
            for n, (u, t, kind) in enumerate(proj_jobs()):
                s = u % 2
                if t == 0:
                    pe.wait_ge(wi_lo_ready[s], st["units"] + u // 2 + 1)
                if n == 0:
                    wait_h(pe, i, KD - 1)
                m = st["proj"] + n
                if m >= 8:
                    pe.wait_ge(proj_copied, m - 7)
                w = unit_w(u)
                for k in range(KD):
                    if n == 0:
                        pe.wait_ge(n_lo_ready, n_count(i) - (KD - 1 - k) * 2)
                    if kind == "tok":
                        for q, (x, y) in enumerate(((n_hi, wi_hi), (n_hi, wi_lo), (n_lo, wi_hi))):
                            last = nc.tensor.matmul(ps[:, m % 8, 0:w], x[:, k, t * P:(t + 1) * P], y[s][:, k, 0:w],
                                                    start=(k == 0 and q == 0), stop=(k == KD - 1 and q == 2))
                    else:
                        f, (a, width) = t // 2, SEGS[t % 2]
                        for q, (x, y) in enumerate(((n_hi, wi_hi), (n_lo, wi_hi), (n_hi, wi_lo))):
                            last = nc.tensor.matmul(ps[:, m % 8, 0:width], y[s][:, k, f * P:(f + 1) * P],
                                                    x[:, k, a:a + width], start=(k == 0 and q == 0),
                                                    stop=(k == KD - 1 and q == 2))
                last.then_inc(proj_done, 1)

        def mix_proj_act(act, i, st):
            for n, (u, t, kind) in enumerate(proj_jobs()):
                m = st["proj"] + n
                act.wait_ge(proj_done, m + 1)
                if kind == "tok":
                    o = 0
                    for _, w, c in UNITS[u][1]:
                        last = nc.scalar.copy(tok[:, t, c:c + w], ps[:, m % 8, o:o + w])
                        o += w
                else:
                    f, j = t // 2, t % 2
                    a, width = SEGS[j]
                    if n == 0:
                        act.wait_ge(dve_act, st["k"] * 2 + 1)
                    c = 2 + conv_col(0 if j == 0 else NX)
                    last = nc.scalar.copy(xbc[:, UNITS[u][1][0][2] + f, c:c + width], ps[:, m % 8, 0:width])
                last.then_inc(proj_copied, 1)
                if t == (NT if kind == "tok" else 4) - 1 and u + 2 < NU + 2:
                    act_split(act, u % 2, st["units"] + (u + 2) // 2 + 1, unit_w(u + 2))
                if t == (NT if kind == "tok" else 4) - 1 and 1 <= u <= 3:
                    for j in (2 * u - 2, 2 * u - 1):
                        act.wait_ge(conv_ready, st["k"] * 6 + j + 1)
                        cb_ = V_CONVB + st["l"] * 6 + j
                        nc.scalar.activation(xbc[:, j, 0:XW - 4], conv_acc[:, j % 2, :], ACT.Silu,
                                             bias=vec[:, cb_:cb_ + 1]).then_inc(xbc_ready, 1)

        def mix_conv_dve(dve, st, j):
            l = st["l"]
            if st["k"] * 6 + j >= 2:
                dve.wait_ge(xbc_ready, st["k"] * 6 + j - 1)
            for k in range(5):
                wcol = vec[:, V_CONVW + (l * 5 + k) * 6 + j:V_CONVW + (l * 5 + k) * 6 + j + 1]
                src = xbc[:, j, k:k + XW - 4]
                if k == 0:
                    dve_link(nc.vector.tensor_scalar(conv_acc[:, j % 2, :], src, wcol, None, ALU.mult))
                else:
                    ins = nc.vector.scalar_tensor_tensor(out=conv_acc[:, j % 2, :], in0=src, scalar=wcol,
                                                         in1=conv_acc[:, j % 2, :], op0=ALU.mult, op1=ALU.add)
                    if k < 4:
                        dve_link(ins)
                    else:
                        ins.then_inc(conv_ready, 1)

        def mix_proj_dve(dve, i, st):
            base = 0
            for u, (kind, _) in enumerate(UNITS):
                n = NT if kind == "tok" else 4
                dve.wait_ge(proj_copied, st["proj"] + base + n)
                base += n
                if u + 2 < NU + 2:
                    dve_split(dve, u % 2, st["units"] + (u + 2) // 2 + 1, unit_w(u + 2))
                if kind == "conv":
                    mix_conv_dve(dve, st, 2 * u)
                    mix_conv_dve(dve, st, 2 * u + 1)

        def rope(link, eng, x1, x2, c, s, t1, t2):
            link(eng.tensor_tensor(t1, x1, s, ALU.mult))
            link(eng.tensor_tensor(t2, x2, s, ALU.mult))
            link(eng.tensor_tensor(x1, x1, c, ALU.mult))
            link(eng.tensor_tensor(x2, x2, c, ALU.mult))
            link(eng.tensor_tensor(x1, x1, t2, ALU.subtract))
            return eng.tensor_tensor(x2, x2, t1, ALU.add)

        def rope_heads(link, eng, col):
            v = tok[:, 0:NX, col:col + 384].rearrange("p t (h f x e) -> p t h f x e", f=2, x=2, e=16)
            cc = C("cosh").rearrange("p (t f e) -> p t f e", t=NX, f=2)
            ss = C("sinh").rearrange("p (t f e) -> p t f e", t=NX, f=2)
            t1 = m_tmp[:, 0:NX, 0:96].rearrange("p t (h e) -> p t h e", e=16)
            t2 = m_tmp[:, 0:NX, 96:192].rearrange("p t (h e) -> p t h e", e=16)
            for f in range(2):
                last = rope(link, eng, v[:, :, :, f, 0], v[:, :, :, f, 1], cc[:, :, f].unsqueeze(2).broadcast_to([P, NX, 6, 16]),
                            ss[:, :, f].unsqueeze(2).broadcast_to([P, NX, 6, 16]), t1, t2)
                if f == 0:
                    link(last)
            return last

        chain_n = {"dve": 0, "act": 0, "pool": 0}

        def make_link(key, eng, s):
            def link(ins):
                chain_n[key] += 1
                ins.then_inc(s, 1)
                eng.wait_ge(s, chain_n[key])
            return link

        dve_link = make_link("dve", nc.vector, dve_chain)
        act_link = make_link("act", nc.scalar, act_chain)
        pool_link = make_link("pool", nc.gpsimd, pool_chain)

        def bc(ap, shape):
            return ap.broadcast_to(shape)

        FCH = {0: [4, 5, 0, 1, 2, 3], 1: [5, 4, 3, 2, 1, 0]}

        def scan_dve(dve, i, st):
            l, k, nq = st["l"], st["k"], st["nq"]
            v = small[:, 0:48].rearrange("p (t e) -> p t e", t=NT)
            na = small[:, 48:96].rearrange("p (t e) -> p t e", t=NT)
            dt = small[:, 144:192].rearrange("p (t e) -> p t e", t=NT)
            a = small[:, 192:240].rearrange("p (t e) -> p t e", t=NT)
            row = lambda name, w: bc(R(l, name).unsqueeze(1), [P, NT, w])
            dve_link(nc.vector.tensor_tensor(v, tok[:, :, DT0:DT0 + 8], row("d_dt_bias", 8), ALU.add))
            nc.vector.scalar_tensor_tensor(out=na, in0=v, scalar=-1.0, in1=v, op0=ALU.mult, op1=ALU.min).then_inc(dve_act, 1)
            dve.wait_ge(act_dve, k * 2 + 1)
            dve_link(nc.vector.scalar_tensor_tensor(out=dt, in0=v, scalar=0.0, in1=na, op0=ALU.max, op1=ALU.add))
            dve_link(nc.vector.scalar_tensor_tensor(out=a, in0=dt, scalar=-1.0, in1=row("d_a_log", 8), op0=ALU.mult, op1=ALU.mult))
            prep_copies(dve, 0, scan_prep(l), st["k"] * PREPS_PER_LAYER[0])
            nc.vector.tensor_copy(small[:, 240:241], small[:, 192:193]).then_inc(a_ready, 1)
            wait_prep(dve, st["prep_scan"] + len(scan_prep(l)))
            for dr in range(2):
                dtb = bc(dt[:, :, dr * 4:dr * 4 + 4].unsqueeze(3), [P, NT, 4, 64])
                ins = nc.vector.tensor_tensor(xdt[:, dr].rearrange("p t (h e) -> p t h e", e=64),
                                              xsb[:, :, 0:256].rearrange("p t (h e) -> p t h e", e=64), dtb, ALU.mult)
                dve_link(ins)
            dve.wait_ge(dt_exps, k + 1)
            ex = stat[:, 0, 0:144]
            for dr in range(2):
                dec = ex[:, 24 + 48 * dr:48 + 48 * dr].rearrange("p (t h) -> p t h", h=4)
                nc.vector.tensor_tensor(xdec[:, dr].rearrange("p t (h e) -> p t h e", e=64),
                                        xdt[:, dr].rearrange("p t (h e) -> p t h e", e=64),
                                        bc(dec.unsqueeze(3), [P, NT, 4, 64]), ALU.mult).then_inc(xdt_ready, 1)
            for dr in range(2):
                dve_link(nc.vector.memset(h_in[:, dr, FCH[dr][0], :], 0.0))
            for n in range(NT - 1):
                for dr in range(2):
                    c, nx = FCH[dr][n], FCH[dr][n + 1]
                    tot = ex[:, 96 + c * 8 + dr * 4:96 + c * 8 + dr * 4 + 4]
                    j = 2 * n + dr
                    dve_link(nc.vector.tensor_tensor(y_tmp[:, dr * 256:dr * 256 + 256].rearrange("p (h e) -> p h e", e=64),
                                                     h_in[:, dr, c, :].rearrange("p (h e) -> p h e", e=64),
                                                     bc(tot.unsqueeze(2), [P, 4, 64]), ALU.mult))
                    dve.wait_ge(st_done, k * 10 + j + 1)
                    ins = nc.vector.tensor_tensor(h_in[:, dr, nx, :], ps[:, j % 4, 0:256],
                                                  y_tmp[:, dr * 256:dr * 256 + 256], ALU.add)
                    ins.then_inc(h_in_ready, 1)
                    dve.wait_ge(h_in_ready, k * 10 + j + 1)
            cbase, ybase = st["cb"], st["y"]
            for t in range(nq):
                dve.wait_ge(cb_done, cbase + t + 1)
                for dr, m in enumerate(("le", "ge")):
                    nc.vector.tensor_tensor(cb[:, t, dr], ps[:, 4 + t % 2, 0:256].rearrange("p (g i) -> p g i", g=2),
                                            bc(C(m).unsqueeze(1), [P, 2, P]), ALU.mult).then_inc(cb_ready, 1)
            def build(j):
                t, dr = j // 2, j % 2
                if j >= 2:
                    dve.wait_ge(seg_done, cbase * 2 + j - 1)
                av = a[:, t, dr * 4:dr * 4 + 4]
                nc.vector.tensor_tensor(seg_rhs[:, j % 2, :].rearrange("p (h i) -> p h i", h=4),
                                        bc(C("le" if dr == 0 else "ge").unsqueeze(1), [P, 4, P]),
                                        bc(av.unsqueeze(2), [P, 4, P]), ALU.mult).then_inc(seg_in, 1)
            build(0)
            build(1)
            dve.wait_ge(cb_ready, 2 * (cbase + nq))
            for t in range(nq):
                for dr in range(2):
                    j = 2 * t + dr
                    dve.wait_ge(seg_exp, cbase * 2 + j + 1)
                    d4 = decay[:, dr, :].rearrange("p (g r i) -> p g r i", g=2, r=2)
                    for g in range(2):
                        last = nc.vector.tensor_tensor(d4[:, g], d4[:, g], bc(cb[:, t, dr, g].unsqueeze(1), [P, 2, P]), ALU.mult)
                    last.then_inc(m_ready, 1)
                    if j + 2 < 2 * nq:
                        build(j + 2)
                dve.wait_ge(y_done, ybase + t + 1)
                o4 = ps[:, 6, :].rearrange("p (d h e) -> p d h e", d=2, h=4)
                e4 = ex[:, 0:96].rearrange("p (d x t h) -> p d x t h", d=2, x=2, t=NT)[:, :, 0, t]
                y4 = y_tmp[:, :].rearrange("p (d h e) -> p d h e", d=2, h=4)
                dve_link(nc.vector.tensor_tensor(y4, o4, bc(e4.unsqueeze(3), [P, 2, 4, 64]), ALU.mult))
                dve_link(nc.vector.tensor_tensor(y_tmp[:, 0:256], y_tmp[:, 0:256], y_tmp[:, 256:512], ALU.add))
                dve_link(nc.vector.tensor_tensor(y_tmp[:, 0:256], y_tmp[:, 0:256], ps[:, 7, 0:256], ALU.add))
                dve_link(nc.vector.tensor_tensor(y_tmp[:, 256:512].rearrange("p (h e) -> p h e", h=4),
                                                 xsb[:, t, 0:256].rearrange("p (h e) -> p h e", h=4),
                                                 bc(R(l, "d_skip").unsqueeze(2), [P, 4, 64]), ALU.mult))
                dve_link(nc.vector.tensor_tensor(y_tmp[:, 0:256], y_tmp[:, 0:256], y_tmp[:, 256:512], ALU.add))
                dve_link(nc.vector.tensor_tensor(tok[:, t, Z0:Z0 + 256], tok[:, t, Z0:Z0 + 256], y_tmp[:, 0:256], ALU.mult))
                dve_link(nc.vector.tensor_tensor(y_tmp[:, 0:256], tok[:, t, Z0:Z0 + 256], tok[:, t, Z0:Z0 + 256], ALU.mult))
                nc.vector.tensor_reduce(small[:, 256 + t:257 + t], y_tmp[:, 0:256], AX_X, ALU.add).then_inc(y_ready, 1)
                dve.wait_ge(y_ready, ybase + t + 1)
            dve.wait_ge(act_dve, k * 2 + 2)
            dve_link(nc.vector.tensor_tensor(tok[:, 0:nq, Z0:Z0 + 256], tok[:, 0:nq, Z0:Z0 + 256],
                                             bc(small[:, 256:256 + nq].unsqueeze(2), [P, nq, 256]), ALU.mult))
            dve_link(nc.vector.tensor_tensor(tok[:, 0:nq, Z0:Z0 + 256], tok[:, 0:nq, Z0:Z0 + 256],
                                             bc(R(l, "d_out_norm").unsqueeze(1), [P, nq, 256]), ALU.mult))

        def scan_act(act, i, st):
            l, k, nq = st["l"], st["k"], st["nq"]
            na = small[:, 48:96]
            act.wait_ge(dve_act, k * 2 + 2)
            act_link(nc.scalar.activation(na, na, ACT.Exp))
            nc.scalar.activation(na, na, ACT.Ln, bias=1.0).then_inc(act_dve, 1)
            prep_copies(act, 1, scan_prep(l), st["k"] * PREPS_PER_LAYER[0])
            act.wait_ge(dt_sums, k + 1)
            nc.scalar.activation(stat[:, 0, 0:144], ps[:, 0, 0:144], ACT.Exp).then_inc(dt_exps, 1)
            cbase = st["cb"]
            for t in range(nq):
                for dr in range(2):
                    j = 2 * t + dr
                    act.wait_ge(seg_done, cbase * 2 + j + 1)
                    if t > 0:
                        act.wait_ge(y_done, st["y"] + t)
                    nc.scalar.activation(decay[:, dr, :], ps[:, 4 + dr, :], ACT.Exp).then_inc(seg_exp, 1)
            act.wait_ge(y_ready, st["y"] + nq)
            act_link(nc.scalar.activation(small[:, 256:256 + nq], small[:, 256:256 + nq], ACT.Ln, bias=eps[:, 0:1], scale=1.0 / 256))
            nc.scalar.activation(small[:, 256:256 + nq], small[:, 256:256 + nq], ACT.Exp, scale=-0.5).then_inc(act_dve, 1)

        def scan_pe(pe, i, st):
            k, nq = st["k"], st["nq"]
            prep_pe(pe, scan_prep(st["l"]), st["prep_scan"])
            pe.wait_ge(a_ready, k + 1)
            a = small[:, 192:240].rearrange("p (t d h) -> p t d h", t=NT, d=2)
            for n, (m, dr) in enumerate((("le", 0), ("gt", 0), ("ge", 1), ("lt", 1))):
                nc.tensor.matmul(ps[:, 0, 24 * n:24 * n + 24].rearrange("p (t h) -> p t h", h=4), C(m), a[:, :, dr, :],
                                 start=True, stop=True)
            nc.tensor.matmul(ps[:, 0, 96:144], ones, small[:, 192:240], start=True, stop=True).then_inc(dt_sums, 1)
            pe.wait_ge(dt_exps, k + 1)
            for n in range(NT - 1):
                for dr in range(2):
                    j, c = 2 * n + dr, FCH[dr][n]
                    pe.wait_ge(xdt_ready, k * 2 + dr + 1)
                    if j >= 4:
                        pe.wait_ge(h_in_ready, k * 10 + j - 3)
                    for g in range(2):
                        last = nc.tensor.matmul(ps[:, j % 4, g * P:(g + 1) * P], xsb[:, c, 256 + g * P:256 + (g + 1) * P],
                                                xdec[:, dr, c, g * P:(g + 1) * P], start=True, stop=True)
                    last.then_inc(st_done, 1)
            wait_prep(pe, st["prep_scan"] + len(scan_prep(st["l"])))
            for t in range(nq):
                c = conv_col(t)
                if t >= 2:
                    pe.wait_ge(cb_ready, 2 * (st["cb"] + t - 1))
                for g in range(2):
                    last = nc.tensor.matmul(ps[:, 4 + t % 2, g * P:(g + 1) * P], xbc[:, 2 + g, c:c + P], xbc[:, 4 + g, c:c + P],
                                            start=True, stop=True)
                last.then_inc(cb_done, 1)
            pe.wait_ge(cb_ready, 2 * (st["cb"] + nq))
            pe.wait_ge(h_in_ready, (k + 1) * 10)

            def seg(j):
                pe.wait_ge(seg_in, st["cb"] * 2 + j + 1)
                if j >= 2:
                    pe.wait_ge(seg_exp, st["cb"] * 2 + j - 1)
                nc.tensor.matmul(ps[:, 4 + j % 2, :], C("gt" if j % 2 == 0 else "lt"), seg_rhs[:, j % 2, :],
                                 start=True, stop=True).then_inc(seg_done, 1)
            seg(0)
            seg(1)
            for t in range(nq):
                if t > 0:
                    pe.wait_ge(y_ready, st["y"] + t)
                c = conv_col(t)
                for dr in range(2):
                    for g in range(2):
                        nc.tensor.matmul(ps[:, 6, dr * 256 + g * P:dr * 256 + (g + 1) * P], xbc[:, 4 + g, c:c + P],
                                         h_in[:, dr, t, g * P:(g + 1) * P], start=True, stop=True)
                pe.wait_ge(m_ready, 2 * (st["cb"] + t + 1))
                for hd in range(4):
                    for dr in range(2):
                        last = nc.tensor.matmul(ps[:, 7, hd * 64:(hd + 1) * 64], decay[:, dr, hd * P:(hd + 1) * P],
                                                xdt[:, dr, t, hd * 64:(hd + 1) * 64], start=(dr == 0), stop=(dr == 1))
                last.then_inc(y_done, 1)
                if t + 1 < nq:
                    seg(2 * t + 2)
                    seg(2 * t + 3)

        def scan_prep(l):
            jobs_ = []
            for t in range(NT):
                c = conv_col(t)
                mm = [("T", q * P, P, xbc[:, q, c:c + P]) for q in range(4)]
                jobs_.append((P, mm, [(xsb[:, t, :], 0, 512, None)]))
            return jobs_

        def qk_prep(name, nq):
            jobs_ = []
            K = 96 if name == "c" else 64
            for hd in range(8 if name == "c" else 6):
                for part, (t0, t1) in enumerate(((0, NX), (NX, NT))):
                    if hd < 4 and t0 >= nq:
                        continue
                    mm = []
                    for t in range(t0, t1):
                        if name == "c":
                            src = (qc if hd < 4 else kc)[:, t, hd % 4, :]
                        else:
                            col = (A0 if name == "a" else B0) + hd * 64
                            src = tok[:, t, col:col + 64]
                        mm.append(("T", (t - t0) * P, P, src))
                    jobs_.append((K, mm, [(qkT[0:K, hd, t0 * P:t1 * P], 0, (t1 - t0) * P, None)]))
            return jobs_

        def latent_prep():
            jobs_ = []
            for f in range(3):
                for t0, t1 in ((0, NX), (NX, NT)):
                    mm = [("T", (t - t0) * P, P, tok[:, t, C0 + f * P:C0 + (f + 1) * P]) for t in range(t0, t1)]
                    jobs_.append((P, mm, [(cT[:, f, t0 * P:t1 * P], 0, (t1 - t0) * P, None)]))
            return jobs_

        def up_prep(nq):
            jobs_ = []
            for t in range(NT):
                if t < nq:
                    mm = [("M", 0, 384, cT[:, f, t * P:(t + 1) * P], w_uq[:, f, :], f == 0, f == 1) for f in range(2)]
                    jobs_.append((P, mm, [(qc[:, t], 0, 384, 96)]))
                mm = [("M", 0, 512, cT[:, 2, t * P:(t + 1) * P], w_ukv[:, :], True, True)]
                jobs_.append((P, mm, [(kc[:, t, :, 0:64], 0, 64, 128), (vc[:, t, :].rearrange("p (h e) -> p h e", e=64), 64, 128, 128)]))
            return jobs_

        def prep_pe(pe, jobs_, n0):
            for n, (K, mm, _) in enumerate(jobs_):
                m = n0 + n
                if m >= 4:
                    pe.wait_ge(prep_copied[m % 2], (m - 4) // 2 + 1)
                for x in mm:
                    o = ps[0:K, 4 + m % 4, x[1]:x[1] + x[2]]
                    if x[0] == "T":
                        last = nc.tensor.transpose(o, x[3], ident)
                    else:
                        last = nc.tensor.matmul(o, x[3], x[4], start=x[5], stop=x[6])
                last.then_inc(prep_done, 1)

        def prep_copies(eng, me, jobs_, n0):
            for n, (K, _, copies) in enumerate(jobs_):
                m = n0 + n
                if m % 2 != me:
                    continue
                eng.wait_ge(prep_done, m + 1)
                for dst, a, b, per in copies:
                    bank = ps[0:K, 4 + m % 4, :]
                    src = bank[:, a:b]
                    if per == 96:
                        src = src.rearrange("p (h e) -> p h e", e=96)
                    elif per == 128:
                        src = bank.rearrange("p (h e) -> p h e", e=128)[:, :, a:b]
                    last = (nc.vector.tensor_copy if me == 0 else nc.scalar.copy)(dst, src)
                last.then_inc(prep_copied[me], 1)

        def wait_prep(eng, n):
            eng.wait_ge(prep_copied[0], (n + 1) // 2)
            if n // 2:
                eng.wait_ge(prep_copied[1], n // 2)

        SPEC = {"a": dict(K=64, v=384, o=A0, scale=HD ** -0.5), "b": dict(K=64, v=B0 + 384, o=B0, scale=HD ** -0.5),
                "c": dict(K=96, v=None, o=C0, scale=96 ** -0.5)}

        def att_steps(name, nq):
            for hd in range(4):
                for t in range(nq):
                    if t >= NX:
                        loc = []
                    elif name == "a":
                        loc = list(range(max(0, t - 1), min(NX, t + 2)))
                    else:
                        loc = list(range(NX))
                    yield hd, t, loc

        def att_pe(pe, st, name):
            sp_, K = SPEC[name], SPEC[name]["K"]
            steps = list(att_steps(name, st["nq"]))
            base = st["att_" + name]
            wait_prep(pe, st["prep_" + name + "_end"])

            def kT(hd):
                return 4 + (hd if name == "c" else hd // 2)

            def scores(n):
                hd, t, loc = steps[n]
                m = base + n
                if m >= 2:
                    pe.wait_ge(exp_done, m - 1)
                b = 2 * (m % 2)
                q = qkT[0:K, hd, t * P:(t + 1) * P]
                if loc:
                    w = len(loc) * P
                    masks = [(x, "prev" if x < t else "next") for x in loc if name == "a" and x != t]
                    nc.tensor.matmul(ps[:, b, 512 - w:512], q, qkT[0:K, kT(hd), loc[0] * P:loc[0] * P + w],
                                     start=True, stop=not masks, skip_group_check=True)
                    for y, (x, mk) in enumerate(masks):
                        c = 512 - w + (x - loc[0]) * P
                        nc.tensor.matmul(ps[:, b, c:c + P], ident, C(mk), start=False, stop=y == len(masks) - 1,
                                         skip_group_check=True)
                nc.tensor.matmul(ps[:, b + 1, 0:CTX], q, qkT[0:K, kT(hd), SEQ:TOK], start=True, stop=True).then_inc(s_done, 1)

            def transposes(n):
                hd, t, loc = steps[n]
                m = base + n
                pe.wait_ge(exp_done, m + 1)
                if m >= 1:
                    pe.wait_ge(t_copied_x, m)
                    pe.wait_ge(t_copied_c, m)
                w = len(loc) * P
                for x in range(len(loc)):
                    c = 512 - w + x * P
                    nc.tensor.transpose(ps[:, 4, c:c + P], probs[:, m % 2, c:c + P], ident)
                for x in range(2):
                    last = nc.tensor.transpose(ps[:, 5, x * P:(x + 1) * P], probs[:, m % 2, 512 + x * P:512 + (x + 1) * P], ident)
                last.then_inc(t_done, 1)

            def values(n):
                hd, t, loc = steps[n]
                m = base + n
                pe.wait_ge(t_copied_x, m + 1)
                pe.wait_ge(t_copied_c, m + 1)
                if m >= 2:
                    pe.wait_ge(o_ready, m - 1)
                w = len(loc) * P
                keys = [(512 - w + y * P, x) for y, x in enumerate(loc)] + [(512, NX), (512 + P, NX + 1)]
                for y, (c, x) in enumerate(keys):
                    if name == "c":
                        v = vc[:, x, hd * 64:(hd + 1) * 64]
                    else:
                        v = tok[:, x, sp_["v"] + (hd // 2) * 64:sp_["v"] + (hd // 2) * 64 + 64]
                    last = nc.tensor.matmul(ps[:, 6 + m % 2, 0:64], probsT[:, m % 2, c:c + P], v,
                                            start=(y == 0), stop=(y == len(keys) - 1))
                last.then_inc(pv_done, 1)

            scores(0)
            for n in range(len(steps)):
                if n + 1 < len(steps):
                    scores(n + 1)
                transposes(n)
                if n >= 1:
                    values(n - 1)
            values(len(steps) - 1)

        def att_act(act, st, name):
            steps = list(att_steps(name, st["nq"]))
            base, sc = st["att_" + name], SPEC[name]["scale"]
            for n in range(len(steps) + 1):
                if n < len(steps):
                    hd, t, loc = steps[n]
                    m = base + n
                    w = len(loc) * P
                    act.wait_ge(bias_ready, m + 1)
                    if m >= 2:
                        act.wait_ge(t_done, m - 1)
                    col = 0 if name != "a" else 1
                    if name == "a":
                        nc.scalar.activation(stat[:, 3, n:n + 1], R(st["l"], "a_sink")[:, hd:hd + 1], ACT.Exp,
                                             bias=stat[:, 1, n:n + 1])
                    src = ps[:, 2 * (m % 2):2 * (m % 2) + 2, :].rearrange("p a b -> p (a b)")
                    nc.scalar.activation(probs[:, m % 2, 512 - w:TOK], src[:, 512 - w:TOK], ACT.Exp, bias=stat[:, 1, n:n + 1],
                                         scale=sc, accum_out=stat[:, 2, n:n + 1]).then_inc(exp_done, 1)
                if n >= 1:
                    m = base + n - 1
                    act.wait_ge(t_done, m + 1)
                    if m >= 2:
                        act.wait_ge(pv_done, m - 1)
                    nc.scalar.copy(probsT[:, m % 2, 512:TOK], ps[:, 5, 0:CTX]).then_inc(t_copied_c, 1)

        def att_dve(dve, st, name):
            steps = list(att_steps(name, st["nq"]))
            base, sc = st["att_" + name], SPEC[name]["scale"]
            for n in range(len(steps) + 2):
                if n < len(steps):
                    hd, t, loc = steps[n]
                    m = base + n
                    w = len(loc) * P
                    dve.wait_ge(s_done, m + 1)
                    src = ps[:, 2 * (m % 2):2 * (m % 2) + 2, :].rearrange("p a b -> p (a b)")
                    dve_link(nc.vector.tensor_reduce(stat[:, 0, n:n + 1], src[:, 512 - w:TOK], AX_X, ALU.max))
                    if name == "a":
                        dve_link(nc.vector.tensor_scalar(stat[:, 0, n:n + 1], stat[:, 0, n:n + 1], sc,
                                                         R(st["l"], "a_sink")[:, hd:hd + 1], ALU.mult, ALU.max))
                        nc.vector.tensor_scalar(stat[:, 1, n:n + 1], stat[:, 0, n:n + 1], -1.0, None, ALU.mult).then_inc(bias_ready, 1)
                    else:
                        nc.vector.tensor_scalar(stat[:, 1, n:n + 1], stat[:, 0, n:n + 1], -sc, None, ALU.mult).then_inc(bias_ready, 1)
                if 1 <= n <= len(steps):
                    hd, t, loc = steps[n - 1]
                    m = base + n - 1
                    w = len(loc) * P
                    dve.wait_ge(t_done, m + 1)
                    if m >= 2:
                        dve.wait_ge(pv_done, m - 1)
                    if w:
                        nc.vector.tensor_copy(probsT[:, m % 2, 512 - w:512], ps[:, 4, 512 - w:512]).then_inc(t_copied_x, 1)
                    else:
                        nc.vector.tensor_copy(stat[:, 0, 150:151], stat[:, 1, n - 1:n]).then_inc(t_copied_x, 1)
                    if name == "a":
                        dve_link(nc.vector.tensor_tensor(stat[:, 2, n - 1:n], stat[:, 2, n - 1:n], stat[:, 3, n - 1:n], ALU.add))
                    dve_link(nc.vector.reciprocal(stat[:, 2, n - 1:n], stat[:, 2, n - 1:n]))
                if n >= 2:
                    hd, t, loc = steps[n - 2]
                    m = base + n - 2
                    dve.wait_ge(pv_done, m + 1)
                    o = SPEC[name]["o"] + hd * 64
                    nc.vector.tensor_scalar(tok[:, t, o:o + 64], ps[:, 6 + m % 2, 0:64], stat[:, 2, n - 2:n - 1], None,
                                            ALU.mult).then_inc(o_ready, 1)

        for st in info:
            if st["kind"] != "mix":
                continue
            k = st["k"]
            nqs = [x["nq"] for x in info if x["kind"] == "mix"]
            counts = lambda q: [("scan", len(scan_prep(0))), ("a", len(qk_prep("a", q))), ("b", len(qk_prep("b", q))),
                                ("lat", len(latent_prep())), ("up", len(up_prep(q))), ("c", len(qk_prep("c", q)))]
            n = sum(sum(c for _, c in counts(q)) for q in nqs[:k])
            for nm, c in counts(st["nq"]):
                st["prep_" + nm] = n
                n += c
                st["prep_" + nm + "_end"] = n
            n = sum(3 * 4 * q for q in nqs[:k])
            for nm in "abc":
                st["att_" + nm] = n
                n += 4 * st["nq"]
            st["cb"] = sum(nqs[:k])
            st["y"] = sum(nqs[:k])
            st["oT"] = sum(8 * (2 if q == NT else 1) for q in nqs[:k])
        PREPS_PER_LAYER = [next((x["prep_scan"] for x in info if x["kind"] == "mix" and x["k"] == 1), 0)]
        norm_stats, norm_rstd = sem("norm_stats"), sem("norm_rstd")
        a_roped, b_roped, c_roped = sem("a_roped"), sem("b_roped"), sem("c_roped")
        fence_n = {e: 0 for e in fence}

        def next_fence(eng, me):
            fence_n[me] += 1
            fence_all(eng, me, fence_n[me])

        def mix_pe(pe, i, st):
            mix_proj_pe(pe, i, st)
            next_fence(pe, "pe")
            scan_pe(pe, i, st)
            next_fence(pe, "pe")
            for nm in "ab":
                prep_pe(pe, qk_prep(nm, st["nq"]), st["prep_" + nm])
                att_pe(pe, st, nm)
                next_fence(pe, "pe")
            prep_pe(pe, latent_prep(), st["prep_lat"])
            wait_prep(pe, st["prep_lat_end"])
            pe.wait_ge(wc_loaded, 32 * (st["k"] + 1))
            prep_pe(pe, up_prep(st["nq"]), st["prep_up"])
            pe.wait_ge(c_roped, st["k"] + 1)
            prep_pe(pe, qk_prep("c", st["nq"]), st["prep_c"])
            att_pe(pe, st, "c")
            next_fence(pe, "pe")
            mix_out_pe(pe, i, st)
            next_fence(pe, "pe")

        def oT_jobs(st):
            for f in range(8):
                for j in range(len(st["osegs"])):
                    yield f, j

        def o_col(f):
            return (A0, B0, C0, Z0)[f // 2] + (f % 2) * P

        def mix_out_pe(pe, i, st):
            for n, (f, j) in enumerate(oT_jobs(st)):
                if n >= 4:
                    pe.wait_ge(oT_lo, st["oT"] + n - 3)
                t0, t1 = ((0, NX), (NX, NT))[j]
                for t in range(t0, t1):
                    last = nc.tensor.transpose(ps[:, n % 4, (t - t0) * P:(t - t0 + 1) * P], tok[:, t, o_col(f):o_col(f) + P], ident)
                last.then_inc(oT_done, 1)
            ns = len(st["osegs"])
            for d in range(KD):
                u = NU + d // 2
                if d % 2 == 0:
                    pe.wait_ge(wi_lo_ready[u % 2], st["units"] + u // 2 + 1)
                for j, (a, width) in enumerate(st["osegs"]):
                    n = d * ns + j
                    if n >= 4:
                        pe.wait_ge(out_added, st["out"] + n - 3)
                    for f in range(8):
                        if n == 0:
                            pe.wait_ge(oT_lo, st["oT"] + 8 * ns)
                        for q, (w, x) in enumerate(((wi_hi, n_hi), (wi_hi, n_lo), (wi_lo, n_hi))):
                            last = nc.tensor.matmul(ps[:, 4 + n % 4, 0:width], w[u % 2][:, f, (d % 2) * P:(d % 2 + 1) * P],
                                                    x[:, f, a:a + width], start=(f == 0 and q == 0), stop=(f == 7 and q == 2))
                    last.then_inc(out_done, 1)

        def mix_act(act, i, st):
            l, k = st["l"], st["k"]
            mix_proj_act(act, i, st)
            act_link(nc.scalar.activation(tok[:, :, Z0:Z0 + 256], tok[:, :, Z0:Z0 + 256], ACT.Silu))
            next_fence(act, "act")
            scan_act(act, i, st)
            act.wait_ge(norm_stats, 3 * k + 1)
            act_link(nc.scalar.activation(small[:, 0:36], small[:, 0:36], ACT.Ln, bias=eps[:, 0:1], scale=1.0 / HD))
            nc.scalar.activation(small[:, 0:36], small[:, 0:36], ACT.Exp, scale=-0.5).then_inc(norm_rstd, 1)
            act.wait_ge(norm_stats, 3 * k + 3)
            act_link(nc.scalar.activation(small[:, 40:46], small[:, 40:46], ACT.Ln, bias=eps[:, 0:1], scale=1.0 / 256))
            act_link(nc.scalar.activation(small[:, 46:52], small[:, 46:52], ACT.Ln, bias=eps[:, 0:1], scale=1.0 / 128))
            nc.scalar.activation(small[:, 40:52], small[:, 40:52], ACT.Exp, scale=-0.5).then_inc(norm_rstd, 1)
            next_fence(act, "act")
            for nm in "ab":
                prep_copies(act, 1, qk_prep(nm, st["nq"]), st["prep_" + nm])
                att_act(act, st, nm)
                next_fence(act, "act")
            prep_copies(act, 1, latent_prep(), st["prep_lat"])
            prep_copies(act, 1, up_prep(st["nq"]), st["prep_up"])
            prep_copies(act, 1, qk_prep("c", st["nq"]), st["prep_c"])
            att_act(act, st, "c")
            next_fence(act, "act")
            for n, (f, j) in enumerate(oT_jobs(st)):
                a, w = SEGS[j]
                act.wait_ge(oT_done, st["oT"] + n + 1)
                nc.scalar.copy(n_hi[:, f, a:a + w], ps[:, n % 4, 0:w]).then_inc(oT_hi, 1)
            for u in (NU + 2, NU + 3):
                act_split(act, u % 2, st["units"] + u // 2 + 1)
            next_fence(act, "act")

        def mix_dve(dve, i, st):
            l, k = st["l"], st["k"]
            dve_link(nc.vector.memset(xbc[:, :, 0:2], 0.0))
            dve_link(nc.vector.memset(xbc[:, :, 2 + SEQ:4 + SEQ], 0.0))
            nc.vector.memset(xbc[:, :, XW - 2:XW], 0.0).then_inc(dve_act, 1)
            mix_proj_dve(dve, i, st)
            next_fence(dve, "dve")
            scan_dve(dve, i, st)
            v = tok[:, :, B0:B0 + 384].rearrange("p t (h e) -> p t h e", e=64)
            tmp = m_sq[:, :, :].rearrange("p t (h e) -> p t h e", e=64)
            dve.wait_ge(a_roped, k + 1)
            dve_link(nc.vector.tensor_tensor(tmp, v, v, ALU.mult))
            nc.vector.tensor_reduce(small[:, 0:36].rearrange("p (t h) -> p t h", h=6), tmp, AX_X, ALU.add).then_inc(norm_stats, 1)
            dve.wait_ge(norm_stats, 3 * k + 1)
            cq = tok[:, :, C0:C0 + 384]
            dve_link(nc.vector.tensor_tensor(m_sq[:, :, :], cq, cq, ALU.mult))
            nc.vector.tensor_reduce(small[:, 40:46], m_sq[:, :, 0:256], AX_X, ALU.add).then_inc(norm_stats, 1)
            nc.vector.tensor_reduce(small[:, 46:52], m_sq[:, :, 256:384], AX_X, ALU.add).then_inc(norm_stats, 1)
            dve.wait_ge(norm_rstd, 2 * k + 1)
            dve_link(nc.vector.tensor_tensor(v, v, bc(small[:, 0:36].rearrange("p (t h) -> p t h", h=6).unsqueeze(3), [P, NT, 6, 64]), ALU.mult))
            dve_link(nc.vector.tensor_tensor(v[:, :, 0:4], v[:, :, 0:4], bc(R(l, "b_q_norm").unsqueeze(1).unsqueeze(1), [P, NT, 4, 64]), ALU.mult))
            dve_link(nc.vector.tensor_tensor(v[:, :, 4:6], v[:, :, 4:6], bc(R(l, "b_k_norm").unsqueeze(1).unsqueeze(1), [P, NT, 2, 64]), ALU.mult))
            dve_link(rope_heads(dve_link, nc.vector, B0))
            dve.wait_ge(norm_rstd, 2 * k + 2)
            for c, w, r, nm in ((C0, 256, 40, "c_q_norm"), (C0 + 256, 128, 46, "c_kv_norm")):
                x = tok[:, :, c:c + w]
                dve_link(nc.vector.tensor_tensor(x, x, bc(small[:, r:r + 6].unsqueeze(2), [P, NT, w]), ALU.mult))
                dve_link(nc.vector.tensor_tensor(x, x, bc(R(l, nm).unsqueeze(1), [P, NT, w]), ALU.mult))
            kr = tok[:, 0:NX, C0 + 384:C0 + 416].rearrange("p t (f x e) -> p t f x e", f=2, x=2)
            ct = C("cosc").rearrange("p (t f e) -> p t f e", t=NX, f=2)
            stb = C("sinc").rearrange("p (t f e) -> p t f e", t=NX, f=2)
            t1 = m_tmp[:, 0:NX, 0:16].rearrange("p t (f e) -> p t f e", f=2)
            t2 = m_tmp[:, 0:NX, 16:32].rearrange("p t (f e) -> p t f e", f=2)
            dve_link(rope(dve_link, nc.vector, kr[:, :, :, 0], kr[:, :, :, 1], ct, stb, t1, t2))
            next_fence(dve, "dve")
            for nm in "ab":
                prep_copies(dve, 0, qk_prep(nm, st["nq"]), st["prep_" + nm])
                att_dve(dve, st, nm)
                next_fence(dve, "dve")
            prep_copies(dve, 0, latent_prep(), st["prep_lat"])
            prep_copies(dve, 0, up_prep(st["nq"]), st["prep_up"])
            wait_prep(dve, st["prep_up_end"])
            for f in range(2):
                q = qc[:, 0:NX, :, 64 + 16 * f:80 + 16 * f]
                cf = bc(ct[:, :, f].unsqueeze(2), [P, NX, 4, 8])
                sf = bc(stb[:, :, f].unsqueeze(2), [P, NX, 4, 8])
                t1 = m_tmp[:, 0:NX, 0:32].rearrange("p t (h e) -> p t h e", h=4)
                t2 = m_tmp[:, 0:NX, 32:64].rearrange("p t (h e) -> p t h e", h=4)
                dve_link(rope(dve_link, nc.vector, q[:, :, :, 0:8], q[:, :, :, 8:16], cf, sf, t1, t2))
            nc.vector.tensor_copy(kc[:, :, :, 64:96], bc(tok[:, :, C0 + 384:C0 + 416].unsqueeze(2), [P, NT, 4, 32])).then_inc(c_roped, 1)
            prep_copies(dve, 0, qk_prep("c", st["nq"]), st["prep_c"])
            att_dve(dve, st, "c")
            next_fence(dve, "dve")
            for n, (f, j) in enumerate(oT_jobs(st)):
                a, w = SEGS[j]
                dve.wait_ge(oT_hi, st["oT"] + n + 1)
                nc.vector.tensor_tensor(n_lo[:, f, a:a + w], ps[:, n % 4, 0:w], n_hi[:, f, a:a + w].bitcast(F32),
                                        ALU.subtract).then_inc(oT_lo, 1)
            ns = len(st["osegs"])
            for d in range(KD):
                if d == 2 or d == 4:
                    u = NU + 2 + (d // 2 - 1)
                    dve_split(dve, u % 2, st["units"] + u // 2 + 1)
                for j, (a, w) in enumerate(st["osegs"]):
                    n = d * ns + j
                    dve.wait_ge(out_done, st["out"] + n + 1)
                    g = mods[:, (l * NMOD + 5) * KD + d, j:j + 1]
                    nc.vector.scalar_tensor_tensor(out=h[:, d, a:a + w], in0=ps[:, 4 + n % 4, 0:w], scalar=g,
                                                   in1=h[:, d, a:a + w], op0=ALU.mult, op1=ALU.add).then_inc(out_added, 1)
            next_fence(dve, "dve")

        def mix_pool(pool, i, st):
            next_fence(pool, "pool")
            rope_heads(pool_link, nc.gpsimd, A0).then_inc(a_roped, 1)
            for _ in range(5):
                next_fence(pool, "pool")

        block = ctx.enter_context(nc.Block())
        xin = place("xin", [P, NT, DM], offset=n_at)
        vrows = place("vrows", [P, 3, P], offset=n_at + NT * DM * 4)
        fin = place("fin", [P, 2, DM], offset=m_at)

        @block.sync
        def _(sp):
            sp.dma_start(cst[:, :], I["cst"]).then_inc(cst_loaded, 16)
            ab = I["ada_b"].rearrange("l (r p) -> (l r) p", p=P)
            sp.dma_start(vrows[:, 0, :], ab[0:P]).then_inc(in_loaded, 16)
            sp.dma_start(vrows[0:16, 1, :], ab[P:144]).then_inc(in_loaded, 16)
            for r, nm in ((16, "ffn1_norm"), (32, "mix_norm"), (48, "ffn2_norm")):
                sp.dma_start(vrows[r:r + 16, 1, :], I[nm].rearrange("l (r p) -> (l r) p", p=P)).then_inc(in_loaded, 16)
            for r, nm in ((64, "final_norm"), (72, "c"), (80, "c_ctx")):
                sp.dma_start(vrows[r:r + 8, 1, :], I[nm].rearrange("(r p) -> r p", p=P)).then_inc(in_loaded, 16)
            sp.dma_start(vrows[0:60, 2, :], I["d_conv_w"].rearrange("l k (r p) -> (l k r) p", p=P)).then_inc(in_loaded, 16)
            sp.dma_start(vrows[60:72, 2, :], I["d_conv_b"].rearrange("l (r p) -> (l r) p", p=P)).then_inc(in_loaded, 16)
            sp.dma_start(xin[:, 0:NX, :], I["x"].rearrange("(t p) n -> p t n", p=P)).then_inc(in_loaded, 16)
            sp.dma_start(xin[:, NX:NT, :], I["ctx"].rearrange("(t p) n -> p t n", p=P)).then_inc(in_loaded, 16)
            for l in range(DEPTH):
                for nm, (a, w) in ROWS.items():
                    sp.dma_start(rows[:, l, a:a + w], I[nm][l:l + 1, :].broadcast_to([P, w])).then_inc(in_loaded, 16)
            for i, st in enumerate(info):
                (ffn_sync if st["kind"] == "ffn" else mix_sync)(sp, i, st)
            if DEBUG:
                wait_h(sp, len(info), KD - 1)
                sp.dma_start(DEBUG["h"], h[:, :, :]).then_inc(stored[0], 16)
                sp.dma_start(DEBUG["mods"], mods[:, :, :]).then_inc(stored[0], 16)
                sp.wait_ge(stored[0], 32)
                return
            for t in range(NX):
                sp.wait_ge(fin_copied, 2 * t + 2)
                sp.dma_start(out[t * P:(t + 1) * P, :], fin[:, t % 2, :]).then_inc(stored[t % 2], 16)
            for s in stored:
                sp.wait_ge(s, 16 * NX // 2)

        NIN = 16 * (12 + DEPTH * len(ROWS))

        @block.gpsimd
        def _(pool):
            ada_pool(pool, *ADA_AT[0])
            for i, st in enumerate(info):
                if st["kind"] == "mix":
                    mix_pool(pool, i, st)
                elif st["ada"]:
                    if i:
                        for e in ("pe", "act", "dve"):
                            pool.wait_ge(fence[e], fence_n["pool"])
                    else:
                        pool.wait_ge(mod_turned, 1)
                    ada_pool(pool, *st["ada"])

        @block.scalar
        def _(act):
            act.wait_ge(vec_copied, 3)
            for j, c in enumerate((V_C, V_CC)):
                last = nc.scalar.activation(silu_c[:, :, j], vec[:, c:c + KD], ACT.Silu)
            last.then_inc(silu_c_ready, 1)
            act.wait_ge(silu_c_ready, 1)
            nc.scalar.copy(silu_r[:, :, 0:2], silu_c[:, :, :]).then_inc(silu_hi_ready, 1)
            for d in range(KD):
                act.wait_ge(h0_done, 2 * d + 1)
                nc.scalar.copy(h[:, d, 0:SEQ], ps[:, (2 * d) % 4, :]).then_inc(h0_x, 1)
            b0, nb = ADA_AT[0]
            for b in range(b0, b0 + nb):
                ada_act(act, b)
                if b > b0:
                    ada_rows_act(act, b - 1, first=b == 1)
            ada_rows_act(act, b0 + nb - 1)
            for l in range(DEPTH):
                act_link(nc.scalar.activation(R(l, "d_a_log"), R(l, "d_a_log"), ACT.Exp))
            for i, st in enumerate(info):
                for s in range(2):
                    act_split(act, s, st["units"] + 1, 256 if st["kind"] == "ffn" else unit_w(s))
                norm_act_sums(act, i, st)
                norm_act_rstd(act, st)
                norm_act_mod(act, i, st)
                (ffn_act if st["kind"] == "ffn" else mix_act)(act, i, st)
            i = len(info)
            if DEBUG:
                return
            norm_act_sums(act, i, final_norm)
            norm_act_rstd(act, final_norm)

        @block.vector
        def _(dve):
            nc.vector.memset(eps[:, :], EPS).then_inc(h_added, 1)
            for n in range(3):
                w = (P, 88, 72)[n]
                dve.wait_ge(vec_done, n + 1)
                nc.vector.tensor_copy(vec[:, (0, P, 216)[n]:(0, P, 216)[n] + w], ps[:, 4 + n, 0:w]).then_inc(vec_copied, 1)
            for d in range(KD):
                dve.wait_ge(h0_done, 2 * d + 2)
                nc.vector.tensor_copy(h[:, d, SEQ:TOK], ps[:, (2 * d + 1) % 4, 0:CTX]).then_inc(h0_c, 1)
            dve.wait_ge(silu_hi_ready, 1)
            nc.vector.tensor_tensor(silu_r[:, :, 2:4], silu_c[:, :, :], silu_r[:, :, 0:2].bitcast(F32), ALU.subtract).then_inc(silu_lo_ready, 1)
            for b in range(ADA_AT[0][0], ADA_AT[0][0] + ADA_AT[0][1]):
                ada_dve(dve, b)
            mods_dve(dve, ADA_AT[0][0])
            for i, st in enumerate(info):
                for s in range(2):
                    dve_split(dve, s, st["units"] + 1, 256 if st["kind"] == "ffn" else unit_w(s))
                norm_dve_sums(dve, i, st)
                norm_dve_mod(dve, i, st)
                (ffn_dve if st["kind"] == "ffn" else mix_dve)(dve, i, st)
            i = len(info)
            if DEBUG:
                return
            norm_dve_sums(dve, i, final_norm)
            dve.wait_ge(rstd_ready, final_norm["norm"] + 1)
            for d in range(KD):
                dve_link(nc.vector.scalar_tensor_tensor(out=h[:, d, 0:SEQ], in0=h[:, d, 0:SEQ], scalar=vec[:, V_FIN + d:V_FIN + d + 1],
                                                        in1=rstd[:, 0:SEQ], op0=ALU.mult, op1=ALU.mult))
            nc.vector.tensor_copy(eps[:, :], h[:, 0, 0:1]).then_inc(h_added, 1)
            for n in range(2 * NX):
                dve.wait_ge(fin_done, n + 1)
                if n // 2 >= 2:
                    dve.wait_ge(stored[(n // 2) % 2], 16 * (n // 4))
                nc.vector.tensor_copy(fin[:, (n // 2) % 2, (n % 2) * 512:(n % 2 + 1) * 512], ps[:, n % 4, :]).then_inc(fin_copied, 1)

        @block.tensor
        def _(pe):
            pe.wait_ge(cst_loaded, 16)
            pe.wait_ge(in_loaded, NIN)
            for n in range(3):
                w = (P, 88, 72)[n]
                nc.tensor.transpose(ps[:, 4 + n, 0:w], vrows[0:w, n, :], ident[0:w, 0:w]).then_inc(vec_done, 1)
            for d in range(KD):
                for j, (t0, t1) in enumerate(((0, NX), (NX, NT))):
                    n = 2 * d + j
                    if n >= 4:
                        pe.wait_ge(h0_x if j == 0 else h0_c, d - 1)
                    for t in range(t0, t1):
                        last = nc.tensor.transpose(ps[:, n % 4, (t - t0) * P:(t - t0 + 1) * P], xin[:, t, d * P:(d + 1) * P], ident)
                    last.then_inc(h0_done, 1)
            pe.wait_ge(silu_lo_ready, 1)
            for b in range(ADA_AT[0][0], ADA_AT[0][0] + ADA_AT[0][1]):
                if b:
                    pe.wait_ge(rows_copied, b)
                ada_pe(pe, b)
            pe.wait_ge(h0_x, KD)
            mods_pe(pe, ADA_AT[0][0])
            for i, st in enumerate(info):
                norm_pe(pe, i, st)
                (ffn_pe if st["kind"] == "ffn" else mix_pe)(pe, i, st)
            if DEBUG:
                return
            norm_pe(pe, len(info), final_norm)
            pe.wait_ge(h_added, jobs + 1)
            for n in range(2 * NX):
                t = n // 2
                if n >= 4:
                    pe.wait_ge(fin_copied, n - 3)
                for q in range(4):
                    d = (n % 2) * 4 + q
                    last = nc.tensor.transpose(ps[:, n % 4, q * P:(q + 1) * P], h[:, d, t * P:(t + 1) * P], ident)
                last.then_inc(fin_done, 1)


def constants():
    import numpy as np
    k, m = np.arange(P)[:, None], np.arange(P)[None, :]
    t = np.zeros((P, CSTW), np.float32)

    def put(name, a):
        c, w = CST[name]
        t[:, c:c + w] = a.reshape(P, w)

    put("ident", np.eye(P))
    put("ones", np.ones((P, P)))
    put("le", (k <= m) * 1.0)
    put("gt", (k > m) * 1.0)
    put("ge", (k >= m) * 1.0)
    put("lt", (k < m) * 1.0)
    put("prev", np.where(m >= k, 0.0, NEG))
    put("next", np.where(m <= k, 0.0, NEG))
    pos = np.arange(SEQ)
    for dim, cn, sn, rep in ((HD, "cosh", "sinh", 1), (C_ROPE, "cosc", "sinc", 1)):
        ax = dim // 2
        inv = np.float32(THETA) ** (-np.arange(0, ax, 2, dtype=np.float32) / np.float32(ax))
        ang = np.stack([(pos // GRID_W)[:, None].astype(np.float32) * inv, (pos % GRID_W)[:, None].astype(np.float32) * inv], 1)
        ang = np.tile(ang.astype(np.float32), (1, rep, 1)).reshape(NX, P, rep * 2 * (ax // 2)).transpose(1, 0, 2)
        put(cn, np.cos(ang.astype(np.float64)))
        put(sn, np.sin(ang.astype(np.float64)))
    return t


NAMES = ["x", "c", "ctx", "c_ctx", "ada_w", "ada_b", "ffn1_norm", "ffn1_wi", "ffn1_wo", "mix_norm", "w_in", "w_out",
         "a_sink", "b_q_norm", "b_k_norm", "c_q_norm", "c_w_uq", "c_kv_norm", "c_w_ukv", "d_conv_w", "d_conv_b",
         "d_a_log", "d_dt_bias", "d_skip", "d_out_norm", "ffn2_norm", "ffn2_wi", "ffn2_wo", "final_norm"]


def kernel(**inputs):
    import numpy as np
    import concourse.bacc as bacc
    from concourse.bass_utils import run_bass_kernel_spmd as run

    nc = bacc.Bacc("TRN2", target_bir_lowering=False, num_devices=1)
    arrays, aps = {}, {}
    for name in NAMES:
        a = np.ascontiguousarray(inputs[name])
        if name in ("x", "ctx"):
            a = a.reshape(a.shape[1:])
        if name == "c":
            a = a.reshape(-1)
        if name in ("d_a_log", "d_dt_bias"):
            a = a.reshape(DEPTH, -1)
        arrays["in_" + name] = a
    arrays["in_cst"] = constants()
    for name, a in arrays.items():
        aps[name[3:]] = nc.dram_tensor(name, a.shape, mybir.dt.from_np(a.dtype), kind="ExternalInput").ap()
    out = nc.dram_tensor("out_0", (SEQ, DM), F32, kind="ExternalOutput").ap()
    if DEBUG is not None:
        for n_, s_ in (("h", (P, KD, TOK)), ("mods", (P, 144, 2)), ("tok", (2, P, NT, TOKW))):
            DEBUG[n_] = nc.dram_tensor("dbg_" + n_, s_, F32, kind="ExternalOutput").ap()
    mod_dram = nc.dram_tensor("mod_dram", (4, DEPTH * NMOD * DM), F32, kind="Internal").ap()
    hybrid_block(nc, aps, out, mod_dram, STOP_AFTER)
    got = run(nc, [arrays], core_ids=[0]).results[0]["out_0"]
    return got.reshape(1, SEQ, DM)
```

```python
from contextlib import ExitStack

import concourse.bass as bass
from concourse import mybir

ALU = mybir.AluOpType
ACT = mybir.ActivationFunctionType
F32 = mybir.dt.float32
F32R = mybir.dt.float32r
AX_X = mybir.AxisListType.X

P = 128
DEPTH = 2
DM = 1024
KD = DM // P
SEQ, CTX = 512, 256
TOK = SEQ + CTX
NX, NT = SEQ // P, TOK // P
FFN = 2816
FT = FFN // P
FG = FT // 2
NMOD = 9
EPS = 1e-6
GRID_W = 64
THETA = 10000.0
HD = 64
C_ROPE = 32
SEGS = [(0, SEQ), (SEQ, CTX)]

A0, B0, C0, Z0 = 0, 512, 1024, 1440
DT0 = Z0 + 256
TOKW = DT0 + 8
XBC_COL = 1696
DT_COL = 2464
XW = TOK + 6
NEG = -float(2 ** 100)

UNITS = [("conv", [(XBC_COL, 256, 0)]), ("conv", [(XBC_COL + 256, 256, 2)]), ("conv", [(XBC_COL + 512, 256, 4)]),
         ("tok", [(1280, 160, 1280), (DT_COL, 8, DT0)]), ("tok", [(1440, 256, Z0)]), ("tok", [(1024, 256, C0)]),
         ("tok", [(512, 256, B0)]), ("tok", [(768, 256, 768)]), ("tok", [(0, 256, A0)]), ("tok", [(256, 256, 256)])]
U_DT, U_Z, U_C, U_B = 3, 4, 5, 7
NU = len(UNITS)
CARRIES = 2 * (NT - 1)
OUTU = 4

CST = {}
_n = 0
for _name, _w in (("ident", P), ("ones", P), ("le", P), ("gt", P), ("ge", P), ("lt", P), ("prev", P), ("next", P),
                  ("cosh", NX * 32), ("sinh", NX * 32), ("cosc", NX * 16), ("sinc", NX * 16)):
    CST[_name] = (_n, _w)
    _n += _w
CSTW = _n

ROWS = {}
_n = 0
for _name, _w in (("b_q_norm", 64), ("b_k_norm", 64), ("c_q_norm", 256), ("c_kv_norm", 128), ("a_sink", 4),
                  ("d_dt_bias", 8), ("d_a_log", 8), ("d_skip", 4), ("d_out_norm", 256)):
    ROWS[_name] = (_n, _w)
    _n += _w
ROWW = _n

V_ADAB, V_FFN1, V_MIX, V_FFN2, V_FIN, V_C, V_CC = 0, 144, 160, 176, 192, 200, 208
V_CONVW, V_CONVB = 216, 276
VECW = 288

ADAW = 256
BATCH = 3 * ADAW
ADA_AT = [(0, 4), (4, 10), (14, 10)]
NBATCH = DEPTH * NMOD * DM // BATCH


def conv_col(t):
    return t * P if t < NX else SEQ + 2 + (t - NX) * P


def hybrid_block(nc, I, out, mod_dram):
    stages = [("ffn", 0, 0), ("mix", 0, 0), ("ffn", 0, 1), ("ffn", 1, 0), ("mix", 1, 0), ("ffn", 1, 1)]
    with ExitStack() as ctx:
        at = [16512]

        def place(name, shape, dt=F32, offset=None):
            size = 4
            for s in shape[1:]:
                size *= s
            size = (size + 31) // 32 * 32
            if offset is None:
                offset = at[0]
                at[0] += size
            assert offset + size <= nc.sbuf_usable_end, (name, offset + size)
            return nc.alloc_sbuf_tensor_at(name, shape, dt, offset=offset)

        def sem(name):
            return ctx.enter_context(nc.semaphore(name))

        h = place("h", [P, KD, TOK])
        mods = place("mods", [P, DEPTH * NMOD * KD, 2])
        vec = place("vec", [P, VECW])
        gain = place("gain", [P, DEPTH, 3, KD, 2])
        half_gate = place("half_gate", [P, DEPTH, 2, KD, 2])
        cst = place("cst", [P, CSTW])
        rows = place("rows", [P, DEPTH, ROWW])
        silu_c = place("silu_c", [P, KD, 2])
        silu_r = place("silu_r", [P, KD, 4], F32R)
        eps = place("eps", [P, 1])
        warm = place("warm", [P, 1])
        sq_at = at[0]
        sq = place("sq", [P, 2, TOK])
        sumsq_at = at[0]
        sumsq = place("sumsq", [P, TOK])
        rstd_at = at[0]
        rstd = place("rstd", [P, TOK])
        wi_raw, wi_lo, wi_hi = [], [], []
        for s in range(2):
            a = at[0]
            wi_raw.append(place(f"wi_raw{s}", [P, KD, 256]))
            wi_lo.append(place(f"wi_lo{s}", [P, KD, 256], F32R, offset=a))
            wi_hi.append(place(f"wi_hi{s}", [P, KD, 256], F32R))
        wo_at = at[0]
        wo_raw = place("wo_raw", [P, 2, DM])
        wo_lo = place("wo_lo", [P, 2, DM], F32R, offset=wo_at)
        wo_hi = place("wo_hi", [P, 2, DM], F32R)
        n_at = at[0]
        n_hi = place("n_hi", [P, KD, TOK], F32R)
        n_lo = place("n_lo", [P, KD, TOK], F32R)
        m_at = at[0]
        n_tmp = sq

        g_hi = place("g_hi", [P, 2, TOK], F32R)
        g_lo = place("g_lo", [P, 2, TOK], F32R)
        silu_a = place("silu_a", [P, 2, TOK], offset=sq_at)
        prod = silu_a
        ada_raw, ada_lo, ada_hi = [], [], []
        for s in range(3):
            a = at[0]
            ada_raw.append(place(f"ada_raw{s}", [P, KD, ADAW]))
            ada_lo.append(place(f"ada_lo{s}", [P, KD, ADAW], F32R, offset=a))
            ada_hi.append(place(f"ada_hi{s}", [P, KD, ADAW], F32R))
        ada_rows = place("ada_rows", [4, 3 * ADAW], offset=rstd_at)
        mod_rows = place("mod_rows", [P, 4, P], offset=m_at + 4 * 2 * TOK * 4)

        at[0] = m_at
        tok = place("tok", [P, NT, TOKW])
        xbc = place("xbc", [P, 6, XW])
        small = place("small", [P, 384], offset=sumsq_at)
        free_at = wo_at
        at[0] = n_at
        xsb = place("xsb", [P, NT, 512])
        xdt = place("xdt", [P, 2, NT, 256])
        xdec_at = at[0]
        xdec = place("xdec", [P, 2, NT, 256])
        cb = place("cb", [P, NT, 2, 2, P], offset=xdec_at)
        h_in = place("h_in", [P, 2, NT, 256])
        assert at[0] <= m_at
        at[0] = free_at
        seg_rhs = place("seg_rhs", [P, 2, 512])
        decay = place("decay", [P, 2, 512])
        y_tmp = place("y_tmp", [P, 512])
        y_sq = place("y_sq", [P, 256], offset=free_at + 2048 * 5 + 3072 + 2048)
        conv_acc = place("conv_acc", [P, 2, XW - 4], offset=free_at)
        at[0] = n_at
        q_hi = place("q_hi", [P, 4, TOK], F32R)
        q_lo = place("q_lo", [P, 4, TOK], F32R)
        k_hl = place("k_hl", [P, 2, TOK], F32R)
        qkT = place("qkT", [96, 8, TOK], offset=n_at)
        vc = place("vc", [P, NT, 256], offset=n_at + 8 * TOK * 4)
        probs = place("probs", [P, 3, TOK])
        probsT = place("probsT", [P, 2, TOK])
        assert at[0] <= m_at
        masks = place("masks", [P, 3, P], F32R, offset=m_at + NT * TOKW * 4 + 6 * XW * 4 // 32 * 32 + 32)
        ident_r = place("ident_r", [P, P], F32R, offset=m_at + NT * TOKW * 4 + 6 * XW * 4 // 32 * 32 + 32 + 3 * P * 4)
        xbc_at = n_at + 2 * KD * TOK * 4 + NT * TOKW * 4
        qc = place("qc", [P, NT, 4, 96], offset=xbc_at)
        kc = place("kc", [P, NT, 4, 96], offset=xbc_at + NT * 384 * 4)
        cT = place("cT", [P, 3, TOK], offset=n_at + 10 * TOK * 4)
        w_uq = place("w_uq", [P, 2, 384], offset=free_at + 2048 * 5)
        w_ukv = place("w_ukv", [P, 512], offset=free_at + 2048 * 5 + 3072)
        m_tmp = place("m_tmp", [P, NX, 192], offset=sq_at)
        m_sq = place("m_sq", [P, NT, 384], offset=free_at)
        stat = place("stat", [P, 4, 160], offset=rstd_at)
        ps = ctx.enter_context(nc.psum_tensor("ps", [P, 8, 512], F32))

        def C(name):
            a, w = CST[name]
            return cst[:, a:a + w]

        def R(l, name):
            a, w = ROWS[name]
            return rows[:, l, a:a + w]

        ident, ones = C("ident"), C("ones")

        x_loaded, rows_loaded = sem("x_loaded"), sem("rows_loaded")
        in_loaded, cst_loaded = sem("in_loaded"), sem("cst_loaded")
        vec_done, vec_copied = sem("vec_done"), sem("vec_copied")
        h0_done, h0_x, h0_c = sem("h0_done"), sem("h0_x"), sem("h0_c")
        silu_c_ready = sem("silu_c_ready")
        ada_loaded = [sem(f"ada_loaded{s}") for s in range(3)]
        ada_hi_ready = [sem(f"ada_hi_ready{s}") for s in range(3)]
        ada_lo_ready = [sem(f"ada_lo_ready{s}") for s in range(3)]
        ada_used = [sem(f"ada_used{s}") for s in range(3)]
        silu_hi_ready, silu_lo_ready = sem("silu_hi_ready"), sem("silu_lo_ready")
        rows_copied, rows_stored, mod_rows_loaded = sem("rows_copied"), sem("rows_stored"), sem("mod_rows_loaded")
        mod_turned = sem("mod_turned")
        wi_loaded = [sem(f"wi_loaded{s}") for s in range(2)]
        wi_hi_ready = [sem(f"wi_hi_ready{s}") for s in range(2)]
        wi_lo_ready = [sem(f"wi_lo_ready{s}") for s in range(2)]
        up_done = [sem(f"up_done{s}") for s in range(2)]
        wo_loaded, wo_hi_ready, wo_lo_ready, down_end = sem("wo_loaded"), sem("wo_hi_ready"), sem("wo_lo_ready"), sem("down_end")
        silu_ready = [sem(f"silu_ready{s}") for s in range(2)]
        prod_ready = [sem(f"prod_ready{s}") for s in range(2)]
        g_hi_ready = [sem(f"g_hi_ready{s}") for s in range(2)]
        g_lo_ready = [sem(f"g_lo_ready{s}") for s in range(2)]
        down_done, h_added = sem("down_done"), sem("h_added")
        sq_ready, sq_summed, ssum_done, rstd_ready = sem("sq_ready"), sem("sq_summed"), sem("ssum_done"), sem("rstd_ready")
        n_tmp_ready, n_hi_ready, n_lo_ready = sem("n_tmp_ready"), sem("n_hi_ready"), sem("n_lo_ready")
        proj_done, proj_copied = sem("proj_done"), sem("proj_copied")
        conv_ready, xbc_ready = sem("conv_ready"), sem("xbc_ready")
        fence = {e: sem(f"fence_{e}") for e in ("pe", "act", "dve", "pool")}
        prep_done = sem("prep_done")
        prep_copied = [sem("prep_copied_dve"), sem("prep_copied_act")]
        qk_turned, qk_hi_ready, qk_lo_ready = sem("qk_turned"), sem("qk_hi_ready"), sem("qk_lo_ready")
        probs_scaled, recip_ready = sem("probs_scaled"), sem("recip_ready")
        s_done, bias_ready, exp_done = sem("s_done"), sem("bias_ready"), sem("exp_done")
        t_done, t_copied_x, t_copied_c = sem("t_done"), sem("t_copied_x"), sem("t_copied_c")
        pv_done, o_ready = sem("pv_done"), sem("o_ready")
        oT_done, oT_hi, oT_lo = sem("oT_done"), sem("oT_hi"), sem("oT_lo")
        out_done, out_added = sem("out_done"), sem("out_added")
        dt_sums, dt_exps = sem("dt_sums"), sem("dt_exps")
        a_ready = sem("a_ready")
        st_done, h_in_ready = sem("st_done"), sem("h_in_ready")
        cb_done, cb_ready = sem("cb_done"), sem("cb_ready")
        seg_in, seg_done, seg_exp, m_ready = sem("seg_in"), sem("seg_done"), sem("seg_exp"), sem("m_ready")
        y_done, y_ready, y_gated, x_skipped = sem("y_done"), sem("y_ready"), sem("y_gated"), sem("x_skipped")
        xdt_ready = sem("xdt_ready")
        wc_loaded = sem("wc_loaded")
        act_dve, dve_act = sem("act_dve"), sem("dve_act")
        fin_done, fin_copied, stored = sem("fin_done"), sem("fin_copied"), [sem("stored0"), sem("stored1")]
        dve_chain, act_chain, pool_chain = sem("dve_chain"), sem("act_chain"), sem("pool_chain")

        info = []
        ffns = mixes = 0
        slot_units, jobs, oj, norms, projs = 0, 1, 0, 0, 0
        NPROJ = sum(NT if k == "tok" else 4 for k, _ in UNITS)
        for kind, l, which in stages:
            last = l == DEPTH - 1
            d = dict(kind=kind, l=l, which=which, units=slot_units, norm=norms)
            norms += 1
            if kind == "ffn":
                nseg = 1 if (last and which == 1) else 2
                d.update(ada=ADA_AT[1 + which] if l == 0 else None)
                d.update(k=ffns, segs=SEGS[:nseg], g0=ffns * FG, jobs=jobs, nj=KD * nseg)
                ffns += 1
                jobs += FG * KD * nseg
                slot_units += FG
            else:
                nseg = 1 if last else 2
                d.update(k=mixes, segs=SEGS, osegs=SEGS[:nseg], nq=NX if last else NT, out=oj, proj=projs)
                mixes += 1
                oj += KD * nseg
                projs += NPROJ
                slot_units += (NU + OUTU) // 2
            info.append(d)
        final_norm = dict(norm=norms, segs=SEGS[:1], kind="final")
        norm_adds = KD - 3

        def fence_all(eng, me, n, without=None):
            eng.drain().then_inc(fence[me], 1)
            for e, s in fence.items():
                if e != me and e != without:
                    eng.wait_ge(s, n)

        def wait_slot_used(eng, i, u):
            st = info[i]
            s = u % 2
            if st["kind"] == "mix" and u >= 2:
                if u - 2 < NU:
                    eng.wait_ge(proj_done, st["proj"] + sum(NT if k == "tok" else 4 for k, _ in UNITS[:u - 1]))
                else:
                    eng.wait_ge(out_done, st["out"] + len(st["osegs"]) * 2 * (u - 1 - NU))
            elif i > 0:
                pr = info[i - 1]
                if pr["kind"] == "ffn":
                    eng.wait_ge(up_done[s], pr["g0"] + FG)
                else:
                    eng.wait_ge(out_done, pr["out"] + len(pr["osegs"]) * 2 * (OUTU - 1 + s))

        def act_split(act, s, n, w=256):
            act.wait_ge(wi_loaded[s], 32 * n)
            nc.scalar.copy(wi_hi[s][:, :, 0:w], wi_raw[s][:, :, 0:w]).then_inc(wi_hi_ready[s], 1)

        def dve_split(dve, s, n, w=256):
            dve.wait_ge(wi_hi_ready[s], n)
            nc.vector.tensor_tensor(wi_lo[s][:, :, 0:w], wi_raw[s][:, :, 0:w], wi_hi[s][:, :, 0:w].bitcast(F32),
                                    ALU.subtract).then_inc(wi_lo_ready[s], 1)

        def unit_w(u):
            return sum(w for _, w, _ in UNITS[u][1]) if u < NU else 256

        def wait_h(eng, i, d):
            if i == 0:
                eng.wait_ge(h0_x, d + 1)
                eng.wait_ge(h0_c, d + 1)
                return
            pr = info[i - 1]
            if pr["kind"] == "ffn":
                eng.wait_ge(h_added, pr["jobs"] + (FG - 1) * pr["nj"] + (d + 1) * len(pr["segs"]))
            else:
                eng.wait_ge(out_added, pr["out"] + (d + 1) * len(pr["osegs"]))

        def ncols(segs):
            return segs[-1][0] + segs[-1][1]

        def norm_act_sums(act, i, st, tiles=range(KD)):
            w = ncols(st["segs"])
            b = st["norm"] * norm_adds
            for d in tiles:
                wait_h(act, i, d)
                if d >= 2:
                    act.wait_ge(sq_summed, b + max(1, d - 2))
                elif i > 0:
                    act.wait_ge(n_lo_ready, st["norm"] and n_count(i - 1))
                nc.scalar.activation(sq[:, d % 2, 0:w], h[:, d, 0:w], ACT.Square).then_inc(sq_ready, 1)

        def n_count(i):
            return sum(KD * len(x["segs"]) for x in info[:i + 1])

        def norm_sums(eng, engine, i, st, tiles=range(KD)):
            w = ncols(st["segs"])
            for d in tiles:
                if not 1 <= d < KD - 2:
                    continue
                eng.wait_ge(sq_ready, st["norm"] * KD + d + 1)
                if d == 1 and st["norm"] > 0:
                    eng.wait_ge(ssum_done, st["norm"])
                if d > 1:
                    eng.wait_ge(sq_summed, st["norm"] * norm_adds + d - 1)
                engine.tensor_tensor(sumsq[:, 0:w], sq[:, 0, 0:w] if d == 1 else sumsq[:, 0:w], sq[:, d % 2, 0:w],
                                        ALU.add).then_inc(sq_summed, 1)

        def norm_pe(pe, i, st):
            if i == 0:
                wait_h(pe, 0, KD - 1)
            for y, x in enumerate((sumsq, sq[:, 0], sq[:, 1])):
                if y == 0:
                    pe.wait_ge(sq_summed, (st["norm"] + 1) * norm_adds)
                else:
                    pe.wait_ge(sq_ready, st["norm"] * KD + KD - 2 + y)
                for j, (a, w) in enumerate(st["segs"]):
                    last = nc.tensor.matmul(ps[:, 1 + j, 0:w], ones, x[:, a:a + w], start=y == 0, stop=y == 2, skip_group_check=True)
            last.then_inc(ssum_done, 1)

        def norm_act_rstd(act, st):
            act_link(nc.scalar.activation(warm[:, :], eps[:, :], ACT.Ln))
            act.wait_ge(ssum_done, st["norm"] + 1)
            act.wait_ge(rows_stored, 16 * sum(nb for _, nb in ADA_AT[:1 + min(2, (st["norm"] + 1) // 2)]))
            if st["norm"] > 0:
                act.wait_ge(n_tmp_ready, n_count(st["norm"] - 1))
            for j, (a, w) in enumerate(st["segs"]):
                act_link(nc.scalar.activation(rstd[:, a:a + w], ps[:, 1 + j, 0:w], ACT.Ln, bias=eps[:, 0:1], scale=1.0 / DM))
            w = ncols(st["segs"])
            nc.scalar.activation(rstd[:, 0:w], rstd[:, 0:w], ACT.Exp, scale=-0.5).then_inc(rstd_ready, 1)

        def shift_of(st, d, j):
            m = {"ffn": 6 * st["which"], "mix": 3}[st["kind"]]
            c = (st["l"] * NMOD + m) * KD + d
            return mods[:, c, j:j + 1]

        def gain_of(st, d, j):
            m = {"ffn": 2 * st["which"], "mix": 1}[st["kind"]]
            return gain[:, st["l"], m, d, j:j + 1]

        def norm_act_mod(act, i, st):
            b = n_count(i - 1) if i else 0
            ns = len(st["segs"])
            for d in range(KD):
                for j, (a, w) in enumerate(st["segs"]):
                    act.wait_ge(n_tmp_ready, b + d * ns + j + 1)
                    nc.scalar.activation(n_hi[:, d, a:a + w], n_tmp[:, d % 2, a:a + w], ACT.Identity,
                                         bias=shift_of(st, d, j)).then_inc(n_hi_ready, 1)

        def norm_dve_mod(dve, i, st):
            b = n_count(i - 1) if i else 0
            ns = len(st["segs"])
            dve.wait_ge(rstd_ready, st["norm"] + 1)
            for d in range(KD + 1):
                if d < KD:
                    for j, (a, w) in enumerate(st["segs"]):
                        if d >= 2:
                            dve.wait_ge(n_lo_ready, b + (d - 2) * ns + j + 1)
                        nc.vector.scalar_tensor_tensor(out=n_tmp[:, d % 2, a:a + w], in0=h[:, d, a:a + w],
                                                       scalar=gain_of(st, d, j), in1=rstd[:, a:a + w],
                                                       op0=ALU.mult, op1=ALU.mult).then_inc(n_tmp_ready, 1)
                if d >= 1:
                    for j, (a, w) in enumerate(st["segs"]):
                        dve.wait_ge(n_hi_ready, b + (d - 1) * ns + j + 1)
                        nc.vector.scalar_tensor_tensor(out=n_lo[:, d - 1, a:a + w], in0=n_tmp[:, (d - 1) % 2, a:a + w],
                                                       scalar=shift_of(st, d - 1, j),
                                                       in1=n_hi[:, d - 1, a:a + w].bitcast(F32),
                                                       op0=ALU.add, op1=ALU.subtract).then_inc(n_lo_ready, 1)

        def ada_load(pool, b, layer, wait=True):
            src = I["ada_w"][layer].rearrange("(k p) n -> p k n", p=P)
            for s in range(3):
                if wait:
                    pool.wait_ge(ada_used[s], b)
                pool.dma_start(ada_raw[s][:, :, :], src[:, :, bass.ds(b * BATCH + (s * ADAW - layer * NMOD * DM), ADAW)]).then_inc(ada_loaded[s], 16)

        def ada_store(pool, b):
            pool.wait_ge(rows_copied, b + 1)
            pool.dma_start(mod_dram[:, bass.ds(b * BATCH, BATCH)], ada_rows[:, :]).then_inc(rows_stored, 16)

        def ada_pool(pool, b0, nb):
            half = NBATCH // DEPTH
            ada_load(pool, b0, b0 // half, wait=b0 > 0)
            cuts = sorted({b0, min(max(half - 1, b0), b0 + nb - 1), b0 + nb - 1})
            for x, y in zip(cuts, cuts[1:]):
                with pool.Fori(x, y) as b:
                    ada_load(pool, b + 1, (x + 1) // half)
                    ada_store(pool, b)
            ada_store(pool, b0 + nb - 1)
            pool.wait_ge(rows_stored, 16 * (b0 + nb))
            n = nb * BATCH // P
            pool.dma_start(mod_rows[0:n, :, :], mod_dram[:, b0 * BATCH:(b0 + nb) * BATCH].rearrange("j (c p) -> c j p", p=P)).then_inc(mod_rows_loaded, 16)

        def ada_act(act, b):
            for s in range(3):
                act.wait_ge(ada_loaded[s], (b + 1) * 16)
                nc.scalar.copy(ada_hi[s][:, :, :], ada_raw[s][:, :, :]).then_inc(ada_hi_ready[s], 1)

        def ada_dve(dve, b):
            for s in range(3):
                dve.wait_ge(ada_hi_ready[s], b + 1)
                nc.vector.tensor_tensor(ada_lo[s][:, :, :], ada_raw[s][:, :, :], ada_hi[s][:, :, :].bitcast(F32),
                                        ALU.subtract).then_inc(ada_lo_ready[s], 1)

        def ada_pe(pe, b, bank=6):
            for s in range(3):
                pe.wait_ge(ada_lo_ready[s], b + 1)
                for k in range(KD):
                    for w in (ada_hi, ada_lo):
                        last = nc.tensor.matmul(ps[0:4, bank + s // 2, (s % 2) * ADAW:(s % 2 + 1) * ADAW], silu_r[:, k, :], w[s][:, k, :],
                                                start=(k == 0 and w is ada_hi), stop=(k == KD - 1 and w is ada_lo))
                last.then_inc(ada_used[s], 1)

        def ada_rows_act(act, b, first=False, bank=6):
            for s in range(3):
                act.wait_ge(ada_used[s], b + 1)
            if not first:
                act.wait_ge(rows_stored, b * 16)
            nc.scalar.copy(ada_rows[:, :], ps[0:4, bank:bank + 2, :].rearrange("p a b -> p (a b)")[:, 0:BATCH]).then_inc(rows_copied, 1)

        def mods_pe(pe, b0):
            grp = [x for x, _ in ADA_AT].index(b0)
            n = ADA_AT[grp][1] * BATCH // P
            pe.wait_ge(mod_rows_loaded, 16 * (grp + 1))
            for j in range(2):
                for r in (j, j + 2):
                    last = nc.tensor.matmul(ps[:, 0, j * P:j * P + n], mod_rows[0:n, r, :], ident[0:n, 0:n], start=(r < 2), stop=(r >= 2))
            last.then_inc(mod_turned, 1)

        def mods_dve(dve, b0):
            grp = [x for x, _ in ADA_AT].index(b0)
            c0, n = b0 * BATCH // P, ADA_AT[grp][1] * BATCH // P
            dve.wait_ge(mod_turned, grp + 1)
            dve_link(nc.vector.tensor_tensor(mods[:, c0:c0 + n, :], ps[:, 0, 0:2 * P].rearrange("p (j c) -> p c j", c=P)[:, 0:n, :],
                                             bc(vec[:, c0:c0 + n].unsqueeze(2), [P, n, 2]), ALU.add))
            for l in range(DEPTH):
                for m, c in ((0, V_FFN1), (1, V_MIX), (2, V_FFN2)):
                    sc = (l * NMOD + 3 * m + 1) * KD
                    if c0 < sc + KD <= c0 + n:
                        dve_link(nc.vector.scalar_tensor_tensor(out=gain[:, l, m], in0=mods[:, sc:sc + KD, :], scalar=1.0,
                                                                in1=bc(vec[:, c + l * KD:c + (l + 1) * KD].unsqueeze(2), [P, KD, 2]),
                                                                op0=ALU.add, op1=ALU.mult))
                for m in range(2):
                    gc = (l * NMOD + 6 * m + 2) * KD
                    if c0 < gc + KD <= c0 + n:
                        dve_link(nc.vector.tensor_scalar(half_gate[:, l, m], mods[:, gc:gc + KD, :], 0.5, None, ALU.mult))

        DOWN_BANKS = (3, 4, 6, 7)

        def wi_src(st, s, g, part):
            w = I["ffn1_wi" if st["which"] == 0 else "ffn2_wi"][st["l"]].rearrange("(k p) n -> p k n", p=P)
            return w[:, :, bass.ds(g * 256 + (s * P + part * FFN), P)]

        def wo_src(st, g):
            w = I["ffn1_wo" if st["which"] == 0 else "ffn2_wo"][st["l"]].rearrange("(k p) n -> p k n", p=P)
            return w[:, bass.ds(g * 2, 2), :]

        def ffn_load_wi(sp, st, s, g):
            for part in range(2):
                sp.dma_start(wi_raw[s][:, :, part * P:(part + 1) * P], wi_src(st, s, g, part)).then_inc(wi_loaded[s], 16)

        def ffn_sync(sp, i, st):
            g0 = st["g0"]
            for s in range(2):
                wait_slot_used(sp, i, s)
                ffn_load_wi(sp, st, s, 0)
            if i > 0 and info[i - 1]["kind"] == "mix":
                for e in ("pe", "act", "dve"):
                    sp.wait_ge(fence[e], 6 * (info[i - 1]["k"] + 1))
            elif g0:
                sp.wait_ge(down_end, g0)
            sp.dma_start(wo_raw[:, :, :], wo_src(st, 0)).then_inc(wo_loaded, 16)
            sp.wait_ge(up_done[0], g0 + 1)
            ffn_load_wi(sp, st, 0, 1)

            def body(g, more):
                sp.wait_ge(up_done[1], g0 + g)
                ffn_load_wi(sp, st, 1, g)
                if more:
                    sp.wait_ge(up_done[0], g0 + g + 1)
                    ffn_load_wi(sp, st, 0, g + 1)
                sp.wait_ge(down_end, g0 + g)
                sp.dma_start(wo_raw[:, :, :], wo_src(st, g)).then_inc(wo_loaded, 16)

            with sp.Fori(1, FG - 1) as g:
                body(g, True)
            body(FG - 1, False)

        def ffn_pe(pe, i, st):
            g0, segs, ns = st["g0"], st["segs"], len(st["segs"])
            if st["kind"] == "ffn" and i > 0 and info[i - 1]["kind"] == "mix":
                wait_h(pe, i, KD - 1)

            def up(s, g, first):
                pe.wait_ge(wi_lo_ready[s], st["units"] + g + 1)
                if first:
                    if g0:
                        pe.wait_ge(prod_ready[s], g0)
                else:
                    pe.wait_ge(prod_ready[s], g0 + g)
                    if s == 1:
                        pe.wait_ge(h_added, g * st["nj"] + (st["jobs"] - 2))
                for part in range(2):
                    for k in range(KD):
                        if first and s == 0 and part == 0:
                            pe.wait_ge(n_lo_ready, n_count(i) - (KD - 1 - k) * ns)
                        cols = slice(part * P, (part + 1) * P)
                        for w, n in ((wi_hi, n_hi), (wi_hi, n_lo), (wi_lo, n_hi)):
                            for j, (a, width) in enumerate(segs):
                                o = ps[:, 3 * s + part, 0:width] if j == 0 else ps[:, 3 * s + 2, part * CTX:(part + 1) * CTX]
                                last = nc.tensor.matmul(o, w[s][:, k, cols], n[:, k, a:a + width],
                                                        start=(k == 0 and n is n_hi and w is wi_hi),
                                                        stop=(k == KD - 1 and w is wi_lo))
                last.then_inc(up_done[s], 1)

            def down(g):
                if st["ada"]:
                    pe.wait_ge(rows_copied, g + st["ada"][0])
                pe.wait_ge(wo_lo_ready, g0 + g + 1)
                pe.wait_ge(g_lo_ready[1], g0 + g + 1)
                for d in range(KD):
                    for j, (a, width) in enumerate(segs):
                        n = d * ns + j
                        pe.wait_ge(h_added, g * st["nj"] + (st["jobs"] + max(0, n - 3)))
                        for f in range(2):
                            for w, x in ((wo_hi, g_hi), (wo_hi, g_lo), (wo_lo, g_hi)):
                                last = nc.tensor.matmul(ps[:, DOWN_BANKS[n % 4], 0:width], w[:, f, d * P:(d + 1) * P],
                                                        x[:, f, a:a + width], start=(f == 0 and w is wo_hi and x is g_hi),
                                                        stop=(f == 1 and w is wo_lo))
                        last.then_inc(down_end if n == st["nj"] - 1 else down_done, 1)

            up(0, 0, True)
            up(1, 0, True)
            with pe.Fori(1, FG) as g:
                up(0, g, False)
                down(g - 1)
                up(1, g, False)
                if st["ada"]:
                    pe.wait_ge(h_added, g * st["nj"] + st["jobs"])
                    ada_pe(pe, g + (st["ada"][0] - 1))
            down(FG - 1)
            if st["ada"]:
                mods_pe(pe, st["ada"][0])

        def ffn_act(act, i, st):
            g0, w = st["g0"], ncols(st["segs"])

            def split_wo(g):
                act.wait_ge(wo_loaded, (g + (g0 + 1)) * 16)
                nc.scalar.copy(wo_hi[:, :, :], wo_raw[:, :, :]).then_inc(wo_hi_ready, 1)

            def split_wi(s, g):
                act_split(act, s, g + (st["units"] + 1))

            def gate(s, g, used=False, first=False):
                act.wait_ge(up_done[s], g + (g0 + 1))
                if g0 or not first:
                    act.wait_ge(g_lo_ready[s], g + g0)
                for j, (a, width) in enumerate(st["segs"]):
                    src = ps[:, 3 * s, 0:width] if j == 0 else ps[:, 3 * s + 2, 0:CTX]
                    last = nc.scalar.activation(silu_a[:, s, a:a + width], src, ACT.Silu)
                last.then_inc(silu_ready[s], 1)
                act.wait_ge(prod_ready[s], g + (g0 + 1))
                if used:
                    act.wait_ge(down_end, g + g0)
                nc.scalar.copy(g_hi[:, s, 0:w], prod[:, s, 0:w]).then_inc(g_hi_ready[s], 1)

            def body(g, rows, first=False):
                split_wo(g - 1)
                split_wi(0, g)
                gate(1, g - 1, first=first)
                if rows:
                    ada_rows_act(act, g + (st["ada"][0] - 2))
                split_wi(1, g)
                gate(0, g, used=True)
                if st["ada"]:
                    ada_act(act, g + (st["ada"][0] - 1))

            gate(0, 0, first=True)
            if st["ada"]:
                body(1, False, first=True)
            with act.Fori(2 if st["ada"] else 1, FG) as g:
                body(g, st["ada"])
            split_wo(FG - 1)
            gate(1, FG - 1)
            if st["ada"]:
                ada_rows_act(act, st["ada"][0] + FG - 2)

        def ffn_dve(dve, i, st):
            g0, w, ns = st["g0"], ncols(st["segs"]), len(st["segs"])

            def split_wo(g):
                dve.wait_ge(wo_hi_ready, g + (g0 + 1))
                nc.vector.tensor_tensor(wo_lo[:, :, :], wo_raw[:, :, :], wo_hi[:, :, :].bitcast(F32),
                                        ALU.subtract).then_inc(wo_lo_ready, 1)

            def split_wi(s, g):
                dve_split(dve, s, g + (st["units"] + 1))

            def gate(s, g):
                dve.wait_ge(silu_ready[s], g + (g0 + 1))
                for j, (a, width) in enumerate(st["segs"]):
                    src = ps[:, 3 * s + 1, 0:width] if j == 0 else ps[:, 3 * s + 2, CTX:2 * CTX]
                    last = nc.vector.tensor_tensor(prod[:, s, a:a + width], silu_a[:, s, a:a + width], src, ALU.mult)
                last.then_inc(prod_ready[s], 1)
                dve.wait_ge(g_hi_ready[s], g + (g0 + 1))
                nc.vector.tensor_tensor(g_lo[:, s, 0:w], prod[:, s, 0:w], g_hi[:, s, 0:w].bitcast(F32),
                                        ALU.subtract).then_inc(g_lo_ready[s], 1)

            def add(g):
                for d in range(KD):
                    for j, (a, width) in enumerate(st["segs"]):
                        n = d * ns + j
                        if n == st["nj"] - 1:
                            dve.wait_ge(down_end, g + (g0 + 1))
                        else:
                            dve.wait_ge(down_done, g * (st["nj"] - 1) + (st["jobs"] - 1 - g0 + n + 1))
                        nc.vector.scalar_tensor_tensor(out=h[:, d, a:a + width], in0=ps[:, DOWN_BANKS[n % 4], 0:width],
                                                       scalar=half_gate[:, st["l"], st["which"], d, j:j + 1],
                                                       in1=h[:, d, a:a + width], op0=ALU.mult,
                                                       op1=ALU.add).then_inc(h_added, 1)

            gate(0, 0)
            with dve.Fori(1, FG) as g:
                split_wo(g - 1)
                split_wi(0, g)
                gate(1, g - 1)
                split_wi(1, g)
                add(g - 1)
                gate(0, g)
                if st["ada"]:
                    ada_dve(dve, g + (st["ada"][0] - 1))
            split_wo(FG - 1)
            gate(1, FG - 1)
            add(FG - 1)
            if st["ada"]:
                mods_dve(dve, st["ada"][0])

        def mix_load(sp, i, st, u):
            l, s = st["l"], u % 2
            wait_slot_used(sp, i, u)
            if u < NU:
                w = I["w_in"][l].rearrange("(k p) n -> p k n", p=P)
                pieces = UNITS[u][1]
                if len(pieces) == 1:
                    c, n, _ = pieces[0]
                    pieces = [(c, n // 2, 0), (c + n // 2, n // 2, 0)]
            else:
                w = I["w_out"][l].rearrange("(k p) n -> p k n", p=P)
                pieces = [((u - NU) * 256, P, 0), ((u - NU) * 256 + P, P, 0)]
            o = 0
            for c, n, _ in pieces:
                sp.dma_start(wi_raw[s][:, :, o:o + n], w[:, :, c:c + n]).then_inc(wi_loaded[s], 16)
                o += n

        def mix_sync(sp, i, st):
            l = st["l"]
            for u in range(NU + 2):
                mix_load(sp, i, st, u)
            sp.wait_ge(fence["pe"], st["k"] * 6 + 1)
            sp.wait_ge(fence["act"], st["k"] * 6 + 1)
            sp.wait_ge(fence["dve"], st["k"] * 6 + 1)
            sp.dma_start(w_uq[:, :, :], I["c_w_uq"][l].rearrange("(k p) n -> p k n", p=P)).then_inc(wc_loaded, 16)
            sp.dma_start(w_ukv[:, :], I["c_w_ukv"][l]).then_inc(wc_loaded, 16)
            for u in range(NU + 2, NU + OUTU):
                mix_load(sp, i, st, u)

        def proj_jobs():
            for u, (kind, _) in enumerate(UNITS):
                for t in range(NT if kind == "tok" else 4):
                    yield u, t, kind

        def mix_proj_pe(pe, i, st):
            for n, (u, t, kind) in enumerate(proj_jobs()):
                s = u % 2
                if t == 0:
                    pe.wait_ge(wi_lo_ready[s], st["units"] + u // 2 + 1)
                if n == 0:
                    wait_h(pe, i, KD - 1)
                m = st["proj"] + n
                if m >= 8:
                    pe.wait_ge(proj_copied, m - 7)
                w = unit_w(u)
                for k in range(KD):
                    if n == 0:
                        pe.wait_ge(n_lo_ready, n_count(i) - (KD - 1 - k) * 2)
                    if kind == "tok":
                        for q, (x, y) in enumerate(((n_hi, wi_hi), (n_hi, wi_lo), (n_lo, wi_hi))):
                            last = nc.tensor.matmul(ps[:, m % 8, 0:w], x[:, k, t * P:(t + 1) * P], y[s][:, k, 0:w],
                                                    start=(k == 0 and q == 0), stop=(k == KD - 1 and q == 2))
                    else:
                        f, (a, width) = t // 2, SEGS[t % 2]
                        for q, (x, y) in enumerate(((n_hi, wi_hi), (n_lo, wi_hi), (n_hi, wi_lo))):
                            last = nc.tensor.matmul(ps[:, m % 8, 0:width], y[s][:, k, f * P:(f + 1) * P],
                                                    x[:, k, a:a + width], start=(k == 0 and q == 0),
                                                    stop=(k == KD - 1 and q == 2))
                last.then_inc(proj_done, 1)

        def mix_proj_act(act, i, st):
            for n, (u, t, kind) in enumerate(proj_jobs()):
                m = st["proj"] + n
                act.wait_ge(proj_done, m + 1)
                if kind == "tok":
                    o = 0
                    for _, w, c in UNITS[u][1]:
                        last = nc.scalar.copy(tok[:, t, c:c + w], ps[:, m % 8, o:o + w])
                        o += w
                else:
                    f, j = t // 2, t % 2
                    a, width = SEGS[j]
                    if n == 0:
                        act.wait_ge(dve_act, st["k"] * 2 + 1)
                    c = 2 + conv_col(0 if j == 0 else NX)
                    last = nc.scalar.copy(xbc[:, UNITS[u][1][0][2] + f, c:c + width], ps[:, m % 8, 0:width])
                last.then_inc(proj_copied, 1)
                if t == (NT if kind == "tok" else 4) - 1 and u + 2 < NU + 1:
                    act_split(act, u % 2, st["units"] + (u + 2) // 2 + 1, unit_w(u + 2))
                if u == U_Z and t == NT - 1:
                    act.wait_ge(proj_copied, m + 1)
                    act_link(nc.scalar.activation(tok[:, :, Z0:Z0 + 256], tok[:, :, Z0:Z0 + 256], ACT.Silu))
                if u == U_C and t == NT - 1:
                    na = small[:, 48:96]
                    act.wait_ge(dve_act, st["k"] * 2 + 2)
                    act_link(nc.scalar.activation(na, na, ACT.Exp))
                    nc.scalar.activation(na, na, ACT.Ln, bias=1.0).then_inc(act_dve, 1)
                if u == U_B + 1 and t == NT - 1:
                    act.wait_ge(norm_stats, 3 * st["k"] + 3)
                    act_link(nc.scalar.activation(BSTAT, BSTAT, ACT.Ln, bias=eps[:, 0:1], scale=1.0 / HD))
                    act_link(nc.scalar.activation(QSTAT, QSTAT, ACT.Ln, bias=eps[:, 0:1], scale=1.0 / 256))
                    act_link(nc.scalar.activation(KVSTAT, KVSTAT, ACT.Ln, bias=eps[:, 0:1], scale=1.0 / 128))
                    nc.scalar.activation(small[:, 300:348], small[:, 300:348], ACT.Exp, scale=-0.5).then_inc(norm_rstd, 1)
                if t == (NT if kind == "tok" else 4) - 1 and 1 <= u <= 3:
                    for j in (2 * u - 2, 2 * u - 1):
                        act.wait_ge(conv_ready, st["k"] * 6 + j + 1)
                        cb_ = V_CONVB + st["l"] * 6 + j
                        nc.scalar.activation(xbc[:, j, 0:XW - 4], conv_acc[:, j % 2, :], ACT.Silu,
                                             bias=vec[:, cb_:cb_ + 1]).then_inc(xbc_ready, 1)

        def mix_conv_dve(dve, st, j):
            l = st["l"]
            if st["k"] * 6 + j >= 2:
                dve.wait_ge(xbc_ready, st["k"] * 6 + j - 1)
            for k in range(5):
                wcol = vec[:, V_CONVW + (l * 5 + k) * 6 + j:V_CONVW + (l * 5 + k) * 6 + j + 1]
                src = xbc[:, j, k:k + XW - 4]
                if k == 0:
                    dve_link(nc.vector.tensor_scalar(conv_acc[:, j % 2, :], src, wcol, None, ALU.mult))
                else:
                    ins = nc.vector.scalar_tensor_tensor(out=conv_acc[:, j % 2, :], in0=src, scalar=wcol,
                                                         in1=conv_acc[:, j % 2, :], op0=ALU.mult, op1=ALU.add)
                    if k < 4:
                        dve_link(ins)
                    else:
                        ins.then_inc(conv_ready, 1)

        BSTAT, QSTAT, KVSTAT = small[:, 300:336], small[:, 336:342], small[:, 342:348]

        def dt_views(l):
            v, na, dt, a = (small[:, c:c + 48].rearrange("p (t e) -> p t e", t=NT) for c in (0, 48, 144, 192))
            return v, na, dt, a, lambda name, w: bc(R(l, name).unsqueeze(1), [P, NT, w])

        def mix_proj_dve(dve, i, st):
            base, l = 0, st["l"]
            for u, (kind, _) in enumerate(UNITS):
                n = NT if kind == "tok" else 4
                dve.wait_ge(proj_copied, st["proj"] + base + n)
                base += n
                if u + 2 < NU + 1:
                    dve_split(dve, u % 2, st["units"] + (u + 2) // 2 + 1, unit_w(u + 2))
                if u == U_DT:
                    dt_v, dt_na, dt_dt, dt_a, row = dt_views(l)
                    dve_link(nc.vector.tensor_tensor(dt_v, tok[:, :, DT0:DT0 + 8], row("d_dt_bias", 8), ALU.add))
                    nc.vector.scalar_tensor_tensor(out=dt_na, in0=dt_v, scalar=-1.0, in1=dt_v, op0=ALU.mult, op1=ALU.min).then_inc(dve_act, 1)
                if u == U_B - 1:
                    dve.wait_ge(act_dve, st["k"] * 2 + 1)
                    dve_link(nc.vector.scalar_tensor_tensor(out=dt_dt, in0=dt_v, scalar=0.0, in1=dt_na, op0=ALU.max, op1=ALU.add))
                    nc.vector.scalar_tensor_tensor(out=dt_a, in0=dt_dt, scalar=-1.0, in1=row("d_a_log", 8), op0=ALU.mult,
                                                   op1=ALU.mult).then_inc(a_ready, 1)
                if u == U_C:
                    dve.wait_ge(xbc_ready, st["k"] * 6 + 6)
                    cq = tok[:, :, C0:C0 + 384]
                    dve_link(nc.vector.tensor_tensor(m_sq[:, :, :], cq, cq, ALU.mult))
                    nc.vector.tensor_reduce(QSTAT, m_sq[:, :, 0:256], AX_X, ALU.add).then_inc(norm_stats, 1)
                    nc.vector.tensor_reduce(KVSTAT, m_sq[:, :, 256:384], AX_X, ALU.add).then_inc(norm_stats, 1)
                if u == U_B:
                    dve.wait_ge(norm_stats, st["k"] * 3 + 2)
                    v = tok[:, :, B0:B0 + 384].rearrange("p t (h e) -> p t h e", e=64)
                    tmp = m_sq[:, :, :].rearrange("p t (h e) -> p t h e", e=64)
                    dve_link(nc.vector.tensor_tensor(tmp, v, v, ALU.mult))
                    nc.vector.tensor_reduce(BSTAT.rearrange("p (t h) -> p t h", h=6), tmp, AX_X, ALU.add).then_inc(norm_stats, 1)
                if kind == "conv":
                    mix_conv_dve(dve, st, 2 * u)
                    mix_conv_dve(dve, st, 2 * u + 1)

        def rope(link, eng, x1, x2, c, s, t1, t2):
            link(eng.tensor_tensor(t1, x1, s, ALU.mult))
            link(eng.tensor_tensor(t2, x2, s, ALU.mult))
            link(eng.tensor_tensor(x1, x1, c, ALU.mult))
            link(eng.tensor_tensor(x2, x2, c, ALU.mult))
            link(eng.tensor_tensor(x1, x1, t2, ALU.subtract))
            return eng.tensor_tensor(x2, x2, t1, ALU.add)

        def rope_heads(link, eng, col, halves=(0, 1)):
            v = tok[:, 0:NX, col:col + 384].rearrange("p t (h f x e) -> p t h f x e", f=2, x=2, e=16)
            cc = C("cosh").rearrange("p (t f e) -> p t f e", t=NX, f=2)
            ss = C("sinh").rearrange("p (t f e) -> p t f e", t=NX, f=2)
            t1 = m_tmp[:, 0:NX, 0:96].rearrange("p t (h e) -> p t h e", e=16)
            t2 = m_tmp[:, 0:NX, 96:192].rearrange("p t (h e) -> p t h e", e=16)
            for f in halves:
                last = rope(link, eng, v[:, :, :, f, 0], v[:, :, :, f, 1], cc[:, :, f].unsqueeze(2).broadcast_to([P, NX, 6, 16]),
                            ss[:, :, f].unsqueeze(2).broadcast_to([P, NX, 6, 16]), t1, t2)
                if f != halves[-1]:
                    link(last)
            return last

        def rope_c():
            return [C(nm).rearrange("p (t f e) -> p t f e", t=NX, f=2) for nm in ("cosc", "sinc")]

        chain_n = {"dve": 0, "act": 0, "pool": 0}

        def make_link(key, eng, s):
            def link(ins):
                chain_n[key] += 1
                ins.then_inc(s, 1)
                eng.wait_ge(s, chain_n[key])
            return link

        dve_link = make_link("dve", nc.vector, dve_chain)
        act_link = make_link("act", nc.scalar, act_chain)
        pool_link = make_link("pool", nc.gpsimd, pool_chain)

        def bc(ap, shape):
            return ap.broadcast_to(shape)

        FCH = {0: [4, 5, 0, 1, 2, 3], 1: [5, 4, 3, 2, 1, 0]}

        def scan_dve(dve, i, st):
            l, k, nq = st["l"], st["k"], st["nq"]
            _, _, dt, a, _ = dt_views(l)
            prep_copies(dve, 0, scan_prep(), st["prep_scan"])
            wait_prep(dve, st["prep_scan"] + len(scan_prep()))
            for dr in range(2):
                dtb = bc(dt[:, :, dr * 4:dr * 4 + 4].unsqueeze(3), [P, NT, 4, 64])
                ins = nc.vector.tensor_tensor(xdt[:, dr].rearrange("p t (h e) -> p t h e", e=64),
                                              xsb[:, :, 0:256].rearrange("p t (h e) -> p t h e", e=64), dtb, ALU.mult)
                dve_link(ins)
            dve.wait_ge(dt_exps, k + 1)
            ex = stat[:, 0, 0:144]
            for dr in range(2):
                dec = ex[:, 24 + 48 * dr:48 + 48 * dr].rearrange("p (t h) -> p t h", h=4)
                nc.vector.tensor_tensor(xdec[:, dr].rearrange("p t (h e) -> p t h e", e=64),
                                        xdt[:, dr].rearrange("p t (h e) -> p t h e", e=64),
                                        bc(dec.unsqueeze(3), [P, NT, 4, 64]), ALU.mult).then_inc(xdt_ready, 1)
            for dr in range(2):
                dve_link(nc.vector.memset(h_in[:, dr, FCH[dr][0], :], 0.0))
            for n in range(NT - 1):
                for dr in range(2):
                    c, nx = FCH[dr][n], FCH[dr][n + 1]
                    tot = ex[:, 96 + c * 8 + dr * 4:96 + c * 8 + dr * 4 + 4]
                    j = 2 * n + dr
                    dve_link(nc.vector.tensor_tensor(y_tmp[:, dr * 256:dr * 256 + 256].rearrange("p (h e) -> p h e", e=64),
                                                     h_in[:, dr, c, :].rearrange("p (h e) -> p h e", e=64),
                                                     bc(tot.unsqueeze(2), [P, 4, 64]), ALU.mult))
                    dve.wait_ge(st_done, k * CARRIES + j + 1)
                    ins = nc.vector.tensor_tensor(h_in[:, dr, nx, :], ps[:, j % 4, 0:256],
                                                  y_tmp[:, dr * 256:dr * 256 + 256], ALU.add)
                    ins.then_inc(h_in_ready, 1)
                    dve.wait_ge(h_in_ready, k * CARRIES + j + 1)
            dve_split(dve, (NU + 1) % 2, st["units"] + (NU + 1) // 2 + 1)
            cbase, ybase = st["cb"], st["y"]
            for t in range(nq):
                dve.wait_ge(cb_done, cbase + t + 1)
                for dr, m in enumerate(("le", "ge")):
                    nc.vector.tensor_tensor(cb[:, t, dr], ps[:, 4 + t % 2, 0:256].rearrange("p (g i) -> p g i", g=2),
                                            bc(C(m).unsqueeze(1), [P, 2, P]), ALU.mult).then_inc(cb_ready, 1)
            dve.wait_ge(cb_ready, 2 * (cbase + nq))
            for t in range(nq):
                for dr in range(2):
                    j = 2 * t + dr
                    dve.wait_ge(seg_exp, cbase * 2 + j + 1)
                    d4 = decay[:, dr, :].rearrange("p (g r i) -> p g r i", g=2, r=2)
                    for g in range(2):
                        last = nc.vector.tensor_tensor(d4[:, g], d4[:, g], bc(cb[:, t, dr, g].unsqueeze(1), [P, 2, P]), ALU.mult)
                    last.then_inc(m_ready, 1)
                dve.wait_ge(y_done, ybase + t + 1)
                o4 = ps[:, 6, :].rearrange("p (d h e) -> p d h e", d=2, h=4)
                e4 = ex[:, 0:96].rearrange("p (d x t h) -> p d x t h", d=2, x=2, t=NT)[:, :, 0, t]
                y4 = y_tmp[:, :].rearrange("p (d h e) -> p d h e", d=2, h=4)
                dve_link(nc.vector.tensor_tensor(y4, o4, bc(e4.unsqueeze(3), [P, 2, 4, 64]), ALU.mult))
                dve_link(nc.vector.tensor_tensor(y_tmp[:, 0:256], y_tmp[:, 0:256], y_tmp[:, 256:512], ALU.add))
                nc.vector.tensor_tensor(y_tmp[:, 0:256], y_tmp[:, 0:256], ps[:, 7, 0:256], ALU.add).then_inc(y_ready, 1)
                dve.wait_ge(y_ready, ybase + t + 1)
                dve.wait_ge(x_skipped, k + 1)
                dve_link(nc.vector.tensor_tensor(y_tmp[:, 0:256], y_tmp[:, 0:256], xsb[:, t, 0:256], ALU.add))
                nc.vector.tensor_tensor(tok[:, t, Z0:Z0 + 256], tok[:, t, Z0:Z0 + 256], y_tmp[:, 0:256], ALU.mult).then_inc(y_gated, 1)

        def scan_act(act, i, st):
            l, k, nq = st["l"], st["k"], st["nq"]
            act.wait_ge(dt_sums, k + 1)
            nc.scalar.activation(stat[:, 0, 0:144], ps[:, 0, 0:144], ACT.Exp).then_inc(dt_exps, 1)
            prep_copies(act, 1, scan_prep(), st["prep_scan"])
            nc.scalar.copy(masks[:, 0, :], C("prev"))
            nc.scalar.activation(masks[:, 1, :], C("prev"), ACT.Copy, scale=0.0)
            nc.scalar.copy(masks[:, 2, :], C("next"))
            nc.scalar.copy(ident_r[:, :], ident)
            act_split(act, (NU + 1) % 2, st["units"] + (NU + 1) // 2 + 1)
            cbase = st["cb"]

            def square(t):
                act.wait_ge(y_gated, st["y"] + t + 1)
                return nc.scalar.activation(y_sq[:, :], tok[:, t, Z0:Z0 + 256], ACT.Square, accum_out=small[:, 256 + t:257 + t])

            for t in range(nq):
                if t > 0:
                    act_link(square(t - 1))
                for dr in range(2):
                    j = 2 * t + dr
                    act.wait_ge(seg_done, cbase * 2 + j + 1)
                    if t > 0:
                        act.wait_ge(y_done, st["y"] + t)
                    nc.scalar.activation(decay[:, dr, :], ps[:, 4 + dr, :], ACT.Exp).then_inc(seg_exp, 1)
            act_link(square(nq - 1))

        def d_rstd_act(act, st):
            v = small[:, 256:256 + st["nq"]]
            act_link(nc.scalar.activation(v, v, ACT.Ln, bias=eps[:, 0:1], scale=1.0 / 256))
            nc.scalar.activation(v, v, ACT.Exp, scale=-0.5).then_inc(act_dve, 1)

        def d_norm_pool(pool, st, n):
            t = n // 2
            z = tok[:, t, Z0:Z0 + 256]
            if n == 0:
                pool.wait_ge(act_dve, st["k"] * 2 + 2)
            if n % 2 == 0:
                pool_link(nc.gpsimd.tensor_scalar(z, z, small[:, 256 + t:257 + t], 1.0, ALU.mult, ALU.mult))
            else:
                pool_link(nc.gpsimd.tensor_tensor(z, z, R(st["l"], "d_out_norm"), ALU.mult))

        def scan_pe(pe, i, st):
            k, nq = st["k"], st["nq"]
            pe.wait_ge(a_ready, k + 1)
            a = small[:, 192:240].rearrange("p (t d h) -> p t d h", t=NT, d=2)
            for n, (m, dr) in enumerate((("le", 0), ("gt", 0), ("ge", 1), ("lt", 1))):
                nc.tensor.matmul(ps[:, 0, 24 * n:24 * n + 24].rearrange("p (t h) -> p t h", h=4), C(m), a[:, :, dr, :],
                                 start=True, stop=True)
            nc.tensor.matmul(ps[:, 0, 96:144], ones, small[:, 192:240], start=True, stop=True).then_inc(dt_sums, 1)
            prep_pe(pe, scan_prep(), st["prep_scan"])
            pe.wait_ge(dt_exps, k + 1)
            for n in range(NT - 1):
                for dr in range(2):
                    j, c = 2 * n + dr, FCH[dr][n]
                    pe.wait_ge(xdt_ready, k * 2 + dr + 1)
                    if j >= 4:
                        pe.wait_ge(h_in_ready, k * CARRIES + j - 3)
                    for g in range(2):
                        last = nc.tensor.matmul(ps[:, j % 4, g * P:(g + 1) * P], xsb[:, c, 256 + g * P:256 + (g + 1) * P],
                                                xdec[:, dr, c, g * P:(g + 1) * P], start=True, stop=True)
                    last.then_inc(st_done, 1)
            wait_prep(pe, st["prep_scan"] + len(scan_prep()))
            for t in range(nq):
                c = conv_col(t)
                if t >= 2:
                    pe.wait_ge(cb_ready, 2 * (st["cb"] + t - 1))
                for g in range(2):
                    last = nc.tensor.matmul(ps[:, 4 + t % 2, g * P:(g + 1) * P], xbc[:, 2 + g, c:c + P], xbc[:, 4 + g, c:c + P],
                                            start=True, stop=True)
                last.then_inc(cb_done, 1)
            pe.wait_ge(cb_ready, 2 * (st["cb"] + nq))
            pe.wait_ge(h_in_ready, (k + 1) * CARRIES)

            def seg(j):
                pe.wait_ge(seg_in, st["cb"] * 2 + j + 1)
                if j >= 2:
                    pe.wait_ge(seg_exp, st["cb"] * 2 + j - 1)
                nc.tensor.matmul(ps[:, 4 + j % 2, :], C("gt" if j % 2 == 0 else "lt"), seg_rhs[:, j % 2, :],
                                 start=True, stop=True).then_inc(seg_done, 1)
            seg(0)
            seg(1)
            for t in range(nq):
                if t > 0:
                    pe.wait_ge(y_ready, st["y"] + t)
                c = conv_col(t)
                for dr in range(2):
                    for g in range(2):
                        nc.tensor.matmul(ps[:, 6, dr * 256 + g * P:dr * 256 + (g + 1) * P], xbc[:, 4 + g, c:c + P],
                                         h_in[:, dr, t, g * P:(g + 1) * P], start=True, stop=True)
                pe.wait_ge(m_ready, 2 * (st["cb"] + t + 1))
                for hd in range(4):
                    for dr in range(2):
                        last = nc.tensor.matmul(ps[:, 7, hd * 64:(hd + 1) * 64], decay[:, dr, hd * P:(hd + 1) * P],
                                                xdt[:, dr, t, hd * 64:(hd + 1) * 64], start=(dr == 0), stop=(dr == 1))
                last.then_inc(y_done, 1)
                if t + 1 < nq:
                    seg(2 * t + 2)
                    seg(2 * t + 3)

        def scan_prep():
            jobs_ = []
            for t in range(NT):
                c = conv_col(t)
                mm = [("T", q * P, P, xbc[:, q, c:c + P]) for q in range(4)]
                jobs_.append((P, mm, [(xsb[:, t, :], 0, 512, None)]))
            return jobs_

        def qk_prep(name, nq):
            jobs_ = []
            K = 96
            for hd in range(8):
                for part, (t0, t1) in enumerate(((0, NX), (NX, NT))):
                    if hd < 4 and t0 >= nq:
                        continue
                    mm = []
                    for t in range(t0, t1):
                        src = (qc if hd < 4 else kc)[:, t, hd % 4, :]
                        mm.append(("T", (t - t0) * P, P, src))
                    jobs_.append((K, mm, [(qkT[0:K, hd, t0 * P:t1 * P], 0, (t1 - t0) * P, None)]))
            return jobs_

        def ab_jobs(name, nq):
            for hd in range(6):
                for t0, t1 in ((0, NX), (NX, NT)):
                    if hd >= 4 or t0 < nq:
                        yield hd, t0, t1

        def ab_prep_pe(pe, st, name):
            for n, (hd, t0, t1) in enumerate(ab_jobs(name, st["nq"])):
                m = st["ab_" + name] + n
                if m >= 4:
                    pe.wait_ge(qk_lo_ready, m - 3)
                col = (A0 if name == "a" else B0) + hd * 64
                for t in range(t0, t1):
                    last = nc.tensor.transpose(ps[0:64, 4 + m % 4, (t - t0) * P:(t - t0 + 1) * P], tok[:, t, col:col + 64], ident)
                last.then_inc(qk_turned, 1)

        def ab_dst(hd):
            return (q_hi[:, hd], q_lo[:, hd]) if hd < 4 else (k_hl[:, hd - 4], k_hl[:, hd - 4])

        def ab_prep_act(act, st, name):
            for n, (hd, t0, t1) in enumerate(ab_jobs(name, st["nq"])):
                m = st["ab_" + name] + n
                act.wait_ge(qk_turned, m + 1)
                src = ps[0:64, 4 + m % 4, 0:(t1 - t0) * P]
                last = nc.scalar.copy(ab_dst(hd)[0][0:64, t0 * P:t1 * P], src)
                if hd < 4:
                    last = nc.scalar.copy(ab_dst(hd)[0][64:P, t0 * P:t1 * P], src)
                last.then_inc(qk_hi_ready, 1)

        def ab_prep_dve(dve, st, name):
            for n, (hd, t0, t1) in enumerate(ab_jobs(name, st["nq"])):
                m = st["ab_" + name] + n
                dve.wait_ge(qk_hi_ready, m + 1)
                hi, lo = ab_dst(hd)
                for p0 in ((0, 64) if hd < 4 else (64,)):
                    last = nc.vector.tensor_tensor(lo[p0:p0 + 64, t0 * P:t1 * P], ps[0:64, 4 + m % 4, 0:(t1 - t0) * P],
                                                   hi[0:64, t0 * P:t1 * P].bitcast(F32), ALU.subtract)
                last.then_inc(qk_lo_ready, 1)

        def latent_prep():
            jobs_ = []
            for f in range(3):
                for t0, t1 in ((0, NX), (NX, NT)):
                    mm = [("T", (t - t0) * P, P, tok[:, t, C0 + f * P:C0 + (f + 1) * P]) for t in range(t0, t1)]
                    jobs_.append((P, mm, [(cT[:, f, t0 * P:t1 * P], 0, (t1 - t0) * P, None)]))
            return jobs_

        def up_prep(nq):
            jobs_ = []
            for t in range(NT):
                if t < nq:
                    mm = [("M", 0, 384, cT[:, f, t * P:(t + 1) * P], w_uq[:, f, :], f == 0, f == 1) for f in range(2)]
                    jobs_.append((P, mm, [(qc[:, t], 0, 384, 96)]))
                mm = [("M", 0, 512, cT[:, 2, t * P:(t + 1) * P], w_ukv[:, :], True, True)]
                jobs_.append((P, mm, [(kc[:, t, :, 0:64], 0, 64, 128), (vc[:, t, :].rearrange("p (h e) -> p h e", e=64), 64, 128, 128)]))
            return jobs_

        def prep_pe(pe, jobs_, n0):
            for n, (K, mm, _) in enumerate(jobs_):
                m = n0 + n
                if m >= 4:
                    pe.wait_ge(prep_copied[m % 2], (m - 4) // 2 + 1)
                for x in mm:
                    o = ps[0:K, 4 + m % 4, x[1]:x[1] + x[2]]
                    if x[0] == "T":
                        last = nc.tensor.transpose(o, x[3], ident)
                    else:
                        last = nc.tensor.matmul(o, x[3], x[4], start=x[5], stop=x[6])
                last.then_inc(prep_done, 1)

        def prep_copies(eng, me, jobs_, n0):
            for n, (K, _, copies) in enumerate(jobs_):
                m = n0 + n
                if m % 2 != me:
                    continue
                eng.wait_ge(prep_done, m + 1)
                for dst, a, b, per in copies:
                    bank = ps[0:K, 4 + m % 4, :]
                    src = bank[:, a:b]
                    if per == 96:
                        src = src.rearrange("p (h e) -> p h e", e=96)
                    elif per == 128:
                        src = bank.rearrange("p (h e) -> p h e", e=128)[:, :, a:b]
                    last = (nc.vector.tensor_copy if me == 0 else nc.scalar.copy)(dst, src)
                last.then_inc(prep_copied[me], 1)

        def wait_prep(eng, n):
            eng.wait_ge(prep_copied[0], (n + 1) // 2)
            if n // 2:
                eng.wait_ge(prep_copied[1], n // 2)

        SPEC = {"a": dict(K=64, v=384, o=A0, scale=HD ** -0.5), "b": dict(K=64, v=B0 + 384, o=B0, scale=HD ** -0.5),
                "c": dict(K=96, v=None, o=C0, scale=96 ** -0.5)}

        def att_steps(name, nq):
            for hd in range(4):
                for t in range(nq):
                    if t >= NX:
                        loc = []
                    elif name == "a":
                        loc = list(range(max(0, t - 1), min(NX, t + 2)))
                    else:
                        loc = list(range(NX))
                    yield hd, t, loc

        def att_pe(pe, st, name):
            sp_, K = SPEC[name], SPEC[name]["K"]
            steps = list(att_steps(name, st["nq"]))
            base = st["att_" + name]
            if name == "c":
                wait_prep(pe, st["prep_c_end"])
            else:
                pe.wait_ge(qk_lo_ready, st["ab_" + name] + len(list(ab_jobs(name, st["nq"]))))

            def qk(o, hd, t, a, b, start, stop):
                q = slice(t * P, (t + 1) * P)
                if name == "c":
                    return nc.tensor.matmul(o, qkT[0:K, hd, q], qkT[0:K, 4 + hd, a:b], start=start, stop=stop, skip_group_check=True)
                for x in (q_hi, q_lo):
                    last = nc.tensor.matmul(o, x[:, hd, q], k_hl[:, hd // 2, a:b], start=start and x is q_hi,
                                            stop=stop and x is q_lo, skip_group_check=True)
                return last

            def scores(n):
                hd, t, loc = steps[n]
                m = base + n
                if m >= 2:
                    pe.wait_ge(exp_done, m - 1)
                b = 2 * (m % 2)
                if loc:
                    w = len(loc) * P
                    o = ps[:, b, 512 - w:512]
                    qk(o, hd, t, loc[0] * P, loc[0] * P + w, True, name != "a")
                    if name == "a":
                        m0 = loc[0] - t + 1
                        nc.tensor.matmul(o, ident_r[:, :], masks[:, m0:m0 + len(loc), :].rearrange("p a b -> p (a b)"), start=False, stop=True,
                                         skip_group_check=True)
                qk(ps[:, b + 1, 0:CTX], hd, t, SEQ, TOK, True, True).then_inc(s_done, 1)

            def transposes(n):
                hd, t, loc = steps[n]
                m = base + n
                pe.wait_ge(probs_scaled, m + 1)
                if m >= 1:
                    pe.wait_ge(t_copied_x, m)
                    pe.wait_ge(t_copied_c, m)
                w = len(loc) * P
                for x in range(len(loc)):
                    c = 512 - w + x * P
                    nc.tensor.transpose(ps[:, 4, c:c + P], probs[:, m % 3, c:c + P], ident)
                for x in range(2):
                    last = nc.tensor.transpose(ps[:, 5, x * P:(x + 1) * P], probs[:, m % 3, 512 + x * P:512 + (x + 1) * P], ident)
                last.then_inc(t_done, 1)

            def values(n):
                hd, t, loc = steps[n]
                m = base + n
                pe.wait_ge(t_copied_x, m + 1)
                pe.wait_ge(t_copied_c, m + 1)
                if m >= 2:
                    pe.wait_ge(o_ready, m - 1)
                w = len(loc) * P
                keys = [(512 - w + y * P, x) for y, x in enumerate(loc)] + [(512, NX), (512 + P, NX + 1)]
                for y, (c, x) in enumerate(keys):
                    if name == "c":
                        v = vc[:, x, hd * 64:(hd + 1) * 64]
                    else:
                        v = tok[:, x, sp_["v"] + (hd // 2) * 64:sp_["v"] + (hd // 2) * 64 + 64]
                    last = nc.tensor.matmul(ps[0:64, 6 + m % 2, 0:P], v, probsT[:, m % 2, c:c + P],
                                            start=(y == 0), stop=(y == len(keys) - 1))
                last.then_inc(pv_done, 1)

            scores(0)
            scores(1)
            for n in range(len(steps)):
                if n + 2 < len(steps):
                    scores(n + 2)
                transposes(n)
                if n >= 1:
                    values(n - 1)
            values(len(steps) - 1)

        def att_act(act, st, name):
            steps = list(att_steps(name, st["nq"]))
            base, sc = st["att_" + name], SPEC[name]["scale"]
            for n in range(len(steps) + 2):
                if n >= 2:
                    m = base + n - 2
                    w = len(steps[n - 2][2]) * P
                    act.wait_ge(t_done, m + 1)
                    if m >= 2:
                        act.wait_ge(pv_done, m - 1)
                    if w:
                        nc.scalar.copy(probsT[:, m % 2, 512 - w:512], ps[:, 4, 512 - w:512]).then_inc(t_copied_x, 1)
                    else:
                        nc.scalar.copy(stat[:, 0, 150:151], stat[:, 1, n - 2:n - 1]).then_inc(t_copied_x, 1)
                if n < len(steps):
                    hd, t, loc = steps[n]
                    m = base + n
                    w = len(loc) * P
                    act.wait_ge(bias_ready, m + 1)
                    if m >= 3:
                        act.wait_ge(t_done, m - 2)
                    if name == "a":
                        nc.scalar.activation(stat[:, 3, n:n + 1], R(st["l"], "a_sink")[:, hd:hd + 1], ACT.Exp,
                                             bias=stat[:, 1, n:n + 1])
                    src = ps[:, 2 * (m % 2):2 * (m % 2) + 2, :].rearrange("p a b -> p (a b)")
                    nc.scalar.activation(probs[:, m % 3, 512 - w:TOK], src[:, 512 - w:TOK], ACT.Exp, bias=stat[:, 1, n:n + 1],
                                         scale=sc, accum_out=stat[:, 2, n:n + 1]).then_inc(exp_done, 1)

        def att_pool(pool, st, name):
            for n, (hd, t, loc) in enumerate(att_steps(name, st["nq"])):
                m, w = st["att_" + name] + n, len(loc) * P
                pool.wait_ge(recip_ready, m + 1)
                p = probs[:, m % 3, 512 - w:TOK]
                nc.gpsimd.tensor_scalar(p, p, stat[:, 2, n:n + 1], 1.0, ALU.mult, ALU.mult).then_inc(probs_scaled, 1)
                if name == "a" and 0 <= n - 2 < 2 * st["nq"]:
                    d_norm_pool(pool, st, n - 2)

        def att_dve(dve, st, name):
            steps = list(att_steps(name, st["nq"]))
            base, sc = st["att_" + name], SPEC[name]["scale"]
            for n in range(len(steps) + 3):
                if 1 <= n <= len(steps):
                    dve.wait_ge(exp_done, base + n)
                    if name == "a":
                        dve_link(nc.vector.tensor_tensor(stat[:, 2, n - 1:n], stat[:, 2, n - 1:n], stat[:, 3, n - 1:n], ALU.add))
                    nc.vector.reciprocal(stat[:, 2, n - 1:n], stat[:, 2, n - 1:n]).then_inc(recip_ready, 1)
                if n < len(steps):
                    hd, t, loc = steps[n]
                    m = base + n
                    w = len(loc) * P
                    dve.wait_ge(s_done, m + 1)
                    src = ps[:, 2 * (m % 2):2 * (m % 2) + 2, :].rearrange("p a b -> p (a b)")
                    dve_link(nc.vector.tensor_reduce(stat[:, 0, n:n + 1], src[:, 512 - w:TOK], AX_X, ALU.max))
                    if name == "a":
                        dve_link(nc.vector.tensor_scalar(stat[:, 0, n:n + 1], stat[:, 0, n:n + 1], sc,
                                                         R(st["l"], "a_sink")[:, hd:hd + 1], ALU.mult, ALU.max))
                        nc.vector.tensor_scalar(stat[:, 1, n:n + 1], stat[:, 0, n:n + 1], -1.0, None, ALU.mult).then_inc(bias_ready, 1)
                    else:
                        nc.vector.tensor_scalar(stat[:, 1, n:n + 1], stat[:, 0, n:n + 1], -sc, None, ALU.mult).then_inc(bias_ready, 1)
                if 2 <= n <= len(steps) + 1:
                    m = base + n - 2
                    dve.wait_ge(t_done, m + 1)
                    if m >= 2:
                        dve.wait_ge(pv_done, m - 1)
                    nc.vector.tensor_copy(probsT[:, m % 2, 512:TOK], ps[:, 5, 0:CTX]).then_inc(t_copied_c, 1)
                if n >= 3:
                    hd, t, loc = steps[n - 3]
                    m = base + n - 3
                    dve.wait_ge(pv_done, m + 1)
                    o, p0 = SPEC[name]["o"] + hd // 2 * P, (hd % 2) * 64
                    nc.vector.tensor_copy(tok[p0:p0 + 64, t, o:o + P], ps[0:64, 6 + m % 2, 0:P]).then_inc(o_ready, 1)

        for st in info:
            if st["kind"] != "mix":
                continue
            k = st["k"]
            nqs = [x["nq"] for x in info if x["kind"] == "mix"]
            counts = lambda q: [("scan", len(scan_prep())),
                                ("lat", len(latent_prep())), ("up", len(up_prep(q))), ("c", len(qk_prep("c", q)))]
            n = sum(sum(c for _, c in counts(q)) for q in nqs[:k])
            for nm, c in counts(st["nq"]):
                st["prep_" + nm] = n
                n += c
                st["prep_" + nm + "_end"] = n
            n = sum(3 * 4 * q for q in nqs[:k])
            for nm in "abc":
                st["att_" + nm] = n
                n += 4 * st["nq"]
            n = sum(2 * len(list(ab_jobs("a", q))) for q in nqs[:k])
            for nm in "ab":
                st["ab_" + nm] = n
                n += len(list(ab_jobs(nm, st["nq"])))
            st["cb"] = sum(nqs[:k])
            st["y"] = sum(nqs[:k])
            st["oT"] = sum(8 * (2 if q == NT else 1) for q in nqs[:k])
        norm_stats, norm_rstd, c_roped = sem("norm_stats"), sem("norm_rstd"), sem("c_roped")
        fence_n = {e: 0 for e in fence}

        def next_fence(eng, me, without=None):
            fence_n[me] += 1
            fence_all(eng, me, fence_n[me], without)

        def mix_pe(pe, i, st):
            mix_proj_pe(pe, i, st)
            next_fence(pe, "pe", without="pool")
            scan_pe(pe, i, st)
            next_fence(pe, "pe")
            for nm in "ab":
                ab_prep_pe(pe, st, nm)
                att_pe(pe, st, nm)
                next_fence(pe, "pe")
            prep_pe(pe, latent_prep(), st["prep_lat"])
            wait_prep(pe, st["prep_lat_end"])
            pe.wait_ge(wc_loaded, 32 * (st["k"] + 1))
            prep_pe(pe, up_prep(st["nq"]), st["prep_up"])
            pe.wait_ge(c_roped, st["k"] + 1)
            prep_pe(pe, qk_prep("c", st["nq"]), st["prep_c"])
            att_pe(pe, st, "c")
            next_fence(pe, "pe")
            mix_out_pe(pe, i, st)

        def oT_jobs(st):
            for f in OUT_ORDER:
                for j in range(len(st["osegs"])):
                    yield f, j

        OUT_ORDER = (6, 7, 0, 1, 2, 3, 4, 5)

        def oT_src(n, f, j):
            t0, t1 = ((0, NX), (NX, NT))[j]
            if f >= 6:
                return ps[:, n % 4, 0:(t1 - t0) * P].rearrange("p (t m) -> p t m", m=P)
            return tok[:, t0:t1, o_col(f):o_col(f) + P]

        def o_col(f):
            return (A0, B0, C0, Z0)[f // 2] + (f % 2) * P

        def mix_out_pe(pe, i, st):
            for n, (f, j) in enumerate(oT_jobs(st)):
                if f < 6:
                    continue
                t0, t1 = ((0, NX), (NX, NT))[j]
                for t in range(t0, t1):
                    last = nc.tensor.transpose(ps[:, n % 4, (t - t0) * P:(t - t0 + 1) * P], tok[:, t, o_col(f):o_col(f) + P], ident)
                last.then_inc(oT_done, 1)
            fence_n["pe"] += 1
            pe.drain().then_inc(fence["pe"], 1)
            ns = len(st["osegs"])
            for d in range(KD):
                u = NU + d // 2
                if d % 2 == 0:
                    pe.wait_ge(wi_lo_ready[u % 2], st["units"] + u // 2 + 1)
                for j, (a, width) in enumerate(st["osegs"]):
                    n = d * ns + j
                    if n >= 4:
                        pe.wait_ge(out_added, st["out"] + n - 3)
                    for y, f in enumerate(OUT_ORDER):
                        if n < ns:
                            pe.wait_ge(oT_lo, st["oT"] + ns * y + j + 1)
                        for q, (w, x) in enumerate(((wi_hi, n_hi), (wi_hi, n_lo), (wi_lo, n_hi))):
                            last = nc.tensor.matmul(ps[:, 4 + n % 4, 0:width], w[u % 2][:, f, (d % 2) * P:(d % 2 + 1) * P],
                                                    x[:, f, a:a + width], start=(y == 0 and q == 0), stop=(y == 7 and q == 2))
                    last.then_inc(out_done, 1)

        def mix_act(act, i, st):
            l, k = st["l"], st["k"]
            mix_proj_act(act, i, st)
            next_fence(act, "act", without="pool")
            scan_act(act, i, st)
            next_fence(act, "act")
            for nm in "ab":
                ab_prep_act(act, st, nm)
                if nm == "a":
                    d_rstd_act(act, st)
                att_act(act, st, nm)
                next_fence(act, "act")
            prep_copies(act, 1, latent_prep(), st["prep_lat"])
            prep_copies(act, 1, up_prep(st["nq"]), st["prep_up"])
            prep_copies(act, 1, qk_prep("c", st["nq"]), st["prep_c"])
            att_act(act, st, "c")
            next_fence(act, "act")
            for n, (f, j) in enumerate(oT_jobs(st)):
                a, w = SEGS[j]
                if f >= 6:
                    act.wait_ge(oT_done, st["oT"] // 4 + n + 1)
                nc.scalar.copy(n_hi[:, f, a:a + w].rearrange("p (t m) -> p t m", m=P), oT_src(n, f, j)).then_inc(oT_hi, 1)
            next_fence(act, "act")
            for u in (NU + 2, NU + 3):
                act_split(act, u % 2, st["units"] + u // 2 + 1)

        def mix_dve(dve, i, st):
            l, k = st["l"], st["k"]
            dve_link(nc.vector.memset(xbc[:, :, 0:2], 0.0))
            dve_link(nc.vector.memset(xbc[:, :, 2 + SEQ:4 + SEQ], 0.0))
            nc.vector.memset(xbc[:, :, XW - 2:XW], 0.0).then_inc(dve_act, 1)
            mix_proj_dve(dve, i, st)
            next_fence(dve, "dve", without="pool")
            scan_dve(dve, i, st)
            next_fence(dve, "dve")
            for nm in "ab":
                ab_prep_dve(dve, st, nm)
                att_dve(dve, st, nm)
                next_fence(dve, "dve")
            prep_copies(dve, 0, latent_prep(), st["prep_lat"])
            prep_copies(dve, 0, up_prep(st["nq"]), st["prep_up"])
            wait_prep(dve, st["prep_up_end"])
            ct, stb = rope_c()
            for f in range(2):
                q = qc[:, 0:NX, :, 64 + 16 * f:80 + 16 * f]
                cf = bc(ct[:, :, f].unsqueeze(2), [P, NX, 4, 8])
                sf = bc(stb[:, :, f].unsqueeze(2), [P, NX, 4, 8])
                t1 = m_tmp[:, 0:NX, 0:32].rearrange("p t (h e) -> p t h e", h=4)
                t2 = m_tmp[:, 0:NX, 32:64].rearrange("p t (h e) -> p t h e", h=4)
                dve_link(rope(dve_link, nc.vector, q[:, :, :, 0:8], q[:, :, :, 8:16], cf, sf, t1, t2))
            nc.vector.tensor_copy(kc[:, :, :, 64:96], bc(tok[:, :, C0 + 384:C0 + 416].unsqueeze(2), [P, NT, 4, 32])).then_inc(c_roped, 1)
            prep_copies(dve, 0, qk_prep("c", st["nq"]), st["prep_c"])
            att_dve(dve, st, "c")
            next_fence(dve, "dve")
            for n, (f, j) in enumerate(oT_jobs(st)):
                a, w = SEGS[j]
                dve.wait_ge(oT_hi, st["oT"] + n + 1)
                nc.vector.tensor_tensor(n_lo[:, f, a:a + w].rearrange("p (t m) -> p t m", m=P), oT_src(n, f, j),
                                        n_hi[:, f, a:a + w].bitcast(F32).rearrange("p (t m) -> p t m", m=P),
                                        ALU.subtract).then_inc(oT_lo, 1)
            next_fence(dve, "dve")
            ns = len(st["osegs"])
            for d in range(KD):
                if d == 2 or d == 4:
                    u = NU + 2 + (d // 2 - 1)
                    dve_split(dve, u % 2, st["units"] + u // 2 + 1)
                for j, (a, w) in enumerate(st["osegs"]):
                    n = d * ns + j
                    dve.wait_ge(out_done, st["out"] + n + 1)
                    g = mods[:, (l * NMOD + 5) * KD + d, j:j + 1]
                    nc.vector.scalar_tensor_tensor(out=h[:, d, a:a + w], in0=ps[:, 4 + n % 4, 0:w], scalar=g,
                                                   in1=h[:, d, a:a + w], op0=ALU.mult, op1=ALU.add).then_inc(out_added, 1)

        def mix_pool(pool, i, st):
            l = st["l"]
            tt = lambda o, x, y: pool_link(nc.gpsimd.tensor_tensor(o, x, y, ALU.mult))
            pool.wait_ge(norm_rstd, st["k"] + 1)
            v = tok[:, :, B0:B0 + 384].rearrange("p t (h e) -> p t h e", e=64)
            tt(v, v, bc(BSTAT.rearrange("p (t h) -> p t h", h=6).unsqueeze(3), [P, NT, 6, 64]))
            tt(v[:, :, 0:4], v[:, :, 0:4], bc(R(l, "b_q_norm").unsqueeze(1).unsqueeze(1), [P, NT, 4, 64]))
            tt(v[:, :, 4:6], v[:, :, 4:6], bc(R(l, "b_k_norm").unsqueeze(1).unsqueeze(1), [P, NT, 2, 64]))
            pool_link(rope_heads(pool_link, nc.gpsimd, B0))
            for c, w, r, nm in ((C0, 256, QSTAT, "c_q_norm"), (C0 + 256, 128, KVSTAT, "c_kv_norm")):
                x = tok[:, :, c:c + w]
                tt(x, x, bc(r.unsqueeze(2), [P, NT, w]))
                tt(x, x, bc(R(l, nm).unsqueeze(1), [P, NT, w]))
            kr = tok[:, 0:NX, C0 + 384:C0 + 416].rearrange("p t (f x e) -> p t f x e", f=2, x=2)
            t1 = m_tmp[:, 0:NX, 0:16].rearrange("p t (f e) -> p t f e", f=2)
            t2 = m_tmp[:, 0:NX, 16:32].rearrange("p t (f e) -> p t f e", f=2)
            pool_link(rope(pool_link, nc.gpsimd, kr[:, :, :, 0], kr[:, :, :, 1], *rope_c(), t1, t2))
            next_fence(pool, "pool")
            k, nq, a = st["k"], st["nq"], dt_views(l)[3]

            def build(j):
                t, dr = j // 2, j % 2
                if j >= 2:
                    pool.wait_ge(seg_done, st["cb"] * 2 + j - 1)
                nc.gpsimd.tensor_tensor(seg_rhs[:, j % 2, :].rearrange("p (h i) -> p h i", h=4),
                                        bc(C("le" if dr == 0 else "ge").unsqueeze(1), [P, 4, P]),
                                        bc(a[:, t, dr * 4:dr * 4 + 4].unsqueeze(2), [P, 4, P]), ALU.mult).then_inc(seg_in, 1)

            build(0)
            build(1)
            pool.wait_ge(xdt_ready, k * 2 + 2)
            xs = xsb[:, :, 0:256].rearrange("p t (h e) -> p t h e", h=4)
            nc.gpsimd.tensor_tensor(xs, xs, bc(R(l, "d_skip").unsqueeze(1).unsqueeze(3), [P, NT, 4, 64]), ALU.mult).then_inc(x_skipped, 1)
            for j in range(2, 2 * nq):
                build(j)
                if j in (3, 5):
                    pool_link(rope_heads(pool_link, nc.gpsimd, A0, halves=(j // 2 - 1,)))
            next_fence(pool, "pool")
            for nm in "abc":
                att_pool(pool, st, nm)
                next_fence(pool, "pool")
            next_fence(pool, "pool")

        block = ctx.enter_context(nc.Block())
        xin = place("xin", [P, NT, DM], offset=n_at)
        vrows = place("vrows", [P, 3, P], offset=n_at + NT * DM * 4)
        fin = place("fin", [P, 2, DM], offset=m_at)

        @block.sync
        def _(sp):
            sp.dma_start(cst[:, :], I["cst"]).then_inc(cst_loaded, 16)
            ab = I["ada_b"].rearrange("l (r p) -> (l r) p", p=P)
            sp.dma_start(vrows[:, 0, :], ab[0:P]).then_inc(in_loaded, 16)
            sp.dma_start(vrows[0:16, 1, :], ab[P:144]).then_inc(in_loaded, 16)
            for r, nm in ((16, "ffn1_norm"), (32, "mix_norm"), (48, "ffn2_norm")):
                sp.dma_start(vrows[r:r + 16, 1, :], I[nm].rearrange("l (r p) -> (l r) p", p=P)).then_inc(in_loaded, 16)
            for r, nm in ((64, "final_norm"), (72, "c"), (80, "c_ctx")):
                sp.dma_start(vrows[r:r + 8, 1, :], I[nm].rearrange("(r p) -> r p", p=P)).then_inc(in_loaded, 16)
            sp.dma_start(vrows[0:60, 2, :], I["d_conv_w"].rearrange("l k (r p) -> (l k r) p", p=P)).then_inc(in_loaded, 16)
            sp.dma_start(vrows[60:72, 2, :], I["d_conv_b"].rearrange("l (r p) -> (l r) p", p=P)).then_inc(in_loaded, 16)
            sp.dma_start(xin[:, 0:NX, :], I["x"].rearrange("(t p) n -> p t n", p=P)).then_inc(x_loaded, 16)
            sp.dma_start(xin[:, NX:NT, :], I["ctx"].rearrange("(t p) n -> p t n", p=P)).then_inc(x_loaded, 16)
            for l in range(DEPTH):
                for nm, (a, w) in ROWS.items():
                    sp.dma_start(rows[:, l, a:a + w], I[nm][l:l + 1, :].broadcast_to([P, w])).then_inc(rows_loaded, 16)
            sp.wait_ge(ada_loaded[2], 16 * ADA_AT[0][1])
            for i, st in enumerate(info):
                (ffn_sync if st["kind"] == "ffn" else mix_sync)(sp, i, st)
            for t in range(NX):
                sp.wait_ge(fin_copied, 2 * t + 2)
                sp.dma_start(out[t * P:(t + 1) * P, :], fin[:, t % 2, :]).then_inc(stored[t % 2], 16)
            for s in stored:
                sp.wait_ge(s, 16 * NX // 2)

        NIN, NROWS = 16 * 10, 16 * DEPTH * len(ROWS)

        @block.gpsimd
        def _(pool):
            ada_pool(pool, *ADA_AT[0])
            pool.wait_ge(rows_loaded, NROWS)
            for i, st in enumerate(info):
                if i:
                    norm_sums(pool, nc.gpsimd, i, st)
                if st["kind"] == "mix":
                    mix_pool(pool, i, st)
                elif st["ada"]:
                    if i:
                        for e in ("pe", "act", "dve"):
                            pool.wait_ge(fence[e], fence_n["pool"])
                        pool.wait_ge(wi_loaded[1], 32 * (st["units"] + 1))
                    else:
                        pool.wait_ge(mod_turned, 1)
                    ada_pool(pool, *st["ada"])
            norm_sums(pool, nc.gpsimd, len(info), final_norm)

        @block.scalar
        def _(act):
            act.wait_ge(vec_copied, 3)
            for j, c in enumerate((V_C, V_CC)):
                last = nc.scalar.activation(silu_c[:, :, j], vec[:, c:c + KD], ACT.Silu)
            last.then_inc(silu_c_ready, 1)
            act.wait_ge(silu_c_ready, 1)
            nc.scalar.copy(silu_r[:, :, 0:2], silu_c[:, :, :]).then_inc(silu_hi_ready, 1)
            for b in range(ADA_AT[0][1]):
                ada_act(act, b)
                if b:
                    ada_rows_act(act, b - 1, first=b == 1, bank=6 - 2 * ((b - 1) % 2))
                for d in (2 * b, 2 * b + 1):
                    act.wait_ge(h0_done, 2 * d + 1)
                    nc.scalar.copy(h[:, d, 0:SEQ], ps[:, (2 * d) % 4, :]).then_inc(h0_x, 1)
                if b:
                    norm_act_sums(act, 0, info[0], (2 * b - 2, 2 * b - 1))
            ada_rows_act(act, b, bank=6 - 2 * (b % 2))
            act.wait_ge(rows_loaded, NROWS)
            for l in range(DEPTH):
                act_link(nc.scalar.activation(R(l, "d_a_log"), R(l, "d_a_log"), ACT.Exp))
            for i, st in enumerate(info):
                split = lambda s: act_split(act, s, st["units"] + 1, 256 if st["kind"] == "ffn" else unit_w(s))
                late = i > 0 and info[i - 1]["kind"] == "mix"
                if not late:
                    split(0)
                    split(1)
                norm_act_sums(act, i, st, range(KD) if i else (KD - 2, KD - 1))
                if late:
                    split(0)
                norm_act_rstd(act, st)
                norm_act_mod(act, i, st)
                if late:
                    split(1)
                (ffn_act if st["kind"] == "ffn" else mix_act)(act, i, st)
            i = len(info)
            norm_act_sums(act, i, final_norm)
            norm_act_rstd(act, final_norm)

        @block.vector
        def _(dve):
            nc.vector.memset(eps[:, :], EPS).then_inc(h_added, 1)
            for n in range(3):
                w = (P, 88, 72)[n]
                dve.wait_ge(vec_done, n + 1)
                nc.vector.tensor_copy(vec[:, (0, P, 216)[n]:(0, P, 216)[n] + w], ps[:, 4 + n, 0:w]).then_inc(vec_copied, 1)
            dve.wait_ge(silu_hi_ready, 1)
            nc.vector.tensor_tensor(silu_r[:, :, 2:4], silu_c[:, :, :], silu_r[:, :, 0:2].bitcast(F32), ALU.subtract).then_inc(silu_lo_ready, 1)
            for b in range(ADA_AT[0][1]):
                ada_dve(dve, b)
                for d in (2 * b, 2 * b + 1):
                    dve.wait_ge(h0_done, 2 * d + 2)
                    nc.vector.tensor_copy(h[:, d, SEQ:TOK], ps[:, (2 * d + 1) % 4, 0:CTX]).then_inc(h0_c, 1)
                if b:
                    norm_sums(dve, nc.vector, 0, info[0], (2 * b - 2, 2 * b - 1))
            mods_dve(dve, ADA_AT[0][0])
            dve.wait_ge(rows_loaded, NROWS)
            for i, st in enumerate(info):
                dve_split(dve, 0, st["units"] + 1, 256 if st["kind"] == "ffn" else unit_w(0))
                norm_dve_mod(dve, i, st)
                dve_split(dve, 1, st["units"] + 1, 256 if st["kind"] == "ffn" else unit_w(1))
                (ffn_dve if st["kind"] == "ffn" else mix_dve)(dve, i, st)
            i = len(info)
            dve.wait_ge(rstd_ready, final_norm["norm"] + 1)
            for d in range(KD):
                dve_link(nc.vector.scalar_tensor_tensor(out=h[:, d, 0:SEQ], in0=h[:, d, 0:SEQ], scalar=vec[:, V_FIN + d:V_FIN + d + 1],
                                                        in1=rstd[:, 0:SEQ], op0=ALU.mult, op1=ALU.mult))
            nc.vector.tensor_copy(eps[:, :], h[:, 0, 0:1]).then_inc(h_added, 1)
            for n in range(2 * NX):
                dve.wait_ge(fin_done, n + 1)
                if n // 2 >= 2:
                    dve.wait_ge(stored[(n // 2) % 2], 16 * (n // 4))
                nc.vector.tensor_copy(fin[:, (n // 2) % 2, (n % 2) * 512:(n % 2 + 1) * 512], ps[:, n % 4, :]).then_inc(fin_copied, 1)

        @block.tensor
        def _(pe):
            pe.wait_ge(cst_loaded, 16)
            pe.wait_ge(in_loaded, NIN)
            for n in range(3):
                w = (P, 88, 72)[n]
                nc.tensor.transpose(ps[:, 4 + n, 0:w], vrows[0:w, n, :], ident[0:w, 0:w]).then_inc(vec_done, 1)
            pe.wait_ge(silu_lo_ready, 1)
            for b in range(ADA_AT[0][1]):
                if b >= 2:
                    pe.wait_ge(rows_copied, b - 1)
                elif b == 1:
                    pe.wait_ge(vec_copied, 3)
                ada_pe(pe, b, bank=6 - 2 * (b % 2))
                if b == 0:
                    pe.wait_ge(x_loaded, 32)
                for d in (2 * b, 2 * b + 1):
                    for j, (t0, t1) in enumerate(((0, NX), (NX, NT))):
                        n = 2 * d + j
                        if n >= 4:
                            pe.wait_ge(h0_x if j == 0 else h0_c, d - 1)
                        for t in range(t0, t1):
                            last = nc.tensor.transpose(ps[:, n % 4, (t - t0) * P:(t - t0 + 1) * P], xin[:, t, d * P:(d + 1) * P], ident)
                        last.then_inc(h0_done, 1)
            pe.wait_ge(h0_x, KD)
            mods_pe(pe, ADA_AT[0][0])
            for i, st in enumerate(info):
                norm_pe(pe, i, st)
                (ffn_pe if st["kind"] == "ffn" else mix_pe)(pe, i, st)
            norm_pe(pe, len(info), final_norm)
            pe.wait_ge(h_added, jobs + 1)
            for n in range(2 * NX):
                t = n // 2
                if n >= 4:
                    pe.wait_ge(fin_copied, n - 3)
                for q in range(4):
                    d = (n % 2) * 4 + q
                    last = nc.tensor.transpose(ps[:, n % 4, q * P:(q + 1) * P], h[:, d, t * P:(t + 1) * P], ident)
                last.then_inc(fin_done, 1)


def constants():
    import numpy as np
    k, m = np.arange(P)[:, None], np.arange(P)[None, :]
    t = np.zeros((P, CSTW), np.float32)

    def put(name, a):
        c, w = CST[name]
        t[:, c:c + w] = a.reshape(P, w)

    put("ident", np.eye(P))
    put("ones", np.ones((P, P)))
    put("le", (k <= m) * 1.0)
    put("gt", (k > m) * 1.0)
    put("ge", (k >= m) * 1.0)
    put("lt", (k < m) * 1.0)
    put("prev", np.where(m >= k, 0.0, NEG))
    put("next", np.where(m <= k, 0.0, NEG))
    pos = np.arange(SEQ)
    for dim, cn, sn, rep in ((HD, "cosh", "sinh", 1), (C_ROPE, "cosc", "sinc", 1)):
        ax = dim // 2
        inv = np.float32(THETA) ** (-np.arange(0, ax, 2, dtype=np.float32) / np.float32(ax))
        ang = np.stack([(pos // GRID_W)[:, None].astype(np.float32) * inv, (pos % GRID_W)[:, None].astype(np.float32) * inv], 1)
        ang = np.tile(ang.astype(np.float32), (1, rep, 1)).reshape(NX, P, rep * 2 * (ax // 2)).transpose(1, 0, 2)
        put(cn, np.cos(ang.astype(np.float64)))
        put(sn, np.sin(ang.astype(np.float64)))
    return t


NAMES = ["x", "c", "ctx", "c_ctx", "ada_w", "ada_b", "ffn1_norm", "ffn1_wi", "ffn1_wo", "mix_norm", "w_in", "w_out",
         "a_sink", "b_q_norm", "b_k_norm", "c_q_norm", "c_w_uq", "c_kv_norm", "c_w_ukv", "d_conv_w", "d_conv_b",
         "d_a_log", "d_dt_bias", "d_skip", "d_out_norm", "ffn2_norm", "ffn2_wi", "ffn2_wo", "final_norm"]


def kernel(**inputs):
    import numpy as np
    import concourse.bacc as bacc
    from concourse.bass_utils import run_bass_kernel_spmd as run

    nc = bacc.Bacc("TRN2", target_bir_lowering=False, num_devices=1)
    arrays, aps = {}, {}
    for name in NAMES:
        a = np.ascontiguousarray(inputs[name])
        if name in ("x", "ctx"):
            a = a.reshape(a.shape[1:])
        if name == "c":
            a = a.reshape(-1)
        if name in ("d_a_log", "d_dt_bias"):
            a = a.reshape(DEPTH, -1)
        arrays["in_" + name] = a
    arrays["in_cst"] = constants()
    for name, a in arrays.items():
        aps[name[3:]] = nc.dram_tensor(name, a.shape, mybir.dt.from_np(a.dtype), kind="ExternalInput").ap()
    out = nc.dram_tensor("out_0", (SEQ, DM), F32, kind="ExternalOutput").ap()
    mod_dram = nc.dram_tensor("mod_dram", (4, DEPTH * NMOD * DM), F32, kind="Internal").ap()
    hybrid_block(nc, aps, out, mod_dram)
    got = run(nc, [arrays], core_ids=[0]).results[0]["out_0"]
    return got.reshape(1, SEQ, DM)
```
